# Optimizing a Trainium2 kernel written in Bass

```python
import jax, jax.numpy as jnp
from jax import lax
import numpy as np

D_MODEL = 1024
BATCH = 1
SEQ = 256
DEPTH = 2

N_MEM = 256
D_MIX = D_MODEL
CONV_HEADS = 4
CONV_DIM = D_MIX // 4
CONV_WIDTH = 3
REC_HEADS = 4
REC_DIM = D_MIX // 2
REC_HEAD_DIM = REC_DIM // REC_HEADS
REC_EXPAND = 128
REC_FDIM = REC_HEADS * REC_EXPAND
CHUNK = 64
POOL_DIM = D_MIX - CONV_DIM - REC_DIM
POOL_WINDOWS = (2, 4, 8, 16)
POOL_GROUP = POOL_DIM // len(POOL_WINDOWS)
D_IN = 3 * CONV_DIM + 2 * REC_FDIM + 2 * REC_DIM + POOL_DIM
CA_HEADS = 4
CA_HEAD_DIM = D_MODEL // CA_HEADS
D_FF = 2816
ALPHA = (2.0 * DEPTH) ** 0.25
BETA = (8.0 * DEPTH) ** -0.25
LN_EPS = 1e-5
RMS_EPS = 1e-6


def layer_norm(x, g, b):
    xf = x.astype(jnp.float32)
    mu = jnp.mean(xf, axis=-1, keepdims=True)
    var = jnp.mean(jnp.square(xf - mu), axis=-1, keepdims=True)
    return ((xf - mu) * lax.rsqrt(var + LN_EPS)).astype(x.dtype) * g + b

def swiglu(x, w_gate, w_up, w_down):
    return (jax.nn.silu(x @ w_gate) * (x @ w_up)) @ w_down

def short_gated_conv(h, b_gate, c_gate, w):
    u = c_gate * h
    s = u.shape[1]
    up = jnp.pad(u, ((0, 0), (CONV_WIDTH - 1, 0), (0, 0)))
    y = sum(w[k] * up[:, k:k + s] for k in range(CONV_WIDTH))
    return b_gate * y

def hgrn2(q, f_logit, v, g, lb, norm_g):
    bsz, s, _ = q.shape
    n_chunks = s // CHUNK
    f32 = jnp.float32
    f = lb + (1.0 - lb) * jax.nn.sigmoid(f_logit.astype(f32))
    logf = jnp.log(f)
    k = 1.0 - f

    def to_chunks(t, d):
        return t.reshape(bsz, n_chunks, CHUNK, REC_HEADS, d).transpose(1, 0, 3, 2, 4)

    qc = to_chunks(q.astype(f32), REC_EXPAND)
    kc = to_chunks(k, REC_EXPAND)
    lc = to_chunks(logf, REC_EXPAND)
    vc = to_chunks(v.astype(f32), REC_HEAD_DIM)
    mask = jnp.tril(jnp.ones((CHUNK, CHUNK), dtype=bool))

    def step(state, inp):
        qb, kb, vb, lb_ = inp
        b = jnp.cumsum(lb_, axis=2)
        diff = b[:, :, :, None, :] - b[:, :, None, :, :]
        decay = jnp.exp(jnp.where(mask[:, :, None], diff, -jnp.inf))
        attn = jnp.einsum('bhtd,bhsd,bhtsd->bhts', qb, kb, decay)
        o = (jnp.einsum('bhts,bhsv->bhtv', attn, vb)
             + jnp.einsum('bhtd,bhdv->bhtv', qb * jnp.exp(b), state))
        b_last = b[:, :, -1:, :]
        new_state = (jnp.exp(b_last[:, :, 0, :])[..., None] * state
                     + jnp.einsum('bhsd,bhsv->bhdv', kb * jnp.exp(b_last - b), vb))
        return new_state, o

    s0 = jnp.zeros((bsz, REC_HEADS, REC_EXPAND, REC_HEAD_DIM), f32)
    _, o = lax.scan(step, s0, (qc, kc, vc, lc))
    o = o.transpose(1, 0, 3, 2, 4).reshape(bsz, s, REC_HEADS, REC_HEAD_DIM)
    o = o * lax.rsqrt(jnp.mean(jnp.square(o), axis=-1, keepdims=True) + RMS_EPS)
    o = o * norm_g.reshape(REC_HEADS, REC_HEAD_DIM).astype(f32)
    o = o.reshape(bsz, s, REC_DIM) * jax.nn.sigmoid(g.astype(f32))
    return o.astype(v.dtype)

def multiscale_pool(u, w_pool, scale):
    bsz, s, _ = u.shape
    uf = u.astype(jnp.float32)
    cs = jnp.cumsum(uf, axis=1)
    t = jnp.arange(s)
    groups = []
    for gi, w in enumerate(POOL_WINDOWS):
        sl = slice(gi * POOL_GROUP, (gi + 1) * POOL_GROUP)
        c = cs[:, :, sl]
        win_sum = c - jnp.pad(c, ((0, 0), (w, 0), (0, 0)))[:, :s]
        count = jnp.minimum(t + 1, w).astype(jnp.float32)[None, :, None]
        groups.append(win_sum / count - uf[:, :, sl])
    p = jnp.stack(groups, axis=2).astype(u.dtype)
    y = jnp.einsum('bsgc,gcd->bsgd', p, w_pool).reshape(bsz, s, POOL_DIM)
    return y * scale

def cross_attn(x, mem, wq, wk, wv, wo):
    bsz, s, _ = x.shape
    m = mem.shape[1]
    q = (x @ wq).reshape(bsz, s, CA_HEADS, CA_HEAD_DIM)
    k = (mem @ wk).reshape(bsz, m, CA_HEADS, CA_HEAD_DIM)
    v = (mem @ wv).reshape(bsz, m, CA_HEADS, CA_HEAD_DIM)
    sc = jnp.einsum('bshd,bmhd->bhsm', q, k).astype(jnp.float32) * (CA_HEAD_DIM ** -0.5)
    p = jax.nn.softmax(sc, axis=-1).astype(v.dtype)
    o = jnp.einsum('bhsm,bmhd->bshd', p, v).reshape(bsz, s, D_MODEL)
    return o @ wo

def first_inputs(seed: int = 0) -> dict:
    key = jax.random.key(seed)
    ks = jax.random.split(key, 24)
    f32 = jnp.float32
    nrm = lambda k, shp, sc: jax.random.normal(k, shp, f32) * sc
    return {
        'x': nrm(ks[0], (BATCH, SEQ, D_MODEL), 1.0),
        'mem': nrm(ks[1], (BATCH, N_MEM, D_MODEL), 1.0),
        'ffn1_gate': nrm(ks[2], (DEPTH, D_MODEL, D_FF), BETA * D_MODEL ** -0.5),
        'ffn1_up': nrm(ks[3], (DEPTH, D_MODEL, D_FF), BETA * D_MODEL ** -0.5),
        'ffn1_down': nrm(ks[4], (DEPTH, D_FF, D_MODEL), BETA * D_FF ** -0.5),
        'w_in': nrm(ks[5], (DEPTH, D_MODEL, D_IN), D_MODEL ** -0.5),
        'conv_w': nrm(ks[6], (DEPTH, CONV_WIDTH, CONV_DIM), CONV_WIDTH ** -0.5),
        'rec_lb': nrm(ks[7], (DEPTH, REC_FDIM), 0.5),
        'rec_norm_g': 1.0 + nrm(ks[8], (DEPTH, REC_DIM), 0.02),
        'pool_w': nrm(ks[9], (DEPTH, len(POOL_WINDOWS), POOL_GROUP, POOL_GROUP), POOL_GROUP ** -0.5),
        'pool_scale': 1.0 + nrm(ks[10], (DEPTH, POOL_DIM), 0.02),
        'w_out': nrm(ks[11], (DEPTH, D_MIX, D_MODEL), BETA * D_MIX ** -0.5),
        'ca_q': nrm(ks[12], (DEPTH, D_MODEL, D_MODEL), D_MODEL ** -0.5),
        'ca_k': nrm(ks[13], (DEPTH, D_MODEL, D_MODEL), D_MODEL ** -0.5),
        'ca_v': nrm(ks[14], (DEPTH, D_MODEL, D_MODEL), BETA * D_MODEL ** -0.5),
        'ca_o': nrm(ks[15], (DEPTH, D_MODEL, D_MODEL), BETA * D_MODEL ** -0.5),
        'ffn2_gate': nrm(ks[16], (DEPTH, D_MODEL, D_FF), BETA * D_MODEL ** -0.5),
        'ffn2_up': nrm(ks[17], (DEPTH, D_MODEL, D_FF), BETA * D_MODEL ** -0.5),
        'ffn2_down': nrm(ks[18], (DEPTH, D_FF, D_MODEL), BETA * D_FF ** -0.5),
        'ln_g': 1.0 + nrm(ks[19], (DEPTH, 4, D_MODEL), 0.02),
        'ln_b': nrm(ks[20], (DEPTH, 4, D_MODEL), 0.02),
    }

def first_block(x, mem, ffn1_gate, ffn1_up, ffn1_down, w_in, conv_w, rec_lb, rec_norm_g,
              pool_w, pool_scale, w_out, ca_q, ca_k, ca_v, ca_o,
              ffn2_gate, ffn2_up, ffn2_down, ln_g, ln_b):
    sm = jax.nn.softmax(rec_lb.astype(jnp.float32), axis=0)
    lbs = jnp.cumsum(sm, axis=0) - sm[0:1]
    split_at = np.cumsum([CONV_DIM, CONV_DIM, CONV_DIM, REC_FDIM, REC_FDIM, REC_DIM, REC_DIM])
    h = x
    for l in range(DEPTH):
        h = layer_norm(ALPHA * h + 0.5 * swiglu(h, ffn1_gate[l], ffn1_up[l], ffn1_down[l]),
                       ln_g[l, 0], ln_b[l, 0])
        z = h @ w_in[l]
        cb, cc, ch, rq, rf, ri, rg, pu = jnp.split(z, split_at, axis=-1)
        y_conv = short_gated_conv(ch, cb, cc, conv_w[l])
        y_rec = hgrn2(rq, rf, ri, rg, lbs[l], rec_norm_g[l])
        y_pool = multiscale_pool(pu, pool_w[l], pool_scale[l])
        mix = jnp.concatenate([y_conv, y_rec, y_pool], axis=-1) @ w_out[l]
        h = layer_norm(ALPHA * h + mix, ln_g[l, 1], ln_b[l, 1])
        h = layer_norm(ALPHA * h + cross_attn(h, mem, ca_q[l], ca_k[l], ca_v[l], ca_o[l]),
                       ln_g[l, 2], ln_b[l, 2])
        h = layer_norm(ALPHA * h + 0.5 * swiglu(h, ffn2_gate[l], ffn2_up[l], ffn2_down[l]),
                       ln_g[l, 3], ln_b[l, 3])
    return h


HEAD_DIM = 64
ROPE_THETA = 10000.0
EPS = 1e-6
Q_BLOCK = 128

A_HEADS = 4
MOBA_BLOCK = 256
MOBA_TOPK = 3
B_HEADS = 8
B_KV_HEADS = 2
WINDOW = 128
C_HEADS = 4
C_HALF = HEAD_DIM // 2

N_BRANCH = 3
CONV_W = 3

A_W = A_HEADS * HEAD_DIM
B_QW = B_HEADS * HEAD_DIM
B_KVW = B_KV_HEADS * HEAD_DIM
C_W = C_HEADS * HEAD_DIM
IN_SIZES = (A_W, A_W, A_W, B_QW, B_KVW, B_KVW, C_W, C_W, C_W, N_BRANCH * D_MODEL)
IN_COLS = sum(IN_SIZES)
SPLIT_POINTS = tuple(np.cumsum(IN_SIZES)[:-1].tolist())


def rms_norm(x, g):
    x32 = x.astype(jnp.float32)
    y = x32 * lax.rsqrt(jnp.mean(x32 * x32, axis=-1, keepdims=True) + EPS)
    return (y * g.astype(jnp.float32)).astype(x.dtype)

def rope_tables(seq, dim):
    inv = 1.0 / (ROPE_THETA ** (jnp.arange(0, dim, 2, dtype=jnp.float32) / dim))
    ang = jnp.arange(seq, dtype=jnp.float32)[:, None] * inv[None, :]
    return jnp.cos(ang), jnp.sin(ang)

def apply_rope(x, cos, sin):
    half = x.shape[-1] // 2
    shape = (1, x.shape[1]) + (1,) * (x.ndim - 3) + (half,)
    c = cos.reshape(shape).astype(x.dtype)
    s = sin.reshape(shape).astype(x.dtype)
    x1, x2 = x[..., :half], x[..., half:]
    return jnp.concatenate([x1 * c - x2 * s, x2 * c + x1 * s], axis=-1)

def moba_attention(q, k, v):
    B, S, H, d = q.shape
    n_blk = -(-S // MOBA_BLOCK)
    pad = n_blk * MOBA_BLOCK - S
    padw = ((0, 0), (0, pad), (0, 0), (0, 0))
    kb = jnp.pad(k, padw).reshape(B, n_blk, MOBA_BLOCK, H, d).transpose(0, 3, 1, 2, 4)
    vb = jnp.pad(v, padw).reshape(B, n_blk, MOBA_BLOCK, H, d).transpose(0, 3, 1, 2, 4)
    k_mean = kb.mean(axis=3)
    topk = min(MOBA_TOPK, n_blk)
    n_chunks = S // Q_BLOCK
    qc = q.reshape(B, n_chunks, Q_BLOCK, H, d).transpose(1, 0, 3, 2, 4)
    b_idx = jnp.arange(B)[:, None, None, None]
    h_idx = jnp.arange(H)[None, :, None, None]
    scale = d ** -0.5
    n_sel = topk * MOBA_BLOCK

    def one_chunk(args):
        c, qh = args
        q_pos = c * Q_BLOCK + jnp.arange(Q_BLOCK)
        own = (c * Q_BLOCK) // MOBA_BLOCK
        gate = jnp.einsum('bhqd,bhnd->bhqn', qh, k_mean).astype(jnp.float32)
        gate = jnp.where(jnp.arange(n_blk) < own, gate, -jnp.inf)
        _, idx = lax.top_k(gate, topk)
        valid = jnp.arange(topk) < own
        k_sel = kb[b_idx, h_idx, idx]
        v_sel = vb[b_idx, h_idx, idx]
        s_sel = jnp.einsum('bhqd,bhqjld->bhqjl', qh, k_sel).astype(jnp.float32) * scale
        s_sel = jnp.where(valid[:, None], s_sel, -jnp.inf).reshape(B, H, Q_BLOCK, n_sel)
        k_own = lax.dynamic_index_in_dim(kb, own, axis=2, keepdims=False)
        v_own = lax.dynamic_index_in_dim(vb, own, axis=2, keepdims=False)
        s_own = jnp.einsum('bhqd,bhld->bhql', qh, k_own).astype(jnp.float32) * scale
        k_pos = own * MOBA_BLOCK + jnp.arange(MOBA_BLOCK)
        s_own = jnp.where(k_pos[None, :] <= q_pos[:, None], s_own, -jnp.inf)
        p = jax.nn.softmax(jnp.concatenate([s_sel, s_own], axis=-1), axis=-1).astype(v.dtype)
        p_sel = p[..., :n_sel].reshape(B, H, Q_BLOCK, topk, MOBA_BLOCK)
        p_own = p[..., n_sel:]
        return (jnp.einsum('bhqjl,bhqjld->bhqd', p_sel, v_sel)
                + jnp.einsum('bhql,bhld->bhqd', p_own, v_own))

    o = lax.map(one_chunk, (jnp.arange(n_chunks), qc))
    return o.transpose(1, 0, 3, 2, 4).reshape(B, S, H * d)

def sliding_window_sink_attention(q, k, v, sinks):
    B, S, Hq, d = q.shape
    Hkv = k.shape[2]
    G = Hq // Hkv
    nb = S // WINDOW
    qb = q.reshape(B, nb, WINDOW, Hkv, G, d)

    def band(t):
        tb = t.reshape(B, nb, WINDOW, Hkv, d)
        prev = jnp.concatenate([jnp.zeros_like(tb[:, :1]), tb[:, :-1]], axis=1)
        return jnp.concatenate([prev, tb], axis=2)

    kband, vband = band(k), band(v)
    s = jnp.einsum('bnqkgd,bnjkd->bnkgqj', qb, kband).astype(jnp.float32) * (d ** -0.5)
    rel = jnp.arange(WINDOW)[:, None] + WINDOW - jnp.arange(2 * WINDOW)[None, :]
    in_win = (rel >= 0) & (rel < WINDOW)
    k_abs = jnp.arange(nb)[:, None] * WINDOW - WINDOW + jnp.arange(2 * WINDOW)[None, :]
    mask = in_win[None, :, :] & (k_abs >= 0)[:, None, :]
    s = jnp.where(mask[None, :, None, None], s, -jnp.inf)
    sink = sinks.astype(jnp.float32).reshape(1, 1, Hkv, G, 1, 1)
    m = jnp.maximum(s.max(axis=-1, keepdims=True), sink)
    p = jnp.exp(s - m)
    denom = p.sum(axis=-1, keepdims=True) + jnp.exp(sink - m)
    o = jnp.einsum('bnkgqj,bnjkd->bnqkgd', (p / denom).astype(v.dtype), vband)
    return o.reshape(B, S, Hq * d)

def differential_attention(q, k, v, lam, subln_g, lam_init):
    B, S, H, _, dh = q.shape
    n_chunks = S // Q_BLOCK
    qc = q.reshape(B, n_chunks, Q_BLOCK, H, 2, dh).transpose(1, 0, 2, 3, 4, 5)
    scale = dh ** -0.5
    k_pos = jnp.arange(S)

    def one_chunk(args):
        c, qq = args
        q_pos = c * Q_BLOCK + jnp.arange(Q_BLOCK)
        s = jnp.einsum('bqhcd,bkhcd->bhcqk', qq, k).astype(jnp.float32) * scale
        s = jnp.where(k_pos[None, :] <= q_pos[:, None], s, -jnp.inf)
        p = jax.nn.softmax(s, axis=-1)
        a = (p[:, :, 0] - lam * p[:, :, 1]).astype(v.dtype)
        return jnp.einsum('bhqk,bkhd->bqhd', a, v)

    o = lax.map(one_chunk, (jnp.arange(n_chunks), qc))
    o = o.transpose(1, 0, 2, 3, 4).reshape(B, S, H, 2 * dh)
    o = rms_norm(o, subln_g) * (1.0 - lam_init)
    return o.reshape(B, S, H * 2 * dh)

def causal_depthwise_conv(u, w, b):
    S = u.shape[1]
    up = jnp.pad(u, ((0, 0), (CONV_W - 1, 0), (0, 0)))
    y = b.astype(u.dtype)
    for j in range(CONV_W):
        y = y + up[:, j:j + S] * w[j]
    return y

def second_inputs(seed: int = 0) -> dict:
    key = jax.random.key(seed)
    ks = jax.random.split(key, 24)
    n = jax.random.normal
    f32 = jnp.float32

    def gain(k, shape):
        return 1.0 + 0.02 * n(k, shape, f32)

    return {
        "x": n(ks[0], (BATCH, SEQ, D_MODEL), f32),
        "attn_norm": gain(ks[1], (DEPTH, D_MODEL)),
        "w_in": n(ks[2], (DEPTH, D_MODEL, IN_COLS), f32) * D_MODEL ** -0.5,
        "qn_a": gain(ks[3], (DEPTH, HEAD_DIM)),
        "kn_a": gain(ks[4], (DEPTH, HEAD_DIM)),
        "qn_b": gain(ks[5], (DEPTH, HEAD_DIM)),
        "kn_b": gain(ks[6], (DEPTH, HEAD_DIM)),
        "sinks": 0.5 * n(ks[7], (DEPTH, B_HEADS), f32),
        "qn_c": gain(ks[8], (DEPTH, C_HALF)),
        "kn_c": gain(ks[9], (DEPTH, C_HALF)),
        "lam_q1": 0.1 * n(ks[10], (DEPTH, C_HALF), f32),
        "lam_k1": 0.1 * n(ks[11], (DEPTH, C_HALF), f32),
        "lam_q2": 0.1 * n(ks[12], (DEPTH, C_HALF), f32),
        "lam_k2": 0.1 * n(ks[13], (DEPTH, C_HALF), f32),
        "subln": gain(ks[14], (DEPTH, HEAD_DIM)),
        "w_pa": n(ks[15], (DEPTH, A_W, D_MODEL), f32) * A_W ** -0.5,
        "w_pb": n(ks[16], (DEPTH, B_QW, D_MODEL), f32) * B_QW ** -0.5,
        "w_pc": n(ks[17], (DEPTH, C_W, D_MODEL), f32) * C_W ** -0.5,
        "w_out": n(ks[18], (DEPTH, D_MODEL, D_MODEL), f32) * D_MODEL ** -0.5,
        "mlp_norm": gain(ks[19], (DEPTH, D_MODEL)),
        "w_up": n(ks[20], (DEPTH, D_MODEL, 2 * D_FF), f32) * D_MODEL ** -0.5,
        "conv_w": 0.5 * n(ks[21], (DEPTH, CONV_W, 2 * D_FF), f32),
        "conv_b": 0.01 * n(ks[22], (DEPTH, 2 * D_FF), f32),
        "w_down": n(ks[23], (DEPTH, D_FF, D_MODEL), f32) * D_FF ** -0.5,
    }

def second_block(x, attn_norm, w_in, qn_a, kn_a, qn_b, kn_b, sinks, qn_c, kn_c,
              lam_q1, lam_k1, lam_q2, lam_k2, subln, w_pa, w_pb, w_pc, w_out,
              mlp_norm, w_up, conv_w, conv_b, w_down):
    B, S, D = x.shape
    cos64, sin64 = rope_tables(S, HEAD_DIM)
    cos32, sin32 = rope_tables(S, C_HALF)
    for i in range(DEPTH):
        lam_init = 0.8 - 0.6 * float(np.exp(-0.3 * i))
        h = rms_norm(x, attn_norm[i])
        proj = h @ w_in[i]
        qa, ka, va, qb, kb, vb, qc, kc, vc, gates = jnp.split(proj, SPLIT_POINTS, axis=-1)

        qa = apply_rope(rms_norm(qa.reshape(B, S, A_HEADS, HEAD_DIM), qn_a[i]), cos64, sin64)
        ka = apply_rope(rms_norm(ka.reshape(B, S, A_HEADS, HEAD_DIM), kn_a[i]), cos64, sin64)
        ya = moba_attention(qa, ka, va.reshape(B, S, A_HEADS, HEAD_DIM))

        qb = apply_rope(rms_norm(qb.reshape(B, S, B_HEADS, HEAD_DIM), qn_b[i]), cos64, sin64)
        kb = apply_rope(rms_norm(kb.reshape(B, S, B_KV_HEADS, HEAD_DIM), kn_b[i]), cos64, sin64)
        yb = sliding_window_sink_attention(qb, kb, vb.reshape(B, S, B_KV_HEADS, HEAD_DIM), sinks[i])

        qc = apply_rope(rms_norm(qc.reshape(B, S, C_HEADS, 2, C_HALF), qn_c[i]), cos32, sin32)
        kc = apply_rope(rms_norm(kc.reshape(B, S, C_HEADS, 2, C_HALF), kn_c[i]), cos32, sin32)
        lam = (jnp.exp(jnp.sum(lam_q1[i].astype(jnp.float32) * lam_k1[i].astype(jnp.float32)))
               - jnp.exp(jnp.sum(lam_q2[i].astype(jnp.float32) * lam_k2[i].astype(jnp.float32)))
               + lam_init)
        yc = differential_attention(qc, kc, vc.reshape(B, S, C_HEADS, HEAD_DIM), lam, subln[i], lam_init)

        g = jax.nn.sigmoid(gates.reshape(B, S, N_BRANCH, D))
        merged = g[:, :, 0] * (ya @ w_pa[i]) + g[:, :, 1] * (yb @ w_pb[i]) + g[:, :, 2] * (yc @ w_pc[i])
        x = x + merged @ w_out[i]

        h = rms_norm(x, mlp_norm[i])
        u = causal_depthwise_conv(h @ w_up[i], conv_w[i], conv_b[i])
        gate_u, val_u = jnp.split(u, 2, axis=-1)
        x = x + (jax.nn.silu(gate_u) * val_u) @ w_down[i]
    return x


def setup_inputs(seed=0):
    out = dict(first_inputs(seed))
    for name, value in second_inputs(seed + 1).items():
        if name != "x":
            out[name + "_2"] = value
    return out


def reference(
    x, mem, ffn1_gate, ffn1_up, ffn1_down, w_in, conv_w, rec_lb, rec_norm_g, pool_w, pool_scale,
    w_out, ca_q, ca_k, ca_v, ca_o, ffn2_gate, ffn2_up, ffn2_down, ln_g, ln_b, attn_norm_2,
    w_in_2, qn_a_2, kn_a_2, qn_b_2, kn_b_2, sinks_2, qn_c_2, kn_c_2, lam_q1_2, lam_k1_2,
    lam_q2_2, lam_k2_2, subln_2, w_pa_2, w_pb_2, w_pc_2, w_out_2, mlp_norm_2, w_up_2, conv_w_2,
    conv_b_2, w_down_2,
):
    x = first_block(
        x, mem, ffn1_gate, ffn1_up, ffn1_down, w_in, conv_w, rec_lb, rec_norm_g, pool_w,
        pool_scale, w_out, ca_q, ca_k, ca_v, ca_o, ffn2_gate, ffn2_up, ffn2_down, ln_g, ln_b,
    )
    return second_block(
        x, attn_norm_2, w_in_2, qn_a_2, kn_a_2, qn_b_2, kn_b_2, sinks_2, qn_c_2, kn_c_2,
        lam_q1_2, lam_k1_2, lam_q2_2, lam_k2_2, subln_2, w_pa_2, w_pb_2, w_pc_2, w_out_2,
        mlp_norm_2, w_up_2, conv_w_2, conv_b_2, w_down_2,
    )


_drawn_inputs = setup_inputs


def setup_inputs(seed=0):
    import zlib

    import numpy as np

    out = dict(_drawn_inputs(seed))
    spreads = {}
    factors = {'rec_norm_g': 8.0,
     'pool_scale': 8.0,
     'attn_norm_2': 2.759,
     'qn_a_2': 8.0,
     'kn_a_2': 8.0,
     'qn_b_2': 8.0,
     'kn_b_2': 8.0,
     'sinks_2': 5.985,
     'qn_c_2': 6.21,
     'kn_c_2': 5.924,
     'lam_k1_2': 6.246,
     'subln_2': 4.83,
     'mlp_norm_2': 3.692,
     'conv_b_2': 6.39}
    for name, (base, spread) in spreads.items():
        noise = np.random.default_rng([zlib.crc32(name.encode()), seed]).standard_normal(out[name].shape)
        drawn = base * np.exp(spread * noise) if base else spread * noise
        out[name] = __import__('jax').numpy.asarray(drawn.astype(out[name].dtype))
    for name, factor in factors.items():
        out[name] = (out[name] * factor).astype(out[name].dtype)
    return out
```

```python
def build_program(nc, dram):
    from contextlib import ExitStack

    import concourse.bass as bass
    from concourse import mybir

    F32, F32R, U8 = mybir.dt.float32, mybir.dt.float32r, mybir.dt.uint8
    ALU, ACT, AX = mybir.AluOpType, mybir.ActivationFunctionType, mybir.AxisListType

    P = 128
    D = 1024
    KT = D // P
    TOK = 256
    TT = TOK // P
    DEPTH = 2
    STEPS = 2816 // 256
    ALPHA = (2.0 * DEPTH) ** 0.25
    LN_EPS, RMS_EPS = 1e-5, 1e-6
    CA_HEADS = 4
    CA_SCALE = (D // CA_HEADS) ** -0.5
    HEADS = 4
    LEVELS = [1, 2, 4, 8, 16, 32, 64]
    F_FLOOR = 2.0 ** -62

    A_FFN1 = 0
    A_RF, A_RQ, A_RI, A_RG = 33, 35, 37, 39
    A_CC, A_CH, A_CB, A_PU = 41, 42, 43, 44
    A_CK = 45
    A_WOUT = 49
    A_CQ, A_CV, A_CO = 53, 57, 61
    A_FFN2 = 65
    A_CHUNKS = 98
    SLOTS = 3

    B_QC, B_KC, B_QA, B_KA, B_QB, B_KVB, B_VA, B_VC = 0, 1, 2, 3, 4, 6, 7, 8
    B_GATE = 9
    B_WC, B_WA, B_WB = 21, 22, 23
    B_WOUT = 25
    B_FFN = 29
    B_CHUNKS = 62
    ZT = 13
    QK_EPS = 1e-6
    GROUPS = 5
    ROUNDS = [(0, 4, 2, 32, [(0, 2, 20), (2, 4, 21)]), (4, 8, 4, 64, [(4, 6, 16), (6, 8, 17)]),
              (8, 12, 6, 64, [(8, 12, 18)]), (12, 13, 2, 64, [(12, 13, 19)])]

    def uses(chunks, slot):
        return len(range(slot, chunks, SLOTS))

    with ExitStack() as ctx:
        def sb(name, shape, dt=F32):
            return ctx.enter_context(nc.sbuf_tensor(name, shape, dt))

        raw = sb("raw", [P, SLOTS, 2048])
        whi = sb("whi", [P, SLOTS, 2048], F32R)
        wlo = sb("wlo", [P, SLOTS, 2048], F32R)
        res = sb("res", [P, TT, D])
        xh = sb("xh", [P, KT, TOK], F32R)
        xl = sb("xl", [P, KT, TOK], F32R)
        yh = sb("yh", [P, KT, TOK], F32R)
        yl = sb("yl", [P, KT, TOK], F32R)
        mh = sb("mh", [P, KT, TOK], F32R)
        ml = sb("ml", [P, KT, TOK], F32R)
        work = sb("work", [P, 17, 1024])
        con = sb("con", [P, dram["con"].shape[1]])
        lvl_mask = sb("lvl_mask", [P, 8, P], U8)
        par = sb("par", [P, dram["par_a"].shape[2]])
        rlb = sb("rlb", [P, 2, HEADS])
        lbt = sb("lbt", [P, 2, 3, HEADS])
        lbc = sb("lbc", [P, 3, HEADS])
        lbw = sb("lbw", [P, 6, HEADS])
        poolw = sb("poolw", [P, 2, P])
        stat = sb("stat", [P, TT, 2, 6])
        mv = sb("mv", [P, TT, 2])
        vare = sb("vare", [P, TT])
        rstd = sb("rstd", [P, TT])
        mhalf = sb("mhalf", [P, 1])
        eps = sb("eps", [P, 1])
        held = sb("held", [P, 2])
        mx = sb("mx", [P, 8])
        nmx = sb("nmx", [P, 8])
        rsum = sb("rsum", [P, 8])
        rinv = sb("rinv", [P, 8])
        ps = ctx.enter_context(nc.psum_tensor("ps", [P, 8, 512], F32))

        parb = sb("parb", [P, dram["par_b"].shape[2]])
        rowb = sb("rowb", [P, dram["row_b"].shape[1]])
        lamw = sb("lamw", [P, 2, 32])
        lams = sb("lams", [P, 4])
        nlam = sb("nlam", [P, 1])
        subg = sb("subg", [P, 1])
        rlam = sb("rlam", [P, 8])
        sinkx = sb("sinkx", [P, 8])
        maskb = sb("maskb", [P, 3, P], mybir.dt.bfloat16)
        OB = sb("OB", [P, 512])
        ident = con[:, 0:128]
        mean128 = con[:, 128:256]
        ones = con[:, 256:384]
        invw = con[:, 384:386]
        edge = con[:, 386:418].rearrange("p (f t) -> p f t", f=2)
        first_half, second_half = con[:, 418:419], con[:, 419:420]

        def units(u, n=1):
            return work[:, u:u + n, :].rearrange("p u n -> p (u n)")

        sg = units(0).rearrange("p (b n) -> p b n", b=2)
        hg = units(1).rearrange("p (b n) -> p b n", b=2)
        tabg, tabb = units(5), units(6)
        ybuf = units(7, 2).rearrange("p (t n) -> p t n", t=TT)
        xf = units(3, 2).rearrange("p (k n) -> p k n", k=KT)
        Q = units(0)
        SIG = units(1)
        KEY = units(2)
        LOGF = units(3)
        EXPD = units(4)
        qlev = [units(5), units(7)]
        klev = [units(6), units(8)]
        AT = units(9).rearrange("p (g t) -> p g t", t=P)
        ATX = work[:, 10, 0:512].rearrange("p (h t) -> p h t", t=P)
        TMP = work[:, 10, 512:1024].rearrange("p (f t) -> p f t", t=TOK)
        VAL = units(11).rearrange("p (t n) -> p t n", t=TT)
        RG = units(12)
        CC = work[:, 13, 0:512].rearrange("p (f t) -> p f t", t=TOK)
        CH = work[:, 13, 512:1024].rearrange("p (f t) -> p f t", t=TOK)
        CB = work[:, 16, 0:512].rearrange("p (f t) -> p f t", t=TOK)
        PU = work[:, 16, 512:1024].rearrange("p (f t) -> p f t", t=TOK)
        CKT = units(14, 2).rearrange("p (k n) -> p k n", k=KT)
        CQT = units(0, 2).rearrange("p (k n) -> p k n", k=KT)
        CVM = units(3, 2).rearrange("p (t n) -> p t n", t=TT)
        PROB = units(7, 2).rearrange("p (g n) -> p g n", g=8)
        PROBT = units(11, 2).rearrange("p (g n) -> p g n", g=8)

        def ln_g(j, k):
            return par[:, j * 8 + k:j * 8 + k + 1]

        def ln_b(j, k):
            return par[:, 32 + j * 8 + k:32 + j * 8 + k + 1]

        def conv_w(tap, ft):
            return par[:, 64 + tap * 2 + ft:65 + tap * 2 + ft]

        def norm_g(h):
            return par[:, 70 + h:71 + h]

        def pool_scale(ft):
            return par[:, 74 + ft:75 + ft]

        flat = work[:].rearrange("p u n -> p (u n)")
        GATE = flat[:, 0:6144].rearrange("p (n c) -> p n c", c=512)
        nbuf = units(0, 2).rearrange("p (t n) -> p t n", t=TT)
        xf2 = units(2, 2).rearrange("p (k n) -> p k n", k=KT)
        junk = units(4)
        cvg = units(5).rearrange("p (b n) -> p b n", b=2)
        cvv = units(6).rearrange("p (b n) -> p b n", b=2)
        Z = flat[:, 6144:9472]
        RZ = flat[:, 9472:12800]
        PR = [flat[:, 9472:11008], flat[:, 11008:12544]]
        PT = flat[:, 12544:14080]
        VA = flat[:, 14080:14592].rearrange("p (t n) -> p t n", t=TT)
        VB = flat[:, 14592:14848].rearrange("p (t n) -> p t n", t=TT)
        VC = flat[:, 14848:15360].rearrange("p (t n) -> p t n", t=TT)
        CONB = flat[:, 15360:17152]
        rope = {64: (CONB[:, 0:256], CONB[:, 256:512]), 32: (CONB[:, 512:768], CONB[:, 768:1024])}
        headmean = {64: CONB[:, 1024:1152], 32: CONB[:, 1152:1280]}
        swap = {64: CONB[:, 1280:1408], 32: CONB[:, 1408:1536]}
        OC = flat[:, 16896:17408]
        CSQ = flat[:, 6144:6656]
        CRS = flat[:, 6656:7168]
        identb, trib, bandb = maskb[:, 0, :], maskb[:, 1, :], maskb[:, 2, :]

        def conv_b2(tile):
            return parb[:, bass.ds(25 + tile, 1)]

        def conv_w2(tap, tile):
            return parb[:, bass.ds(69 + 44 * tap + tile, 1)]

        class Signal:

            def __init__(self, name, per_layer, base=0, sem=None):
                self.sem = ctx.enter_context(nc.semaphore(name)) if sem is None else sem
                self.per_layer, self.base = per_layer, base

            def nth(self, l, n):
                return l * self.per_layer + (self.base + n)

            def again(self, per_layer):
                return Signal(None, per_layer, self.base + DEPTH * self.per_layer, self.sem)

        class Order:

            def __init__(self, eng, results):
                self.eng, self.results, self.n, self.l = eng, results, 0, None

            def layer(self, l):
                self.l, self.n = l, 0

            def next_decoder(self, results):
                self.close()
                self.results, self.l, self.n = results, None, results.base

            def put(self, instruction):
                instruction.then_inc(self.results.sem, 1)
                self.n += 1

            def settle(self):
                if self.l is None:
                    self.eng.wait_ge(self.results.sem, self.n)
                else:
                    self.eng.wait_ge(self.results.sem, self.results.nth(self.l, self.n))

            def close(self):
                want = self.results.base if self.l is None else self.results.per_layer
                assert self.n == want, (self.results.sem, self.n, want)

        raw_full = [Signal(f"raw_full{s}", 16 * uses(A_CHUNKS, s)) for s in range(SLOTS)]
        hi_ready = [Signal(f"hi_ready{s}", uses(A_CHUNKS, s)) for s in range(SLOTS)]
        split_ready = [Signal(f"split_ready{s}", uses(A_CHUNKS, s), 1) for s in range(SLOTS)]
        chunk_done = [Signal(f"chunk_done{s}", uses(A_CHUNKS, s), 1) for s in range(SLOTS)]

        inputs_in = Signal("inputs_in", 0)
        mem_in = Signal("mem_in", 0)
        params_in = Signal("params_in", 48)
        tables_in = Signal("tables_in", 4 * 32)
        const_set = Signal("const_set", 0)
        bounds_ready = Signal("bounds_ready", 0)
        bounds_exp = Signal("bounds_exp", 0)
        bounds_max = Signal("bounds_max", 0)

        gate_ready = Signal("gate_ready", 2 * STEPS)
        hidden_ready = Signal("hidden_ready", 2 * STEPS)
        hidden_hi = Signal("hidden_hi", 2 * STEPS)
        hidden_split = Signal("hidden_split", 2 * STEPS)

        var_ready = Signal("var_ready", 8)
        rstd_ready = Signal("rstd_ready", 8)
        normed = Signal("normed", 8)
        turned = Signal("turned", 16, 8)
        x_full = Signal("x_full", 16, 8)
        x_ready = Signal("x_ready", 16, 8)
        residual_ready = Signal("residual_ready", 4, 1)

        evacuated = Signal("evacuated", 24)
        floored = Signal("floored", 1)
        logs_ready = Signal("logs_ready", 1)
        keys_ready = Signal("keys_ready", 1)
        decay_ready = Signal("decay_ready", 1)
        spread_ready = Signal("spread_ready", 8)
        decay_exp = Signal("decay_exp", 8)
        level_ready = Signal("level_ready", 8)
        level_scored = Signal("level_scored", 9)
        level_merged = Signal("level_merged", 8)
        cross_ready = Signal("cross_ready", 1)
        o_ready = Signal("o_ready", 1)
        o_squared = Signal("o_squared", 1)
        o_summed = Signal("o_summed", 1)
        o_rstd = Signal("o_rstd", 1)
        gate_exp = Signal("gate_exp", 1)
        rec_full = Signal("rec_full", 1)
        rec_hi = Signal("rec_hi", 1)
        rec_ready = Signal("rec_ready", 1)
        conv_ready = Signal("conv_ready", 1)
        windows_ready = Signal("windows_ready", 1)
        pooled = Signal("pooled", 1)
        pool_full = Signal("pool_full", 1)
        pool_ready = Signal("pool_ready", 1)

        scored = Signal("scored", 2)
        max_ready = Signal("max_ready", 2)
        prob_ready = Signal("prob_ready", 2)
        prob_normed = Signal("prob_normed", 2)
        prob_turned = Signal("prob_turned", 4)
        probt_act = Signal("probt_act", 2)
        probt_dve = Signal("probt_dve", 2)
        attn_ready = Signal("attn_ready", 4)
        attn_hi = Signal("attn_hi", 4)
        attn_split = Signal("attn_split", 4)

        act_order = Signal("act_order", 3)
        dve_order = Signal("dve_order", 84, 22)
        pool_order = Signal("pool_order", 43, 2)
        out_stored = Signal("out_stored", 0)

        class Ring:

            def __init__(self, full, hi, split, done, chunks):
                self.full, self.hi, self.split, self.done, self.chunks = full, hi, split, done, chunks

        A = Ring(raw_full, hi_ready, split_ready, chunk_done, A_CHUNKS)
        B = Ring([raw_full[s].again(16 * uses(B_CHUNKS, s)) for s in range(SLOTS)],
                 *[[kind[s].again(uses(B_CHUNKS, s)) for s in range(SLOTS)] for kind in (hi_ready, split_ready, chunk_done)],
                 B_CHUNKS)

        b_params_in = Signal("b_params_in", 32)
        b_consts_in = Signal("b_consts_in", 0)
        b_masks_set = Signal("b_masks_set", 0)
        b_hidden_ready, b_hidden_hi, b_hidden_split, b_gate_ready = [
            x.again(STEPS) for x in (hidden_ready, hidden_hi, hidden_split, gate_ready)]
        b_gate_scaled = Signal("b_gate_scaled", STEPS)
        b_gate_conv = Signal("b_gate_conv", STEPS)
        b_value_scaled = Signal("b_value_scaled", STEPS)
        b_value_conv = Signal("b_value_conv", STEPS)
        b_taps = Signal("b_taps", 6 * STEPS)
        b_res_ready = Signal("b_res_ready", 4, 1)
        b_squares = Signal("b_squares", 4)
        b_var_ready, b_rstd_ready, b_normed = [x.again(4) for x in (var_ready, rstd_ready, normed)]
        b_turned, b_x_full, b_x_ready = [x.again(8) for x in (turned, x_full, x_ready)]
        b_evacuated = Signal("b_evacuated", 21)
        b_summed = Signal("b_summed", 4)
        b_qk_rstd = Signal("b_qk_rstd", 4)
        b_qk_normed = Signal("b_qk_normed", 4)
        b_rotated = Signal("b_rotated", 4)
        b_sine = Signal("b_sine", 4)
        b_roped = Signal("b_roped", 4)
        b_cosine = Signal("b_cosine", 4)
        b_lam_sums = Signal("b_lam_sums", 1)
        b_lam_exp = Signal("b_lam_exp", 1)
        b_scored = Signal("b_scored", GROUPS)
        b_row_scored = Signal("b_row_scored", 3 * 2 + 3)
        b_max = Signal("b_max", GROUPS)
        b_prob = Signal("b_prob", GROUPS)
        b_prob_normed = Signal("b_prob_normed", GROUPS)
        b_prob_turned = Signal("b_prob_turned", GROUPS)
        b_pt_act = Signal("b_pt_act", GROUPS)
        b_pt_dve = Signal("b_pt_dve", GROUPS)
        b_pv = Signal("b_pv", GROUPS)
        b_o_out = Signal("b_o_out", GROUPS)
        b_y_ready = Signal("b_y_ready", 3)
        b_c_squared = Signal("b_c_squared", 1)
        b_c_summed = Signal("b_c_summed", 1)
        b_c_rstd = Signal("b_c_rstd", 1)
        b_yc_ready = Signal("b_yc_ready", 1)
        b_gates_open = Signal("b_gates_open", 3)
        b_branch_done = Signal("b_branch_done", 12)
        b_gated = Signal("b_gated", 12)
        b_pair_merged = Signal("b_pair_merged", 4)
        b_merge_ready = Signal("b_merge_ready", 4)
        act_order_b = act_order.again(9)
        dve_order_b = dve_order.again(60)
        pool_order_b = pool_order.again(0)

        def chunk(c, more=0):
            return c % SLOTS, c // SLOTS + more

        def chunk_wait(eng, l, c, more=0, ring=A):
            s, u = chunk(c, more)
            eng.wait_ge(ring.done[s].sem, ring.done[s].nth(l, u + 1))

        block = ctx.enter_context(nc.Block())

        @block.sync
        def _(sp):
            sp.dma_start(con[:], dram["con"]).then_inc(inputs_in.sem, 16)
            sp.dma_start(res[:], dram["x"].rearrange("(t p) n -> p t n", p=P)).then_inc(inputs_in.sem, 16)
            sp.dma_start(units(11), dram["lvl_mask"]).then_inc(inputs_in.sem, 16)
            sp.dma_start(rlb[:], dram["rec_lb"].rearrange("p (l h) -> p l h", l=2)).then_inc(inputs_in.sem, 16)
            sp.dma_start(units(9, 2).rearrange("p (t n) -> p t n", t=TT),
                         dram["mem"].rearrange("(t p) n -> p t n", p=P)).then_inc(mem_in.sem, 16)

            def load(ring, l, s, u, src):
                sp.wait_ge(ring.split[s].sem, ring.split[s].nth(l, u))
                sp.dma_start(raw[:, s, :], src).then_inc(ring.full[s].sem, 16)

            for ring, name in ((A, "stream_a"), (B, "stream_b")):
                stream, count = dram[name], ring.chunks
                with sp.Fori(0, DEPTH) as l:
                    with sp.Fori(0, count // SLOTS) as u:
                        for s in range(SLOTS):
                            load(ring, l, s, u, stream[bass.ds(l * (count * P) + u * (SLOTS * P) + s * P, P), :])
                    for c in range(count // SLOTS * SLOTS, count):
                        load(ring, l, c % SLOTS, c // SLOTS, stream[bass.ds(l * (count * P) + c * P, P), :])

            sp.wait_ge(b_res_ready.sem, b_res_ready.nth(DEPTH, 0))
            sp.dma_start(dram["out"].rearrange("(t p) n -> p t n", p=P), res[:]).then_inc(out_stored.sem, 16)
            sp.wait_ge(out_stored.sem, 16)

        @block.tensor
        def _(pe):
            def chunk_in(l, c, more=0, ring=A):
                s, u = chunk(c, more)
                pe.wait_ge(ring.split[s].sem, ring.split[s].nth(l, u + 1))

            def parts(s, tiles):
                n = 2048 // tiles
                return (whi[:, s, :].rearrange("p (k n) -> p k n", n=n),
                        wlo[:, s, :].rearrange("p (k n) -> p k n", n=n))

            def feature_tiles(l, c, bank, ah, al, more=0, ring=A):
                chunk_in(l, c, more, ring)
                s, _ = chunk(c, more)
                wh, wl = parts(s, KT)
                for ft in range(2):
                    out = ps[:, bank, ft * TOK:(ft + 1) * TOK]
                    cols = slice(ft * P, (ft + 1) * P)
                    for k in range(KT):
                        nc.tensor.matmul(out, wh[:, k, cols], ah[:, k, :], start=(k == 0), stop=False)
                        nc.tensor.matmul(out, wh[:, k, cols], al[:, k, :], start=False, stop=False)
                        last = nc.tensor.matmul(out, wl[:, k, cols], ah[:, k, :], start=False, stop=(k == KT - 1))
                last.then_inc(chunk_done[s].sem, 1)

            def token_tiles(l, c, bank, ah, al, ring=A):
                chunk_in(l, c, 0, ring)
                s, _ = chunk(c)
                wh, wl = parts(s, KT)
                for t in range(TT):
                    out = ps[:, bank, t * 256:(t + 1) * 256]
                    rows = slice(t * P, (t + 1) * P)
                    for k in range(KT):
                        nc.tensor.matmul(out, ah[:, k, rows], wh[:, k, :], start=(k == 0), stop=False)
                        nc.tensor.matmul(out, ah[:, k, rows], wl[:, k, :], start=False, stop=False)
                        last = nc.tensor.matmul(out, al[:, k, rows], wh[:, k, :], start=False, stop=(k == KT - 1))
                last.then_inc(chunk_done[s].sem, 1)

            def accumulate(l, c, ah, al, first, final, more=0, ring=A):
                chunk_in(l, c, more, ring)
                s, _ = chunk(c, more)
                wh, wl = parts(s, 2)
                for k in range(2):
                    for t in range(TT):
                        rows = slice(t * P, (t + 1) * P)
                        for n, (a, w) in enumerate(((ah, wh), (ah, wl), (al, wh))):
                            for half in range(2):
                                last = nc.tensor.matmul(
                                    ps[:, 4 + 2 * t + half, :], a[:, k, rows], w[:, k, half * 512:(half + 1) * 512],
                                    start=(first and k == 0 and n == 0), stop=(final and k == 1 and n == 2))
                last.then_inc(chunk_done[s].sem, 1)

            def turn(src, bank0, done=turned):
                for t in range(TT):
                    yield t
                    for k in range(KT):
                        last = nc.tensor.transpose(
                            ps[:, bank0 + k // 2, (k % 2) * TOK + t * P:(k % 2) * TOK + (t + 1) * P],
                            src[:, t, k * P:(k + 1) * P], ident)
                        if t == TT - 1 and k % 2 == 1:
                            last.then_inc(turned.sem, 1)

            def ffn(l, c0, f, ring=A, ready=hidden_ready, split=hidden_split):
                def pair(i, more):
                    if i >= 2:
                        pe.wait_ge(ready.sem, ready.nth(l, f * STEPS + i - 1 + more))
                    b = 2 * (i % 2)
                    c = c0 if i == 0 else c0 + 2 + 3 * (i - 1)
                    feature_tiles(l, c, b, xh, xl, more, ring)
                    feature_tiles(l, c + 1, b + 1, xh, xl, more, ring)

                def down(i, more):
                    b = i % 2
                    pe.wait_ge(split.sem, split.nth(l, f * STEPS + i + 1 + more))
                    c = c0 + 2 + 3 * i + 2 if i < STEPS - 1 else c0 + 3 * STEPS - 1
                    accumulate(l, c, yh[:, 2 * b:2 * b + 2, :], yl[:, 2 * b:2 * b + 2, :],
                               i == 0, i == STEPS - 1, more, ring)

                pair(0, 0)
                for i in (1, 2):
                    pair(i, 0)
                    down(i - 1, 0)
                with pe.Fori(0, (STEPS - 3) // 2) as r:
                    for i in (3, 4):
                        pair(i, 2 * r)
                        down(i - 1, 2 * r)
                down(STEPS - 1, 0)

            def norm_turn(l, j):
                for t in turn(ybuf, 0):
                    pe.wait_ge(normed.sem, normed.nth(l, 2 * j + t + 1))

            def level(l, n):
                b = 4 + 2 * (n % 2)
                if n == 0:
                    pe.wait_ge(keys_ready.sem, keys_ready.nth(l, 1))
                    pe.wait_ge(evacuated.sem, evacuated.nth(l, 4))
                else:
                    pe.wait_ge(level_ready.sem, level_ready.nth(l, n))
                if n == 3:
                    pe.wait_ge(cross_ready.sem, cross_ready.nth(l, 1))
                elif n >= 2:
                    pe.wait_ge(level_merged.sem, level_merged.nth(l, max(n - 2, 1)))
                q, k = (Q, KEY) if n == 0 else (qlev[n % 2], klev[n % 2])
                if n == 1:
                    for h in range(HEADS):
                        last = nc.tensor.matmul(ps[:, b, h * P:(h + 1) * P], k[:, h * TOK:h * TOK + P],
                                                q[:, h * TOK + P:(h + 1) * TOK], start=True, stop=True)
                else:
                    for g in range(HEADS * TT):
                        last = nc.tensor.matmul(ps[:, b + g // 4, (g % 4) * P:(g % 4 + 1) * P],
                                                k[:, g * P:(g + 1) * P], q[:, g * P:(g + 1) * P], start=True, stop=True)
                last.then_inc(level_scored.sem, 1)

            def recurrence_out(l):
                pe.wait_ge(level_merged.sem, level_merged.nth(l, 8))
                pe.wait_ge(cross_ready.sem, cross_ready.nth(l, 1))
                pe.wait_ge(evacuated.sem, evacuated.nth(l, 6))
                for h in range(HEADS):
                    v = [VAL[:, t, h * P:(h + 1) * P] for t in range(TT)]
                    out = ps[:, 4 + h // 2, (h % 2) * TOK:(h % 2 + 1) * TOK]
                    nc.tensor.matmul(out[:, 0:P], v[0], AT[:, 2 * h, :], start=True, stop=True)
                    nc.tensor.matmul(out[:, P:TOK], v[0], ATX[:, h, :], start=True, stop=False)
                    last = nc.tensor.matmul(out[:, P:TOK], v[1], AT[:, 2 * h + 1, :], start=False, stop=True)
                last.then_inc(o_ready.sem, 1)

            def recurrence_sums(l):
                pe.wait_ge(o_squared.sem, o_squared.nth(l, 1))
                for b in range(2):
                    last = nc.tensor.matmul(ps[:, 6 + b, :], mean128, EXPD[:, b * 512:(b + 1) * 512], start=True, stop=True)
                last.then_inc(o_summed.sem, 1)

            def mixer(l):
                def bank(c):
                    n = c - A_RF
                    if n >= 4:
                        pe.wait_ge(evacuated.sem, evacuated.nth(l, n - 3))
                    return n % 4

                pe.wait_ge(x_ready.sem, x_ready.nth(l, 4))
                pe.wait_ge(hidden_ready.sem, hidden_ready.nth(l, STEPS))
                for c in range(A_RF, A_WOUT):
                    b = bank(c)
                    if A_RI <= c < A_RG:
                        token_tiles(l, c, b, xh, xl)
                    elif c >= A_CK:
                        feature_tiles(l, c, b, mh, ml)
                    else:
                        feature_tiles(l, c, b, xh, xl)
                    if A_RI <= c < A_RI + 9:
                        level(l, c - A_RI)
                    if c == A_CK + 2:
                        recurrence_out(l)
                recurrence_sums(l)

                pe.wait_ge(windows_ready.sem, windows_ready.nth(l, 1))
                pe.wait_ge(params_in.sem, params_in.nth(l, 48))
                pe.wait_ge(evacuated.sem, evacuated.nth(l, 16))
                for ft in range(2):
                    last = nc.tensor.matmul(ps[:, 0, ft * TOK:(ft + 1) * TOK], poolw[:, ft, :], TMP[:, ft, :],
                                            start=True, stop=True)
                last.then_inc(pooled.sem, 1)

                pe.wait_ge(conv_ready.sem, conv_ready.nth(l, 1))
                pe.wait_ge(pool_ready.sem, pool_ready.nth(l, 1))
                pe.wait_ge(rec_full.sem, rec_full.nth(l, 1))
                for n, tiles in enumerate((0, 6, 2, 4)):
                    if n == 2:
                        pe.wait_ge(rec_ready.sem, rec_ready.nth(l, 1))
                    accumulate(l, A_WOUT + n, yh[:, tiles:tiles + 2, :], yl[:, tiles:tiles + 2, :], n == 0, n == 3)

            def cross_attention(l):
                pe.wait_ge(x_ready.sem, x_ready.nth(l, 8))
                for n in range(4):
                    feature_tiles(l, A_CQ + n, n, xh, xl)
                pe.wait_ge(evacuated.sem, evacuated.nth(l, 20))
                for t in range(TT):
                    for h in range(CA_HEADS):
                        out = ps[:, 4 + 2 * t + h // 2, (h % 2) * 256:(h % 2 + 1) * 256]
                        for k in range(2):
                            last = nc.tensor.matmul(out, CQT[:, 2 * h + k, t * P:(t + 1) * P], CKT[:, 2 * h + k, :],
                                                    start=(k == 0), stop=(k == 1))
                    last.then_inc(scored.sem, 1)
                for n in range(4):
                    token_tiles(l, A_CV + n, n, mh, ml)
                for t in range(TT):
                    pe.wait_ge(prob_normed.sem, prob_normed.nth(l, 2))
                    for mt in range(2):
                        for h in range(CA_HEADS):
                            g = mt * CA_HEADS + h
                            last = nc.tensor.transpose(
                                ps[:, 4 + g // 2, (g % 2) * TOK + t * P:(g % 2) * TOK + (t + 1) * P],
                                PROB[:, t * CA_HEADS + h, mt * P:(mt + 1) * P], ident)
                            if t == TT - 1 and g % 2 == 1:
                                last.then_inc(prob_turned.sem, 1)
                pe.wait_ge(probt_act.sem, probt_act.nth(l, 2))
                pe.wait_ge(probt_dve.sem, probt_dve.nth(l, 2))
                pe.wait_ge(evacuated.sem, evacuated.nth(l, 24))
                for ft in range(KT):
                    for mt in range(2):
                        last = nc.tensor.matmul(ps[:, ft // 2, (ft % 2) * TOK:(ft % 2 + 1) * TOK],
                                                CVM[:, mt, ft * P:(ft + 1) * P],
                                                PROBT[:, mt * CA_HEADS + ft // 2, :], start=(mt == 0), stop=(mt == 1))
                    if ft % 2 == 1:
                        last.then_inc(attn_ready.sem, 1)
                for n in range(4):
                    pe.wait_ge(attn_split.sem, attn_split.nth(l, n + 1))
                    accumulate(l, A_CO + n, yh[:, 2 * n:2 * n + 2, :], yl[:, 2 * n:2 * n + 2, :], n == 0, n == 3)

            for s in range(SLOTS):
                pe.sem_inc(chunk_done[s].sem, 1)
            pe.wait_ge(inputs_in.sem, 64)
            for _ in turn(res, 0):
                pass
            pe.wait_ge(mem_in.sem, 16)
            for _ in turn(units(9, 2).rearrange("p (t n) -> p t n", t=TT), 4):
                pass
            with pe.Fori(0, DEPTH) as l:
                pe.wait_ge(x_ready.sem, x_ready.nth(l, 0))
                ffn(l, A_FFN1, 0)
                norm_turn(l, 0)
                mixer(l)
                norm_turn(l, 1)
                cross_attention(l)
                norm_turn(l, 2)
                pe.wait_ge(x_ready.sem, x_ready.nth(l, 12))
                ffn(l, A_FFN2, 1)
                norm_turn(l, 3)

            def rms_turn(l, j):
                for t in turn(nbuf, 0):
                    pe.wait_ge(b_normed.sem, b_normed.nth(l, 2 * j + t + 1))
                pe.wait_ge(b_x_ready.sem, b_x_ready.nth(l, 4 * j + 4))

            def head_sums(l, r):
                z0, z1, bank, dim, _ = ROUNDS[r]
                pe.wait_ge(b_evacuated.sem, b_evacuated.nth(l, (2, 4, 6, 7)[r]))
                if r == 3:
                    pe.wait_ge(b_sine.sem, b_sine.nth(l, 1))
                for n, z in enumerate(range(z0, z1, 2)):
                    w = min(2, z1 - z) * TOK
                    last = nc.tensor.matmul(ps[:, bank + n, 0:w], headmean[dim], RZ[:, z * TOK:z * TOK + w], start=True, stop=True)
                last.then_inc(b_summed.sem, 1)

            def rotate(l, r):
                z0, z1, bank, dim, _ = ROUNDS[r]
                pe.wait_ge(b_qk_normed.sem, b_qk_normed.nth(l, r + 1))
                for n, z in enumerate(range(z0, z1, 2)):
                    w = min(2, z1 - z) * TOK
                    last = nc.tensor.matmul(ps[:, bank + n, 0:w], swap[dim], Z[:, z * TOK:z * TOK + w], start=True, stop=True)
                last.then_inc(b_rotated.sem, 1)

            def rows_of(g):
                if g < 2:
                    return [(g, 2 + g, slice(32 * j, 32 * j + 32)) for j in range(4)]
                tile = 4 if g == 2 else 8 + 2 * (g - 3)
                return [(tile + j // 2, 6 + j // 2 if g == 2 else 12, slice(64 * (j % 2), 64 * (j % 2) + 64)) for j in range(4)]

            def scores(l, g):
                if g == 0:
                    pe.wait_ge(b_roped.sem, b_roped.nth(l, 4))
                    pe.wait_ge(b_sine.sem, b_sine.nth(l, 4))
                else:
                    pe.wait_ge(b_prob.sem, b_prob.nth(l, g))
                turns = list(range(4)) if g < 2 else [0, 2, 1, 3]
                for n, j in enumerate(turns):
                    qt, kt, rows = rows_of(g)[j]
                    if n and rows != rows_of(g)[turns[n - 1]][2]:
                        pe.wait_ge(b_row_scored.sem, b_row_scored.nth(l, 3 * g + n if g < 2 else 6 + g - 1))
                    q, k = [Z[rows, z * TOK:(z + 1) * TOK] for z in (qt, kt)]
                    for out, qs, ks, mask in (
                            (ps[:, 2, j * P:(j + 1) * P], 0, 0, trib),
                            (ps[:, 3 + j // 2, (j % 2) * 256:(j % 2) * 256 + P], P, 0, bandb if g >= 3 else None),
                            (ps[:, 3 + j // 2, (j % 2) * 256 + P:(j % 2 + 1) * 256], P, P, trib)):
                        last = nc.tensor.matmul(out, q[:, qs:qs + P], k[:, ks:ks + P], start=True, stop=mask is None)
                        if mask is not None:
                            last = nc.tensor.matmul(out, identb, mask, start=False, stop=True)
                    if n < 3 and rows != rows_of(g)[turns[n + 1]][2]:
                        last.then_inc(b_row_scored.sem, 1)
                last.then_inc(b_scored.sem, 1)

            def heads_of(g):
                return 2 if g < 2 else 4

            def prob_turn(l, g):
                pe.wait_ge(b_prob_normed.sem, b_prob_normed.nth(l, g + 1))
                if g:
                    pe.wait_ge(b_o_out.sem, b_o_out.nth(l, g))
                first = PR[g % 2][:, 0:512].rearrange("p (j n) -> p j n", n=P)
                second = PR[g % 2][:, 512:1536].rearrange("p (j n) -> p j n", n=256)
                for n in range(heads_of(g)):
                    j = 2 * n if g < 2 else n
                    near = ps[:, 5 + n // 2, (n % 2) * TOK:(n % 2 + 1) * TOK]
                    nc.tensor.transpose(near[:, 0:P], first[:, j, :], ident)
                    nc.tensor.transpose(near[:, P:TOK], second[:, j, 0:P], ident)
                    last = nc.tensor.transpose(ps[:, 7, n * P:(n + 1) * P], second[:, j, P:256], ident)
                last.then_inc(b_prob_turned.sem, 1)

            def values(l, g):
                pe.wait_ge(b_pt_act.sem, b_pt_act.nth(l, g + 1))
                pe.wait_ge(b_pt_dve.sem, b_pt_dve.nth(l, g + 1))
                for n in range(heads_of(g)):
                    v, head = (VC, 2 * g + n) if g < 2 else (VA, n) if g == 2 else (VB, n % 2)
                    v = v[:, :, head * 64:(head + 1) * 64]
                    out = ps[64 * (n % 2):64 * (n % 2) + 64, 5, (n // 2) * TOK:(n // 2 + 1) * TOK]
                    near, far = PT[:, n * TOK:(n + 1) * TOK], PT[:, 1024 + n * P:1024 + (n + 1) * P]
                    nc.tensor.matmul(out[:, 0:P], v[:, 0, :], near[:, 0:P], start=True, stop=True)
                    nc.tensor.matmul(out[:, P:TOK], v[:, 0, :], near[:, P:TOK], start=True, stop=False)
                    last = nc.tensor.matmul(out[:, P:TOK], v[:, 1, :], far, start=False, stop=True)
                last.then_inc(b_pv.sem, 1)

            def attention(l):
                for c in range(B_GATE + 12):
                    bank = c % 2
                    if c >= 2:
                        pe.wait_ge(b_evacuated.sem, b_evacuated.nth(l, c - 1))
                    if c == B_KVB:
                        chunk_in(l, c, 0, B)
                        s, _ = chunk(c)
                        wh, wl = parts(s, KT)
                        out = ps[:, bank, 0:TOK]
                        for k in range(KT):
                            nc.tensor.matmul(out, wh[:, k, 0:P], xh[:, k, :], start=(k == 0), stop=False)
                            nc.tensor.matmul(out, wh[:, k, 0:P], xl[:, k, :], start=False, stop=False)
                            nc.tensor.matmul(out, wl[:, k, 0:P], xh[:, k, :], start=False, stop=(k == KT - 1))
                        for t in range(TT):
                            out = ps[:, bank, TOK + t * P:TOK + (t + 1) * P]
                            rows = slice(t * P, (t + 1) * P)
                            for k in range(KT):
                                nc.tensor.matmul(out, xh[:, k, rows], wh[:, k, P:256], start=(k == 0), stop=False)
                                nc.tensor.matmul(out, xh[:, k, rows], wl[:, k, P:256], start=False, stop=False)
                                last = nc.tensor.matmul(out, xl[:, k, rows], wh[:, k, P:256], start=False, stop=(k == KT - 1))
                        last.then_inc(chunk_done[s].sem, 1)
                    elif c in (B_VA, B_VC):
                        token_tiles(l, c, bank, xh, xl, B)
                    else:
                        feature_tiles(l, c, bank, xh, xl, 0, B)
                    if c in (2, 4, 6, 8):
                        head_sums(l, c // 2 - 1)
                    if c in (4, 6, 8, 10):
                        rotate(l, c // 2 - 2)
                    g = c - (B_GATE + 3)
                    if 2 <= g < GROUPS + 2:
                        values(l, g - 2)
                    if 0 <= g < GROUPS:
                        scores(l, g)
                    if 1 <= g < GROUPS + 1:
                        prob_turn(l, g - 1)
                    if g == GROUPS:
                        pe.wait_ge(b_c_squared.sem, b_c_squared.nth(l, 1))
                        nc.tensor.matmul(ps[:, 2, :], headmean[64], CSQ, start=True, stop=True).then_inc(b_c_summed.sem, 1)

            def branch(l, chunks, y0, bank0):
                for c in chunks:
                    chunk_in(l, c, 0, B)
                both = [parts(c % SLOTS, 2) for c in chunks]
                for ft in range(KT):
                    cols = slice(ft * P, (ft + 1) * P)
                    out = ps[:, bank0 + ft // 2, (ft % 2) * TOK:(ft % 2 + 1) * TOK]
                    steps = [(wh, wl, k, y0 + 2 * n + k) for n, (wh, wl) in enumerate(both) for k in range(2)]
                    for n, (wh, wl, k, y) in enumerate(steps):
                        nc.tensor.matmul(out, wh[:, k, cols], yh[:, y, :], start=(n == 0), stop=False)
                        nc.tensor.matmul(out, wh[:, k, cols], yl[:, y, :], start=False, stop=False)
                        last = nc.tensor.matmul(out, wl[:, k, cols], yh[:, y, :], start=False, stop=(n == len(steps) - 1))
                    if ft % 2 == 1:
                        last.then_inc(b_branch_done.sem, 1)
                for c in chunks:
                    pe.wait_ge(b_branch_done.sem, b_branch_done.nth(l, 4 * (1 + (B_WC, B_WA, B_WB).index(chunks[0]))))
                    pe.sem_inc(chunk_done[c % SLOTS].sem, 1)

            def merge(l):
                pe.wait_ge(b_evacuated.sem, b_evacuated.nth(l, 21))
                pe.wait_ge(b_c_rstd.sem, b_c_rstd.nth(l, 1))
                pe.wait_ge(b_yc_ready.sem, b_yc_ready.nth(l, 1))
                branch(l, [B_WC], 6, 0)
                pe.wait_ge(b_o_out.sem, b_o_out.nth(l, GROUPS))
                pe.wait_ge(b_y_ready.sem, b_y_ready.nth(l, 1))
                branch(l, [B_WA], 0, 4)
                pe.wait_ge(b_y_ready.sem, b_y_ready.nth(l, 3))
                pe.wait_ge(b_gated.sem, b_gated.nth(l, 4))
                branch(l, [B_WB, B_WB + 1], 2, 0)
                pe.wait_ge(b_gated.sem, b_gated.nth(l, 8))
                for n in range(4):
                    pe.wait_ge(b_merge_ready.sem, b_merge_ready.nth(l, n + 1))
                    accumulate(l, B_WOUT + n, xh[:, 2 * n:2 * n + 2, :], xl[:, 2 * n:2 * n + 2, :], n == 0, n == 3, 0, B)

            pe.wait_ge(b_consts_in.sem, 16)
            pe.wait_ge(b_masks_set.sem, 2)
            with pe.Fori(0, DEPTH) as l:
                rms_turn(l, 0)
                attention(l)
                merge(l)
                rms_turn(l, 1)
                ffn(l, B_FFN, 0, B, b_hidden_ready, b_hidden_split)

        @block.scalar
        def _(act):
            order = Order(act, act_order)

            def high(l, c, more=0, ring=A):
                if isinstance(more, int) and c + 3 * more >= ring.chunks:
                    return
                s, u = chunk(c, more)
                act.wait_ge(ring.full[s].sem, ring.full[s].nth(l, (u + 1) * 16))
                act.wait_ge(ring.done[s].sem, ring.done[s].nth(l, u))
                nc.scalar.activation(whi[:, s, :], raw[:, s, :], ACT.Copy).then_inc(hi_ready[s].sem, 1)

            def ffn(l, c0, f):
                def step(i, more):
                    b, c = i % 2, c0 + 2 + 3 * (i - 1)
                    if i == 0:
                        c = c0
                    n = f * STEPS + i + more
                    high(l, c + 2, more)
                    chunk_wait(act, l, c, more)
                    if i >= 2:
                        act.wait_ge(hidden_ready.sem, hidden_ready.nth(l, n - 1))
                    nc.scalar.activation(sg[:, b, :], ps[:, 2 * b, :], ACT.Silu).then_inc(gate_ready.sem, 1)
                    high(l, c + 3, more)
                    if i:
                        high(l, c + 4, more)
                    act.wait_ge(hidden_ready.sem, hidden_ready.nth(l, n + 1))
                    nc.scalar.activation(yh[:, 2 * b:2 * b + 2, :], hg[:, b, :].rearrange("p (k n) -> p k n", k=2),
                                         ACT.Copy).then_inc(hidden_hi.sem, 1)

                for i in range(3):
                    step(i, 0)
                with act.Fori(0, (STEPS - 5) // 2) as r:
                    for i in (3, 4):
                        step(i, 2 * r)
                for i in (STEPS - 2, STEPS - 1):
                    step(i, 0)
                high(l, c0 + 3 * STEPS - 1 + 2)

            def widen(l, n, j):
                for b in range(4):
                    act.wait_ge(turned.sem, turned.nth(l, n + b + 1))
                    if j is None:
                        nc.scalar.activation(xf[:, 2 * b:2 * b + 2, :],
                                             ps[:, n + 8 + b if n == -4 else b, :].rearrange("p (k n) -> p k n", k=2),
                                             ACT.Copy).then_inc(x_full.sem, 1)
                        continue
                    for k in (2 * b, 2 * b + 1):
                        last = nc.scalar.activation(xf[:, k, :], ps[:, b, (k % 2) * TOK:(k % 2 + 1) * TOK], ACT.Identity,
                                                    scale=ln_g(j, k), bias=ln_b(j, k))
                    last.then_inc(x_full.sem, 1)

            def mixer(l):
                def half(buf, n):
                    return buf[:, n * 512:(n + 1) * 512]

                homes = {A_RF: half(SIG, 0), A_RF + 1: half(SIG, 1), A_RQ: half(Q, 0), A_RQ + 1: half(Q, 1),
                         A_RG: half(RG, 0), A_RG + 1: half(RG, 1), A_CC: CC, A_CH: CH, A_CB: CB, A_PU: PU}
                for n in range(4):
                    homes[A_CK + n] = CKT[:, 2 * n:2 * n + 2, :]
                for n in range(2):
                    homes[A_RI + n] = VAL[:, :, n * 256:(n + 1) * 256]

                def spread(buf, side, h):
                    return buf.rearrange("p (n s h) -> p n s h", s=2, h=h)[:, :, side, :]

                def decays(n):
                    if n == 1:
                        act.wait_ge(decay_ready.sem, decay_ready.nth(l, 1))
                    act.wait_ge(spread_ready.sem, spread_ready.nth(l, n))
                    if n >= 2:
                        act.wait_ge(level_ready.sem, level_ready.nth(l, n - 1))
                    h = P if n == 1 else LEVELS[::-1][n - 2]
                    late = SIG if n == 1 else LOGF
                    nc.scalar.activation(spread(EXPD, 1, h), spread(late, 1, h), ACT.Exp)
                    nc.scalar.activation(spread(EXPD, 0, h), spread(LOGF, 0, h), ACT.Exp, scale=-1.0)\
                        .then_inc(decay_exp.sem, 1)

                for c in range(A_RF, A_WOUT):
                    high(l, c + 2)
                    chunk_wait(act, l, c)
                    if c == A_CK:
                        pass
                    out = homes[c]
                    src = ps[:, (c - A_RF) % 4, :]
                    if len(out.shape) == 3:
                        src = src.rearrange("p (a n) -> p a n", a=2)
                    if c == A_RF:
                        act.wait_ge(x_ready.sem, x_ready.nth(l, 4))
                    nc.scalar.activation(out, src, ACT.Sigmoid if c < A_RQ else ACT.Copy).then_inc(evacuated.sem, 1)
                    if c == A_RF + 1:
                        act.wait_ge(floored.sem, floored.nth(l, 1))
                        for h in range(HEADS):
                            s = slice(h * TOK, (h + 1) * TOK)
                            last = nc.scalar.activation(LOGF[:, s], SIG[:, s], ACT.Ln,
                                                        scale=lbc[:, 1, h:h + 1], bias=lbc[:, 0, h:h + 1])
                        last.then_inc(logs_ready.sem, 1)
                    if A_RQ + 1 <= c < A_RQ + 9:
                        decays(c - A_RQ)
                    if c == A_RI + 3:
                        act.wait_ge(level_scored.sem, level_scored.nth(l, 2))
                        nc.scalar.activation(ATX, ps[:, 6, :].rearrange("p (h t) -> p h t", t=P), ACT.Copy)\
                            .then_inc(cross_ready.sem, 1)
                    if c == A_CC:
                        act.wait_ge(evacuated.sem, evacuated.nth(l, 8))
                        nc.scalar.activation(RG, RG, ACT.Exp, scale=-1.0).then_inc(gate_exp.sem, 1)
                act.wait_ge(o_ready.sem, o_ready.nth(l, 1))
                act.wait_ge(level_ready.sem, level_ready.nth(l, 8))
                nc.scalar.activation(EXPD, ps[:, 4:6, :].rearrange("p b n -> p (b n)"), ACT.Square)\
                    .then_inc(o_squared.sem, 1)
                act.wait_ge(o_summed.sem, o_summed.nth(l, 1))
                order.put(nc.scalar.activation(LOGF, ps[:, 6:8, :].rearrange("p b n -> p (b n)"), ACT.Ln, bias=eps[:]))
                order.settle()
                nc.scalar.activation(LOGF, LOGF, ACT.Exp, scale=-0.5).then_inc(o_rstd.sem, 1)
                act.wait_ge(pooled.sem, pooled.nth(l, 1))
                for ft in range(2):
                    order.put(nc.scalar.activation(PU[:, ft, :], ps[:, 0, ft * TOK:(ft + 1) * TOK], ACT.Identity,
                                                   scale=pool_scale(ft)))
                order.settle()
                nc.scalar.activation(yh[:, 6:8, :], PU, ACT.Copy).then_inc(pool_full.sem, 1)
                act.wait_ge(rec_full.sem, rec_full.nth(l, 1))
                nc.scalar.activation(yh[:, 2:6, :], Q.rearrange("p (k n) -> p k n", n=TOK), ACT.Copy)\
                    .then_inc(rec_hi.sem, 1)
                for c in range(A_WOUT, A_CQ):
                    high(l, c + 2)

            def cross_attention(l):
                for n in range(4):
                    high(l, A_CQ + n + 2)
                    chunk_wait(act, l, A_CQ + n)
                    nc.scalar.activation(CQT[:, 2 * n:2 * n + 2, :], ps[:, n, :].rearrange("p (k n) -> p k n", k=2),
                                         ACT.Copy).then_inc(evacuated.sem, 1)
                high(l, A_CV + 2)
                act.wait_ge(residual_ready.sem, residual_ready.nth(l, 2))
                for t in range(TT):
                    act.wait_ge(max_ready.sem, max_ready.nth(l, t + 1))
                    for h in range(CA_HEADS):
                        g = t * CA_HEADS + h
                        last = nc.scalar.activation(PROB[:, g, :], ps[:, 4 + g // 2, (g % 2) * 256:(g % 2 + 1) * 256],
                                                    ACT.Exp, scale=CA_SCALE, bias=nmx[:, g:g + 1],
                                                    accum_out=rsum[:, g:g + 1])
                    last.then_inc(prob_ready.sem, 1)
                for n in range(4):
                    if n:
                        high(l, A_CV + n + 2)
                    chunk_wait(act, l, A_CV + n)
                    nc.scalar.activation(CVM[:, :, n * 256:(n + 1) * 256], ps[:, n, :].rearrange("p (t n) -> p t n", t=2),
                                         ACT.Copy).then_inc(evacuated.sem, 1)
                for b in range(2):
                    act.wait_ge(prob_turned.sem, prob_turned.nth(l, b + 1))
                    nc.scalar.activation(PROBT[:, 2 * b:2 * b + 2, :], ps[:, 4 + b, :].rearrange("p (g n) -> p g n", g=2),
                                         ACT.Copy).then_inc(probt_act.sem, 1)
                for b in range(4):
                    act.wait_ge(attn_ready.sem, attn_ready.nth(l, b + 1))
                    nc.scalar.activation(yh[:, 2 * b:2 * b + 2, :], ps[:, b, :].rearrange("p (k n) -> p k n", k=2),
                                         ACT.Copy).then_inc(attn_hi.sem, 1)
                for n in range(4):
                    high(l, A_CO + n + 2)

            act.wait_ge(bounds_max.sem, 1)
            nc.scalar.activation(lbw[:, 3:5, :], lbw[:, 1:3, :], ACT.Exp).then_inc(bounds_exp.sem, 1)
            widen(0, -8, None)
            act.wait_ge(x_ready.sem, 4)
            widen(0, -4, None)
            with act.Fori(0, DEPTH) as l:
                order.layer(l)
                high(l, 0)
                high(l, 1)
                ffn(l, A_FFN1, 0)
                widen(l, 0, 0)
                mixer(l)
                widen(l, 4, 1)
                cross_attention(l)
                widen(l, 8, 2)
                ffn(l, A_FFN2, 1)
                widen(l, 12, 3)

            order.next_decoder(act_order_b)

            def squares(l, j):
                for t in range(TT):
                    act.wait_ge(b_res_ready.sem, b_res_ready.nth(l, 0 if j == 0 else t + 1))
                    if t:
                        order.settle()
                    order.put(nc.scalar.activation(junk, res[:, t, :], ACT.Square, accum_out=mv[:, t, 0:1]))
                    order.settle()
                    nc.scalar.activation(mv[:, t, 1:2], mv[:, t, 0:1], ACT.Copy).then_inc(b_squares.sem, 1)

            def rms_widen(l, j):
                for b in range(4):
                    act.wait_ge(b_turned.sem, b_turned.nth(l, 4 * j + b + 1))
                    for k in (2 * b, 2 * b + 1):
                        last = nc.scalar.activation(xf2[:, k, :], ps[:, b, (k % 2) * TOK:(k % 2 + 1) * TOK], ACT.Identity,
                                                    scale=parb[:, 8 * j + k:8 * j + k + 1])
                    last.then_inc(b_x_full.sem, 1)

            def qk_rstd(l, r):
                z0, z1, bank, _, _ = ROUNDS[r]
                out = RZ[:, z0 * TOK:z1 * TOK]
                act.wait_ge(b_summed.sem, b_summed.nth(l, r + 1))
                src = ps[:, bank:bank + 2, :].rearrange("p b n -> p (b n)")[:, 0:(z1 - z0) * TOK]
                order.put(nc.scalar.activation(out, src, ACT.Ln, bias=eps[:]))
                order.settle()
                nc.scalar.activation(out, out, ACT.Exp, scale=-0.5).then_inc(b_qk_rstd.sem, 1)

            def exponentials(l, g):
                scale = (32 if g < 2 else 64) ** -0.5
                act.wait_ge(b_max.sem, b_max.nth(l, g + 1))
                if g >= 2:
                    act.wait_ge(b_prob_turned.sem, b_prob_turned.nth(l, g - 1))
                for j in range(4):
                    nc.scalar.activation(PR[g % 2][:, j * P:(j + 1) * P], ps[:, 2, j * P:(j + 1) * P], ACT.Exp, scale=scale,
                                         bias=nmx[:, j:j + 1], accum_out=rsum[:, j:j + 1])
                for j in range(4):
                    last = nc.scalar.activation(PR[g % 2][:, 512 + j * 256:768 + j * 256],
                                                ps[:, 3 + j // 2, (j % 2) * 256:(j % 2 + 1) * 256], ACT.Exp, scale=scale,
                                                bias=nmx[:, 4 + j:5 + j], accum_out=rsum[:, 4 + j:5 + j])
                if g >= 3:
                    last = nc.scalar.activation(sinkx[:], sinkx[:], ACT.Exp)
                last.then_inc(b_prob.sem, 1)

            def attention(l):
                for c in range(B_GATE + 12):
                    high(l, c + 2, 0, B)
                    chunk_wait(act, l, c, 0, B)
                    bank = ps[:, c % 2, :]
                    if c == B_VA or c == B_VC:
                        nc.scalar.activation(VA if c == B_VA else VC, bank.rearrange("p (t n) -> p t n", t=TT), ACT.Copy)\
                            .then_inc(b_evacuated.sem, 1)
                    elif c >= B_GATE:
                        nc.scalar.activation(GATE[:, c - B_GATE, :], bank, ACT.Copy).then_inc(b_evacuated.sem, 1)
                    else:
                        w = TOK if c == B_KVB else 512
                        cols = slice(c * 512, c * 512 + w)
                        nc.scalar.activation(Z[:, cols], bank[:, 0:w], ACT.Copy)
                        if c == B_KVB:
                            nc.scalar.activation(VB, bank[:, TOK:].rearrange("p (t n) -> p t n", t=TT), ACT.Copy)
                        nc.scalar.activation(RZ[:, cols], bank[:, 0:w], ACT.Square).then_inc(b_evacuated.sem, 1)
                    if c == 1:
                        act.wait_ge(b_lam_sums.sem, b_lam_sums.nth(l, 1))
                        nc.scalar.activation(lams[:, 2:4], lams[:, 0:2], ACT.Exp).then_inc(b_lam_exp.sem, 1)
                    if c in (3, 5, 7, 9):
                        qk_rstd(l, (c - 3) // 2)
                    g = c - (B_GATE + 3)
                    if 2 <= g < GROUPS + 2:
                        act.wait_ge(b_pv.sem, b_pv.nth(l, g - 1))
                        if g - 2 < 2:
                            nc.scalar.activation(OC[:, (g - 2) * TOK:(g - 1) * TOK], ps[:, 5, 0:TOK], ACT.Copy).then_inc(b_o_out.sem, 1)
                        else:
                            if g - 2 > 2:
                                act.wait_ge(b_y_ready.sem, b_y_ready.nth(l, g - 4))
                            nc.scalar.activation(OB[:], ps[:, 5, :], ACT.Copy).then_inc(b_o_out.sem, 1)
                    if g == 3:
                        act.wait_ge(b_o_out.sem, b_o_out.nth(l, 2))
                        nc.scalar.activation(CSQ, OC, ACT.Square).then_inc(b_c_squared.sem, 1)
                    if 1 <= g < GROUPS + 1:
                        act.wait_ge(b_prob_turned.sem, b_prob_turned.nth(l, g))
                        if g >= 2:
                            act.wait_ge(b_pv.sem, b_pv.nth(l, g - 1))
                        n = 512 if g - 1 < 2 else 1024
                        nc.scalar.activation(PT[:, 0:n], ps[:, 5:7, :].rearrange("p b n -> p (b n)")[:, 0:n], ACT.Copy)\
                            .then_inc(b_pt_act.sem, 1)
                    if 0 <= g < GROUPS:
                        exponentials(l, g)
                    if g == GROUPS + 1:
                        act.wait_ge(b_c_summed.sem, b_c_summed.nth(l, 1))
                        order.put(nc.scalar.activation(CRS, ps[:, 2, :], ACT.Ln, bias=eps[:]))
                        order.settle()
                        nc.scalar.activation(CRS, CRS, ACT.Exp, scale=-0.5).then_inc(b_c_rstd.sem, 1)
                act.wait_ge(b_evacuated.sem, b_evacuated.nth(l, 21))
                for n in (2, 0, 1):
                    gates = flat[:, n * 2048:(n + 1) * 2048]
                    nc.scalar.activation(gates, gates, ACT.Sigmoid).then_inc(b_gates_open.sem, 1)
                for c in range(B_WC, B_FFN):
                    high(l, c + 2, 0, B)

            def conv_ffn(l):
                def step(i, more):
                    b, c = i % 2, B_FFN + 2 + 3 * (i - 1)
                    if i == 0:
                        c = B_FFN
                    n = i + more
                    if i >= 2:
                        act.wait_ge(b_hidden_split.sem, b_hidden_split.nth(l, n - 1))
                    chunk_wait(act, l, c, more, B)
                    high(l, c + 2, more, B)
                    for ft in range(2):
                        tile = 2 * n + ft
                        last = nc.scalar.activation(cvg[:, b, ft * TOK:(ft + 1) * TOK], ps[:, 2 * b, ft * TOK:(ft + 1) * TOK],
                                                    ACT.Identity, scale=conv_w2(2, tile), bias=conv_b2(tile))
                    last.then_inc(b_gate_scaled.sem, 1)
                    chunk_wait(act, l, c + 1, more, B)
                    high(l, c + 3, more, B)
                    for ft in range(2):
                        tile = 2 * n + 22 + ft
                        last = nc.scalar.activation(cvv[:, b, ft * TOK:(ft + 1) * TOK], ps[:, 2 * b + 1, ft * TOK:(ft + 1) * TOK],
                                                    ACT.Identity, scale=conv_w2(2, tile), bias=conv_b2(tile))
                    last.then_inc(b_value_scaled.sem, 1)
                    act.wait_ge(b_gate_conv.sem, b_gate_conv.nth(l, n + 1))
                    nc.scalar.activation(cvg[:, b, :], cvg[:, b, :], ACT.Silu).then_inc(gate_ready.sem, 1)
                    if i:
                        high(l, c + 4, more, B)
                    act.wait_ge(b_hidden_ready.sem, b_hidden_ready.nth(l, n + 1))
                    nc.scalar.activation(yh[:, 2 * b:2 * b + 2, :], cvv[:, b, :].rearrange("p (k n) -> p k n", k=2),
                                         ACT.Copy).then_inc(hidden_hi.sem, 1)

                for i in range(3):
                    step(i, 0)
                with act.Fori(0, (STEPS - 5) // 2) as r:
                    for i in (3, 4):
                        step(i, 2 * r)
                for i in (STEPS - 2, STEPS - 1):
                    step(i, 0)

            act.wait_ge(b_res_ready.sem, 1)
            with act.Fori(0, DEPTH) as l:
                order.layer(l)
                high(l, 0, 0, B)
                high(l, 1, 0, B)
                squares(l, 0)
                act.wait_ge(b_params_in.sem, b_params_in.nth(l, 32))
                rms_widen(l, 0)
                attention(l)
                squares(l, 1)
                rms_widen(l, 1)
                conv_ffn(l)
            order.close()

        @block.vector
        def _(dve):
            order = Order(dve, dve_order)

            def hold():
                order.settle()
                order.put(nc.vector.tensor_copy(held[:, 0:1], eps[:]))

            def low(l, c, more=0, ring=A):
                if isinstance(more, int) and c + 3 * more >= ring.chunks:
                    return
                s, u = chunk(c, more)
                dve.wait_ge(ring.hi[s].sem, ring.hi[s].nth(l, u + 1))
                nc.vector.tensor_tensor(wlo[:, s, :], raw[:, s, :], whi[:, s, :].bitcast(F32), ALU.subtract)\
                    .then_inc(split_ready[s].sem, 1)

            def ffn(l, c0, f):
                def step(i, more):
                    b, c = i % 2, c0 + 2 + 3 * (i - 1)
                    if i == 0:
                        c = c0
                    n = f * STEPS + i + more
                    low(l, c + 2, more)
                    low(l, c + 3, more)
                    dve.wait_ge(gate_ready.sem, gate_ready.nth(l, n + 1))
                    chunk_wait(dve, l, c + 1, more)
                    nc.vector.scalar_tensor_tensor(hg[:, b, :], sg[:, b, :], 0.5, ps[:, 2 * b + 1, :], ALU.mult, ALU.mult)\
                        .then_inc(hidden_ready.sem, 1)
                    if i:
                        low(l, c + 4, more)
                    dve.wait_ge(hidden_hi.sem, hidden_hi.nth(l, n + 1))
                    nc.vector.tensor_tensor(yl[:, 2 * b:2 * b + 2, :], hg[:, b, :].rearrange("p (k n) -> p k n", k=2),
                                            yh[:, 2 * b:2 * b + 2, :].bitcast(F32), ALU.subtract)\
                        .then_inc(hidden_split.sem, 1)

                for i in range(3):
                    step(i, 0)
                with dve.Fori(0, (STEPS - 5) // 2) as r:
                    for i in (3, 4):
                        step(i, 2 * r)
                for i in (STEPS - 2, STEPS - 1):
                    step(i, 0)
                low(l, c0 + 3 * STEPS - 1 + 2)

            def split_stream(l, n, hi, lo):
                for b in range(4):
                    tiles = slice(2 * b, 2 * b + 2)
                    dve.wait_ge(x_full.sem, x_full.nth(l, n + b + 1))
                    order.put(nc.vector.tensor_copy(hi[:, tiles, :], xf[:, tiles, :]))
                    order.settle()
                    nc.vector.tensor_tensor(lo[:, tiles, :], xf[:, tiles, :], hi[:, tiles, :].bitcast(F32), ALU.subtract)\
                        .then_inc(x_ready.sem, 1)

            def norm(l, j, c):
                if j == 0:
                    dve.wait_ge(params_in.sem, params_in.nth(l, 48))
                dve.wait_ge(residual_ready.sem, residual_ready.nth(l, j))
                chunk_wait(dve, l, c)
                for t in range(TT):
                    order.put(nc.vector.scalar_tensor_tensor(
                        ybuf[:, t, :], res[:, t, :], ALPHA, ps[:, 4 + 2 * t:6 + 2 * t, :].rearrange("p b n -> p (b n)"),
                        ALU.mult, ALU.add))
                for t in range(TT):
                    order.settle()
                    for half in range(2):
                        order.put(nc.vector.bn_stats(stat[:, t, half, :], ybuf[:, t, half * 512:(half + 1) * 512]))
                    hold()
                    order.put(nc.vector.bn_aggr(mv[:, t, :], stat[:, t, :, :].rearrange("p a b -> p (a b)")))
                    order.settle()
                    nc.vector.tensor_scalar_add(vare[:, t:t + 1], mv[:, t, 1:2], LN_EPS).then_inc(var_ready.sem, 1)
                for t in range(TT):
                    dve.wait_ge(rstd_ready.sem, rstd_ready.nth(l, 2 * j + t + 1))
                    nc.vector.tensor_scalar(ybuf[:, t, :], ybuf[:, t, :], mv[:, t, 0:1], rstd[:, t:t + 1],
                                            ALU.subtract, ALU.mult).then_inc(normed.sem, 1)
                split_stream(l, 4 * j, xh, xl)

            def mixer(l):
                def spread(buf, side, h):
                    return buf.rearrange("p (n s h) -> p n s h", s=2, h=h)[:, :, side, :]

                def decayed(n):
                    if n == 1:
                        dve.wait_ge(residual_ready.sem, residual_ready.nth(l, 1))
                        dve.wait_ge(evacuated.sem, evacuated.nth(l, 4))
                    if n >= 2:
                        dve.wait_ge(level_scored.sem, level_scored.nth(l, n - 1))
                    dve.wait_ge(decay_exp.sem, decay_exp.nth(l, n))
                    h = P if n == 1 else LEVELS[::-1][n - 2]
                    order.put(nc.vector.tensor_tensor(spread(qlev[n % 2], 1, h), spread(Q, 1, h), spread(EXPD, 1, h), ALU.mult))
                    order.settle()
                    nc.vector.tensor_tensor(spread(klev[n % 2], 0, h), spread(KEY, 0, h), spread(EXPD, 0, h), ALU.mult)\
                        .then_inc(level_ready.sem, 1)

                def merge(n):
                    dve.wait_ge(level_scored.sem, level_scored.nth(l, n + 1))
                    m = 0 if n == 0 else 9 - n
                    b = 4 + 2 * (n % 2)
                    if n:
                        dve.wait_ge(level_merged.sem, level_merged.nth(l, n - 1))
                    hold()
                    nc.vector.copy_predicated(
                        AT, lvl_mask[:, m:m + 1, :].broadcast_to([P, HEADS * TT, P]),
                        ps[:, b:b + 2, :].rearrange("p b (g t) -> p (b g) t", t=P)).then_inc(level_merged.sem, 1)

                for c in range(A_RF, A_WOUT):
                    low(l, c + 2)
                    if c == A_RF + 1:
                        dve.wait_ge(evacuated.sem, evacuated.nth(l, 2))
                        order.put(nc.vector.tensor_scalar_max(SIG, SIG, F_FLOOR))
                        order.settle()
                        order.put(nc.vector.tensor_copy(lbc[:], lbt[:, bass.ds(l, 1), :, :].rearrange("p l a h -> p (l a) h")))
                        order.settle()
                        for h in range(HEADS):
                            s = slice(h * TOK, (h + 1) * TOK)
                            last = nc.vector.tensor_scalar(KEY[:, s], SIG[:, s], lbc[:, 2, h:h + 1], lbc[:, 1, h:h + 1],
                                                           ALU.mult, ALU.add)
                            if h == 0:
                                last.then_inc(floored.sem, 1)
                        last.then_inc(keys_ready.sem, 1)
                    if c == A_RQ:
                        dve.wait_ge(logs_ready.sem, logs_ready.nth(l, 1))
                        dve.wait_ge(keys_ready.sem, keys_ready.nth(l, 1))
                        for g in range(HEADS * TT):
                            s = slice(g * P, (g + 1) * P)
                            last = nc.vector.tensor_tensor_scan(SIG[:, s], ones, LOGF[:, s], 0.0, ALU.mult, ALU.add)
                        last.then_inc(decay_ready.sem, 1)
                    if A_RI <= c < A_RI + 8:
                        decayed(c - A_RI + 1)
                    if c == A_RI + 1:
                        merge(0)
                    if A_RI + 3 <= c < A_RI + 10:
                        merge(c - A_RI - 1)
                    if c == A_CB:
                        dve.wait_ge(gate_exp.sem, gate_exp.nth(l, 1))
                        order.put(nc.vector.tensor_scalar_add(RG, RG, 1.0))
                        order.settle()
                        order.put(nc.vector.reciprocal(RG, RG))
                dve.wait_ge(o_rstd.sem, o_rstd.nth(l, 1))
                order.settle()
                for h in range(HEADS):
                    s = slice(h * TOK, (h + 1) * TOK)
                    order.put(nc.vector.scalar_tensor_tensor(Q[:, s], ps[:, 4 + h // 2, (h % 2) * TOK:(h % 2 + 1) * TOK],
                                                             norm_g(h), LOGF[:, s], ALU.mult, ALU.mult))
                order.settle()
                nc.vector.tensor_tensor(Q, Q, RG, ALU.mult).then_inc(rec_full.sem, 1)
                dve.wait_ge(pool_full.sem, pool_full.nth(l, 1))
                nc.vector.tensor_tensor(yl[:, 6:8, :], PU, yh[:, 6:8, :].bitcast(F32), ALU.subtract).then_inc(pool_ready.sem, 1)
                dve.wait_ge(rec_hi.sem, rec_hi.nth(l, 1))
                nc.vector.tensor_tensor(yl[:, 2:6, :], Q.rearrange("p (k n) -> p k n", n=TOK), yh[:, 2:6, :].bitcast(F32),
                                        ALU.subtract).then_inc(rec_ready.sem, 1)
                for c in range(A_WOUT, A_CQ):
                    low(l, c + 2)

            def cross_attention(l):
                for n in range(4):
                    low(l, A_CQ + n + 2)
                low(l, A_CV + 2)
                for t in range(TT):
                    g = slice(t * CA_HEADS, (t + 1) * CA_HEADS)
                    dve.wait_ge(scored.sem, scored.nth(l, t + 1))
                    order.put(nc.vector.tensor_reduce(
                        mx[:, g], ps[:, 4 + 2 * t:6 + 2 * t, :].rearrange("p b (h n) -> p (b h) n", n=256), AX.X, ALU.max))
                    order.settle()
                    nc.vector.tensor_scalar_mul(nmx[:, g], mx[:, g], -CA_SCALE).then_inc(max_ready.sem, 1)
                for t in range(TT):
                    g = slice(t * CA_HEADS, (t + 1) * CA_HEADS)
                    dve.wait_ge(prob_ready.sem, prob_ready.nth(l, t + 1))
                    order.put(nc.vector.reciprocal(rinv[:, g], rsum[:, g]))
                    order.settle()
                    nc.vector.tensor_tensor(PROB[:, g, :], PROB[:, g, :], rinv[:, g].unsqueeze(2).broadcast_to([P, CA_HEADS, 256]),
                                            ALU.mult).then_inc(prob_normed.sem, 1)
                for n in range(1, 4):
                    low(l, A_CV + n + 2)
                for b in range(2, 4):
                    dve.wait_ge(prob_turned.sem, prob_turned.nth(l, b + 1))
                    nc.vector.tensor_copy(PROBT[:, 2 * b:2 * b + 2, :], ps[:, 4 + b, :].rearrange("p (g n) -> p g n", g=2))\
                        .then_inc(probt_dve.sem, 1)
                for b in range(4):
                    dve.wait_ge(attn_hi.sem, attn_hi.nth(l, b + 1))
                    nc.vector.tensor_tensor(yl[:, 2 * b:2 * b + 2, :], ps[:, b, :].rearrange("p (k n) -> p k n", k=2),
                                            yh[:, 2 * b:2 * b + 2, :].bitcast(F32), ALU.subtract).then_inc(attn_split.sem, 1)
                for n in range(4):
                    low(l, A_CO + n + 2)

            def bounds():
                m, e = lbw[:, 0, :], lbw[:, 3:5, :]
                order.put(nc.vector.tensor_tensor(m, rlb[:, 0, :], rlb[:, 1, :], ALU.max))
                order.settle()
                order.put(nc.vector.tensor_tensor(lbw[:, 1, :], rlb[:, 0, :], m, ALU.subtract))
                nc.vector.tensor_tensor(lbw[:, 2, :], rlb[:, 1, :], m, ALU.subtract).then_inc(bounds_max.sem, 1)
                order.settle()
                dve.wait_ge(bounds_exp.sem, 1)
                order.put(nc.vector.tensor_tensor(m, lbw[:, 3, :], lbw[:, 4, :], ALU.add))
                order.settle()
                order.put(nc.vector.reciprocal(lbw[:, 5, :], m))
                order.settle()
                for i in range(2):
                    order.put(nc.vector.tensor_tensor(lbw[:, 1 + i, :], lbw[:, 3 + i, :], lbw[:, 5, :], ALU.mult))
                order.settle()
                order.put(nc.vector.tensor_tensor(lbw[:, 3, :], lbw[:, 1, :], lbw[:, 2, :], ALU.add))
                order.put(nc.vector.tensor_tensor(lbt[:, 0, 0, :], lbw[:, 1, :], lbw[:, 1, :], ALU.subtract))
                order.settle()
                order.put(nc.vector.tensor_tensor(lbt[:, 1, 0, :], lbw[:, 3, :], lbw[:, 1, :], ALU.subtract))
                order.settle()
                order.put(nc.vector.tensor_scalar(lbt[:, :, 1, :], lbt[:, :, 0, :], -1.0, 1.0, ALU.mult, ALU.add))
                order.put(nc.vector.tensor_scalar_add(lbt[:, :, 2, :], lbt[:, :, 0, :], -1.0))
                order.settle()

            for s in range(SLOTS):
                dve.sem_inc(split_ready[s].sem, 1)
            order.put(nc.vector.memset(eps[:], RMS_EPS))
            dve.wait_ge(inputs_in.sem, 64)
            order.put(nc.vector.tensor_copy(lvl_mask[:], units(11).rearrange("p (v t) -> p v t", t=P)))
            bounds()
            split_stream(0, -8, xh, xl)
            split_stream(0, -4, mh, ml)
            dve.wait_ge(mem_in.sem, 16)
            dve.wait_ge(turned.sem, 8)
            order.put(nc.vector.memset(AT, 0.0))
            order.settle()
            order.close()
            with dve.Fori(0, DEPTH) as l:
                order.layer(l)
                low(l, 0)
                low(l, 1)
                ffn(l, A_FFN1, 0)
                norm(l, 0, A_FFN1 + 3 * STEPS - 1)
                mixer(l)
                norm(l, 1, A_CQ - 1)
                cross_attention(l)
                norm(l, 2, A_FFN2 - 1)
                ffn(l, A_FFN2, 1)
                norm(l, 3, A_CHUNKS - 1)

            order.next_decoder(dve_order_b)

            def add_to_stream(l, c):
                chunk_wait(dve, l, c, 0, B)
                for t in range(TT):
                    nc.vector.tensor_tensor(res[:, t, :], res[:, t, :], ps[:, 4 + 2 * t:6 + 2 * t, :].rearrange("p b n -> p (b n)"),
                                            ALU.add).then_inc(b_res_ready.sem, 1)

            def rms(l, j):
                for t in range(TT):
                    dve.wait_ge(b_squares.sem, b_squares.nth(l, 2 * j + t + 1))
                    nc.vector.tensor_scalar(vare[:, t:t + 1], mv[:, t, 1:2], 1.0 / D, QK_EPS, ALU.mult, ALU.add)\
                        .then_inc(var_ready.sem, 1)
                for t in range(TT):
                    dve.wait_ge(b_rstd_ready.sem, b_rstd_ready.nth(l, 2 * j + t + 1))
                    nc.vector.tensor_scalar(nbuf[:, t, :], res[:, t, :], rstd[:, t:t + 1], None, ALU.mult)\
                        .then_inc(normed.sem, 1)
                for b in range(4):
                    tiles = slice(2 * b, 2 * b + 2)
                    dve.wait_ge(b_x_full.sem, b_x_full.nth(l, 4 * j + b + 1))
                    order.put(nc.vector.tensor_copy(xh[:, tiles, :], xf2[:, tiles, :]))
                    order.settle()
                    nc.vector.tensor_tensor(xl[:, tiles, :], xf2[:, tiles, :], xh[:, tiles, :].bitcast(F32), ALU.subtract)\
                        .then_inc(x_ready.sem, 1)

            def lambdas(l):
                v = rowb[:, 0:128].rearrange("p (a b n) -> p a b n", a=2, b=2)
                order.put(nc.vector.tensor_tensor(lamw[:], v[:, :, 0, :], v[:, :, 1, :], ALU.mult))
                order.settle()
                nc.vector.tensor_reduce(lams[:, 0:2], lamw[:], AX.X, ALU.add).then_inc(b_lam_sums.sem, 1)
                order.put(nc.vector.tensor_tensor(subg[:], parb[:, 22:23], parb[:, 24:25], ALU.mult))
                dve.wait_ge(b_lam_exp.sem, b_lam_exp.nth(l, 1))
                order.put(nc.vector.tensor_tensor(nlam[:], lams[:, 3:4], lams[:, 2:3], ALU.subtract))
                order.settle()
                order.put(nc.vector.tensor_tensor(nlam[:], nlam[:], parb[:, 23:24], ALU.subtract))

            def qk_norm(l, r):
                z0, z1, bank, _, gains = ROUNDS[r]
                dve.wait_ge(b_qk_rstd.sem, b_qk_rstd.nth(l, r + 1))
                for a, b, col in gains:
                    cols = slice(a * TOK, b * TOK)
                    last = nc.vector.scalar_tensor_tensor(Z[:, cols], Z[:, cols], parb[:, col:col + 1], RZ[:, cols],
                                                          ALU.mult, ALU.mult)
                last.then_inc(b_qk_normed.sem, 1)

            def sine(l, r):
                z0, z1, bank, dim, _ = ROUNDS[r]
                n = z1 - z0
                dve.wait_ge(b_rotated.sem, b_rotated.nth(l, r + 1))
                src = ps[:, bank:bank + 2, :].rearrange("p b n -> p (b n)")[:, 0:n * TOK].rearrange("p (z t) -> p z t", t=TOK)
                out = RZ[:, z0 * TOK:z1 * TOK].rearrange("p (z t) -> p z t", t=TOK)
                nc.vector.tensor_tensor(out, src, rope[dim][1].unsqueeze(1).broadcast_to([P, n, TOK]), ALU.mult)\
                    .then_inc(b_sine.sem, 1)

            def maxima(l, g):
                scale = (32 if g < 2 else 64) ** -0.5
                dve.wait_ge(b_scored.sem, b_scored.nth(l, g + 1))
                order.put(nc.vector.tensor_reduce(mx[:, 0:4], ps[:, 2, :].rearrange("p (j n) -> p j n", n=P), AX.X, ALU.max))
                order.put(nc.vector.tensor_reduce(mx[:, 4:8], ps[:, 3:5, :].rearrange("p b (j n) -> p (b j) n", n=256), AX.X, ALU.max))
                order.settle()
                if g < 3:
                    nc.vector.tensor_scalar_mul(nmx[:], mx[:], -scale).then_inc(b_max.sem, 1)
                    return
                sink = rowb[:, 128 + 4 * (g - 3):132 + 4 * (g - 3)]
                for t in range(TT):
                    order.put(nc.vector.scalar_tensor_tensor(mx[:, 4 * t:4 * t + 4], mx[:, 4 * t:4 * t + 4], scale, sink,
                                                             ALU.mult, ALU.max))
                order.settle()
                order.put(nc.vector.tensor_scalar_mul(nmx[:], mx[:], -1.0))
                order.settle()
                for t in range(TT):
                    last = nc.vector.tensor_tensor(sinkx[:, 4 * t:4 * t + 4], nmx[:, 4 * t:4 * t + 4], sink, ALU.add)
                    if t == 0:
                        order.put(last)
                last.then_inc(b_max.sem, 1)

            def normalise(l, g):
                dve.wait_ge(b_prob.sem, b_prob.nth(l, g + 1))
                if g >= 3:
                    order.put(nc.vector.tensor_tensor(rsum[:], rsum[:], sinkx[:], ALU.add))
                    order.settle()
                order.put(nc.vector.reciprocal(rinv[:], rsum[:]))
                order.settle()
                first = PR[g % 2][:, 0:512].rearrange("p (j n) -> p j n", n=P)
                second = PR[g % 2][:, 512:1536].rearrange("p (j n) -> p j n", n=256)
                if g >= 2:
                    nc.vector.tensor_tensor(first, first, rinv[:, 0:4].unsqueeze(2).broadcast_to([P, 4, P]), ALU.mult)
                    nc.vector.tensor_tensor(second, second, rinv[:, 4:8].unsqueeze(2).broadcast_to([P, 4, 256]), ALU.mult)\
                        .then_inc(b_prob_normed.sem, 1)
                    return
                order.put(nc.vector.tensor_scalar(rlam[:], rinv[:], nlam[:], None, ALU.mult))
                for t, part in enumerate((first, second)):
                    for h in range(2):
                        order.put(nc.vector.tensor_scalar(part[:, 2 * h, :], part[:, 2 * h, :],
                                                          rinv[:, 4 * t + 2 * h:4 * t + 2 * h + 1], None, ALU.mult))
                order.settle()
                for t, part in enumerate((first, second)):
                    for h in range(2):
                        j = 4 * t + 2 * h + 1
                        last = nc.vector.scalar_tensor_tensor(part[:, 2 * h, :], part[:, 2 * h + 1, :], rlam[:, j:j + 1],
                                                              part[:, 2 * h, :], ALU.mult, ALU.add)
                last.then_inc(b_prob_normed.sem, 1)

            def split_y(src, y0, done):
                order.put(nc.vector.tensor_copy(yh[:, y0:y0 + 2, :], src.rearrange("p (k n) -> p k n", n=TOK)))
                order.settle()
                nc.vector.tensor_tensor(yl[:, y0:y0 + 2, :], src.rearrange("p (k n) -> p k n", n=TOK),
                                        yh[:, y0:y0 + 2, :].bitcast(F32), ALU.subtract).then_inc(done.sem, 1)

            def attention(l):
                for c in range(B_GATE + 12):
                    low(l, c + 2, 0, B)
                    if c == 1:
                        lambdas(l)
                    if c in (4, 6, 8, 10):
                        qk_norm(l, c // 2 - 2)
                    if c in (5, 7, 9, 11):
                        sine(l, (c - 5) // 2)
                    g = c - (B_GATE + 3)
                    if 0 <= g < GROUPS:
                        maxima(l, g)
                    if 4 <= g < GROUPS + 2:
                        dve.wait_ge(b_o_out.sem, b_o_out.nth(l, g - 1))
                        split_y(OB[:], 2 * (g - 4), b_y_ready)
                    if 1 <= g < GROUPS + 1:
                        dve.wait_ge(b_prob_turned.sem, b_prob_turned.nth(l, g))
                        if g >= 2:
                            dve.wait_ge(b_pv.sem, b_pv.nth(l, g - 1))
                        n = 256 if g - 1 < 2 else 512
                        nc.vector.tensor_copy(PT[:, 1024:1024 + n], ps[:, 7, 0:n]).then_inc(b_pt_dve.sem, 1)
                    if 0 <= g < GROUPS:
                        normalise(l, g)
                    if g == GROUPS + 1:
                        dve.wait_ge(b_c_rstd.sem, b_c_rstd.nth(l, 1))
                        order.put(nc.vector.scalar_tensor_tensor(OC, OC, subg[:], CRS, ALU.mult, ALU.mult))
                        order.settle()
                        split_y(OC, 6, b_yc_ready)
                for n, (chunks, gate0, bank0) in enumerate((([B_WC], 8, 0), ([B_WA], 0, 4), ([B_WB, B_WB + 1], 4, 0))):
                    for c in chunks:
                        low(l, c + 2, 0, B)
                    dve.wait_ge(b_gates_open.sem, b_gates_open.nth(l, n + 1))
                    for b in range(4):
                        dve.wait_ge(b_branch_done.sem, b_branch_done.nth(l, 4 * n + b + 1))
                        nc.vector.tensor_tensor(GATE[:, gate0 + b, :], GATE[:, gate0 + b, :], ps[:, bank0 + b, :], ALU.mult)\
                            .then_inc(b_gated.sem, 1)
                        if n < 2:
                            continue
                        dve.wait_ge(b_gated.sem, b_gated.nth(l, 8 + b + 1))
                        dve.wait_ge(b_pair_merged.sem, b_pair_merged.nth(l, b + 1))
                        order.put(nc.vector.tensor_tensor(GATE[:, 8 + b, :], GATE[:, 8 + b, :], GATE[:, 4 + b, :], ALU.add))
                        order.settle()
                        m = GATE[:, 8 + b, :].rearrange("p (k n) -> p k n", n=TOK)
                        tiles = slice(2 * b, 2 * b + 2)
                        order.put(nc.vector.tensor_copy(xh[:, tiles, :], m))
                        order.settle()
                        nc.vector.tensor_tensor(xl[:, tiles, :], m, xh[:, tiles, :].bitcast(F32), ALU.subtract)\
                            .then_inc(b_merge_ready.sem, 1)
                for c in range(B_WOUT, B_FFN):
                    low(l, c + 2, 0, B)

            def conv_ffn(l):
                def taps(buf, bank, b, tile, done):
                    for lag in (1, 2):
                        for ft in range(2):
                            t0 = ft * TOK
                            out = buf[:, b, t0 + lag:t0 + TOK]
                            last = nc.vector.scalar_tensor_tensor(out, ps[:, bank, t0:t0 + TOK - lag], conv_w2(2 - lag, tile + ft), out,
                                                                  ALU.mult, ALU.add)
                            if not (lag == 2 and ft == 1):
                                last.then_inc(done[0].sem, 1)
                        if lag == 1:
                            dve.wait_ge(done[0].sem, done[1])
                    return last

                def step(i, more):
                    b, c = i % 2, B_FFN + 2 + 3 * (i - 1)
                    if i == 0:
                        c = B_FFN
                    n = i + more
                    low(l, c + 2, more, B)
                    dve.wait_ge(b_gate_scaled.sem, b_gate_scaled.nth(l, n + 1))
                    taps(cvg, 2 * b, b, 2 * n, (b_taps, b_taps.nth(l, 6 * n + 2))).then_inc(b_gate_conv.sem, 1)
                    low(l, c + 3, more, B)
                    dve.wait_ge(b_value_scaled.sem, b_value_scaled.nth(l, n + 1))
                    taps(cvv, 2 * b + 1, b, 2 * n + 22, (b_taps, b_taps.nth(l, 6 * n + 5))).then_inc(b_value_conv.sem, 1)
                    dve.wait_ge(gate_ready.sem, b_gate_ready.nth(l, n + 1))
                    dve.wait_ge(b_value_conv.sem, b_value_conv.nth(l, n + 1))
                    dve.wait_ge(b_taps.sem, b_taps.nth(l, 6 * n + 6))
                    nc.vector.tensor_tensor(cvv[:, b, :], cvv[:, b, :], cvg[:, b, :], ALU.mult).then_inc(hidden_ready.sem, 1)
                    if i:
                        low(l, c + 4, more, B)
                    dve.wait_ge(b_hidden_hi.sem, b_hidden_hi.nth(l, n + 1))
                    nc.vector.tensor_tensor(yl[:, 2 * b:2 * b + 2, :], cvv[:, b, :].rearrange("p (k n) -> p k n", k=2),
                                            yh[:, 2 * b:2 * b + 2, :].bitcast(F32), ALU.subtract).then_inc(hidden_split.sem, 1)

                for i in range(3):
                    step(i, 0)
                with dve.Fori(0, (STEPS - 5) // 2) as r:
                    for i in (3, 4):
                        step(i, 2 * r)
                for i in (STEPS - 2, STEPS - 1):
                    step(i, 0)

            dve.wait_ge(b_consts_in.sem, 16)
            nc.vector.tensor_copy(maskb[:, 0, :], ident).then_inc(b_masks_set.sem, 1)
            nc.vector.tensor_copy(maskb[:, 1:3, :], CONB[:, 1536:1792].rearrange("p (a n) -> p a n", a=2)).then_inc(b_masks_set.sem, 1)
            dve.wait_ge(residual_ready.sem, residual_ready.nth(DEPTH, 0))
            dve.wait_ge(x_ready.sem, x_ready.nth(DEPTH, 0))
            dve.sem_inc(b_res_ready.sem, 1)
            with dve.Fori(0, DEPTH) as l:
                order.layer(l)
                low(l, 0, 0, B)
                low(l, 1, 0, B)
                rms(l, 0)
                attention(l)
                add_to_stream(l, B_FFN - 1)
                rms(l, 1)
                conv_ffn(l)
                add_to_stream(l, B_CHUNKS - 1)
            order.close()

        @block.gpsimd
        def _(pool):
            order = Order(pool, pool_order)

            def hold():
                order.settle()
                order.put(nc.gpsimd.tensor_tensor(held[:, 1:2], mhalf[:], mhalf[:], ALU.mult))

            def norm(l, j):
                for t in range(TT):
                    pool.wait_ge(var_ready.sem, var_ready.nth(l, 2 * j + t + 1))
                    nc.gpsimd.tensor_tensor(rstd[:, t:t + 1], vare[:, t:t + 1], mhalf[:], ALU.pow).then_inc(rstd_ready.sem, 1)
                pool.wait_ge(normed.sem, normed.nth(l, 2 * j + 2))
                for tab, name in ((tabg, "ln_g"), (tabb, "ln_b")):
                    pool.dma_start(tab, dram[name][bass.ds(l * 4 + j, 1), :].rearrange("a n -> (a n)").partition_broadcast(P))\
                        .then_inc(tables_in.sem, 16)
                pool.wait_ge(tables_in.sem, tables_in.nth(l, 32 * (j + 1)))
                for t in range(TT):
                    order.put(nc.gpsimd.tensor_tensor(res[:, t, :], ybuf[:, t, :], tabg, ALU.mult))
                order.settle()
                for t in range(TT):
                    last = nc.gpsimd.tensor_tensor(res[:, t, :], res[:, t, :], tabb, ALU.add)
                last.then_inc(residual_ready.sem, 1)

            def spreads(l):
                pool.wait_ge(decay_ready.sem, decay_ready.nth(l, 1))
                for n in range(1, 9):
                    if n >= 2:
                        pool.wait_ge(decay_exp.sem, decay_exp.nth(l, n - 1))
                    if n == 1:
                        d = LOGF.rearrange("p (n s) -> p n s", s=TOK)[:, :, 0:P]
                        b = SIG.rearrange("p (n s) -> p n s", s=TOK)
                        nc.gpsimd.tensor_tensor(d, b[:, :, 0:P], b[:, :, P - 1:P].broadcast_to([P, HEADS, P]), ALU.subtract)\
                            .then_inc(spread_ready.sem, 1)
                        continue
                    h = LEVELS[::-1][n - 2]
                    d = LOGF.rearrange("p (n s) -> p n s", s=2 * h)
                    b = SIG.rearrange("p (n s) -> p n s", s=2 * h)
                    nc.gpsimd.tensor_tensor(d, b, b[:, :, h - 1:h].broadcast_to([P, 1024 // (2 * h), 2 * h]), ALU.subtract)\
                        .then_inc(spread_ready.sem, 1)

            def short_conv(l):
                pool.wait_ge(evacuated.sem, evacuated.nth(l, 11))
                order.put(nc.gpsimd.tensor_tensor(CC, CC, CH, ALU.mult))
                hold()
                for ft in range(2):
                    order.put(nc.gpsimd.tensor_scalar(CH[:, ft, :], CC[:, ft, :], conv_w(2, ft), None, ALU.mult))
                for lag in (1, 2):
                    for ft in range(2):
                        order.put(nc.gpsimd.tensor_scalar(TMP[:, ft, lag:], CC[:, ft, :TOK - lag], conv_w(2 - lag, ft), None,
                                                          ALU.mult))
                    order.settle()
                    order.put(nc.gpsimd.tensor_tensor(CH[:, :, lag:], CH[:, :, lag:], TMP[:, :, lag:], ALU.add))
                    hold()
                order.put(nc.gpsimd.tensor_tensor(CH, CH, CB, ALU.mult))
                hold()
                order.put(nc.gpsimd.tensor_copy(yh[:, 0:2, :], CH))
                order.settle()
                nc.gpsimd.tensor_tensor(yl[:, 0:2, :], CH, yh[:, 0:2, :].bitcast(F32), ALU.subtract).then_inc(conv_ready.sem, 1)

            def windows(l):
                def widen(dst, src, w, f0):
                    order.put(nc.gpsimd.tensor_copy(dst[:, f0:, 0:w], src[:, f0:, 0:w]))
                    order.put(nc.gpsimd.tensor_tensor(dst[:, f0:, w:], src[:, f0:, w:], src[:, f0:, :TOK - w], ALU.add))
                    hold()

                s, t = CC, CH
                pool.wait_ge(conv_ready.sem, conv_ready.nth(l, 1))
                pool.wait_ge(evacuated.sem, evacuated.nth(l, 12))
                hold()
                widen(s, PU, 1, 0)
                widen(t, s, 2, 0)
                widen(s, t, 4, 1)
                widen(t, s, 8, 1)
                order.put(nc.gpsimd.tensor_scalar(s, s, first_half, None, ALU.mult))
                order.put(nc.gpsimd.tensor_scalar(t, t, second_half, None, ALU.mult))
                order.settle()
                order.put(nc.gpsimd.tensor_tensor(s, s, t, ALU.add))
                hold()
                for ft in range(2):
                    order.put(nc.gpsimd.tensor_scalar(TMP[:, ft, 16:], s[:, ft, 16:], invw[:, ft:ft + 1], None, ALU.mult))
                order.put(nc.gpsimd.tensor_tensor(TMP[:, :, 0:16], s[:, :, 0:16], edge, ALU.mult))
                order.settle()
                nc.gpsimd.tensor_tensor(TMP, TMP, PU, ALU.subtract).then_inc(windows_ready.sem, 1)

            order.put(nc.gpsimd.memset(mhalf[:], -0.5))
            order.put(nc.gpsimd.memset(poolw[:], 0.0))
            pool.wait_ge(inputs_in.sem, 64)
            pool.sem_inc(residual_ready.sem, 1)
            order.settle()
            order.close()
            with pool.Fori(0, DEPTH) as l:
                order.layer(l)
                pool.wait_ge(x_ready.sem, x_ready.nth(l, 0))
                pool.dma_start(par[:], dram["par_a"][bass.ds(l, 1), :, :].rearrange("l p n -> (l p) n")).then_inc(params_in.sem, 16)
                for half in range(2):
                    rows = slice(half * 64, (half + 1) * 64)
                    pool.dma_start(poolw[rows, :, rows],
                                   dram["pool_w"][bass.ds(l, 1), half:4:2, :, :].rearrange("l g c d -> c (l g) d"))\
                        .then_inc(params_in.sem, 16)
                norm(l, 0)
                spreads(l)
                short_conv(l)
                windows(l)
                norm(l, 1)
                norm(l, 2)
                norm(l, 3)

            order.close()
            pool.dma_start(CONB, dram["con_b"]).then_inc(b_consts_in.sem, 16)
            with pool.Fori(0, DEPTH) as l:
                pool.wait_ge(b_res_ready.sem, b_res_ready.nth(l, 0))
                pool.dma_start(parb[:], dram["par_b"][bass.ds(l, 1), :, :].rearrange("l p n -> (l p) n")).then_inc(b_params_in.sem, 16)
                pool.dma_start(rowb[:], dram["row_b"][bass.ds(l, 1), :].rearrange("l n -> (l n)").partition_broadcast(P))\
                    .then_inc(b_params_in.sem, 16)
                for j in range(2):
                    for t in range(TT):
                        pool.wait_ge(b_var_ready.sem, b_var_ready.nth(l, 2 * j + t + 1))
                        nc.gpsimd.tensor_tensor(rstd[:, t:t + 1], vare[:, t:t + 1], mhalf[:], ALU.pow).then_inc(rstd_ready.sem, 1)
                    if j:
                        continue
                    for r, (z0, z1, _, dim, _) in enumerate(ROUNDS):
                        z = Z[:, z0 * TOK:z1 * TOK].rearrange("p (z t) -> p z t", t=TOK)
                        pool.wait_ge(b_rotated.sem, b_rotated.nth(l, r + 1))
                        nc.gpsimd.tensor_tensor(z, z, rope[dim][0].unsqueeze(1).broadcast_to([P, z1 - z0, TOK]), ALU.mult)\
                            .then_inc(b_cosine.sem, 1)
                        pool.wait_ge(b_cosine.sem, b_cosine.nth(l, r + 1))
                        pool.wait_ge(b_sine.sem, b_sine.nth(l, r + 1))
                        nc.gpsimd.tensor_tensor(z, z, RZ[:, z0 * TOK:z1 * TOK].rearrange("p (z t) -> p z t", t=TOK), ALU.add)\
                            .then_inc(b_roped.sem, 1)
                    for b in range(4):
                        pool.wait_ge(b_gated.sem, b_gated.nth(l, 4 + b + 1))
                        nc.gpsimd.tensor_tensor(GATE[:, 8 + b, :], GATE[:, 8 + b, :], GATE[:, b, :], ALU.add).then_inc(b_pair_merged.sem, 1)


def kernel(**inputs):
    import numpy as np
    import concourse.bacc as bacc
    from concourse import mybir
    from concourse.bass_utils import run_bass_kernel_spmd

    P = 128
    a = {k: np.asarray(v) for k, v in inputs.items()}

    def columns(w, c0):
        n = w.shape[0]
        return w[:, :, c0:c0 + 256].reshape(n, 8, P, 256).transpose(0, 2, 1, 3).reshape(n, P, 2048)

    def rows(w, r0):
        n = w.shape[0]
        return w[:, r0:r0 + 256, :].reshape(n, 2, P, 1024).transpose(0, 2, 1, 3).reshape(n, P, 2048)

    def stream(chunks):
        out = np.empty((2, len(chunks), P, 2048), np.float32)
        for i, (cut, w, at) in enumerate(chunks):
            out[:, i] = cut(w, at)
        return out.reshape(-1, 2048)

    def ffn(gate, up, down):
        seq = []
        for i in range(11):
            seq += [(columns, *gate(i)), (columns, *up(i))]
            if i:
                seq.append((rows, down, 256 * (i - 1)))
        return seq + [(rows, down, 2560)]

    def plain_ffn(g, u, d):
        return ffn(lambda i: (a[g], 256 * i), lambda i: (a[u], 256 * i), a[d])

    conv, rec = 256, 512
    cb, cc, ch, rq = 0, conv, 2 * conv, 3 * conv
    rf, ri, rg, pu = rq + rec, rq + 2 * rec, rq + 3 * rec, rq + 4 * rec
    seq = plain_ffn("ffn1_gate", "ffn1_up", "ffn1_down")
    seq += [(columns, a["w_in"], c) for c in (rf, rf + 256, rq, rq + 256, ri, ri + 256, rg, rg + 256, cc, ch, cb, pu)]
    seq += [(columns, a["ca_k"], 256 * n) for n in range(4)]
    seq += [(rows, a["w_out"], r) for r in (0, 768, 256, 512)]
    seq += [(columns, a["ca_q"], 256 * n) for n in range(4)]
    seq += [(columns, a["ca_v"], 256 * n) for n in range(4)]
    seq += [(rows, a["ca_o"], 256 * n) for n in range(4)]
    seq += plain_ffn("ffn2_gate", "ffn2_up", "ffn2_down")
    stream_a = stream(seq)

    def features(v):
        return v.reshape(2, -1, P).transpose(0, 2, 1)

    par_a = np.concatenate([features(a[n]) for n in ("ln_g", "ln_b", "conv_w", "rec_norm_g", "pool_scale")], axis=2)
    rec_lb = features(a["rec_lb"]).transpose(1, 0, 2).reshape(P, 8)

    a_w, b_q, b_kv, c_w = 256, 512, 128, 256
    w2 = a["w_in_2"]
    qa, ka, va, qb = 0, a_w, 2 * a_w, 3 * a_w
    kb = qb + b_q
    qc = kb + 2 * b_kv
    kc, vc, gates = qc + c_w, qc + 2 * c_w, qc + 3 * c_w
    paired = np.concatenate([np.arange(64) + 64 * h for i in range(4) for h in (i, i + 4)])
    wqb = w2[:, :, qb:kb][:, :, paired]
    wpb = a["w_pb_2"][:, paired, :]
    up, down = a["w_up_2"], a["w_down_2"]
    seq = [(columns, w2, qc), (columns, w2, kc), (columns, w2, qa), (columns, w2, ka), (columns, wqb, 0), (columns, wqb, 256),
           (columns, w2, kb), (columns, w2, va), (columns, w2, vc)]
    seq += [(columns, w2, gates + 256 * n) for n in range(12)]
    seq += [(rows, a["w_pc_2"], 0), (rows, a["w_pa_2"], 0), (rows, wpb, 0), (rows, wpb, 256)]
    seq += [(rows, a["w_out_2"], 256 * n) for n in range(4)]
    seq += ffn(lambda i: (up, 256 * i), lambda i: (up, 2816 + 256 * i), down)
    stream_b = stream(seq)

    lam_init = np.array([0.8 - 0.6 * float(np.exp(-0.3 * l)) for l in range(2)], np.float32)
    per_layer = np.stack([lam_init, np.float32(1.0) - lam_init], axis=1)
    par_b = np.concatenate(
        [features(a["attn_norm_2"]), features(a["mlp_norm_2"])]
        + [features(np.tile(a[n], (1, P // a[n].shape[1])))
           for n in ("qn_a_2", "kn_a_2", "qn_b_2", "kn_b_2", "qn_c_2", "kn_c_2", "subln_2")]
        + [np.broadcast_to(per_layer[:, None, :], (2, P, 2)), features(a["conv_b_2"]), features(a["conv_w_2"])], axis=2)
    grouped = [(j % 2) * 4 + 2 * g + j // 2 for g in range(2) for j in range(4)]
    row_b = np.concatenate([a["lam_q1_2"], a["lam_k1_2"], a["lam_q2_2"], a["lam_k2_2"], a["sinks_2"][:, grouped]], axis=1)

    i = np.arange(P)
    widths = np.array([[2, 8], [4, 16]])[i // 64]
    edge = 1.0 / np.minimum(np.arange(16)[None, None, :] + 1, widths[:, :, None])
    con = np.concatenate([np.eye(P), np.full((P, P), 1.0 / P), np.ones((P, P)), 1.0 / widths, edge.reshape(P, 32),
                          i[:, None] < 64, i[:, None] >= 64], axis=1).astype(np.float32)
    s, t = i[:, None], i[None, :]
    masks = [s == t] + [(s // (2 * h) == t // (2 * h)) & (s // h % 2 == 0) & (t // h % 2 == 1)
                        for h in (1, 2, 4, 8, 16, 32, 64)]
    lvl_mask = np.concatenate(masks, axis=1).astype(np.float32)

    def rope_table(dim):
        inv = np.float32(1.0) / (np.float32(10000.0) ** (np.arange(0, dim, 2, dtype=np.float32) / np.float32(dim)))
        ang = np.arange(256, dtype=np.float32)[None, :] * inv[i % (dim // 2)][:, None]
        return [np.cos(ang), np.sin(ang)]

    def head_mean(dim):
        return (s // dim == t // dim) / dim

    def swap_halves(dim):
        half = dim // 2
        return np.where((s == t + half) & (t % dim < half), -1.0, 0.0) + np.where((s == t - half) & (t % dim >= half), 1.0, 0.0)

    con_b = np.concatenate(rope_table(64) + rope_table(32) + [head_mean(64), head_mean(32), swap_halves(64), swap_halves(32)]
                           + [np.where(t <= s, 0.0, -1e30), np.where(t > s, 0.0, -1e30)], axis=1).astype(np.float32)

    arrays = {
        "stream_b": stream_b, "par_b": par_b, "row_b": row_b, "con_b": con_b,
        "x": a["x"][0], "mem": a["mem"][0], "stream_a": stream_a, "par_a": par_a, "rec_lb": rec_lb,
        "ln_g": a["ln_g"].reshape(8, 1024), "ln_b": a["ln_b"].reshape(8, 1024), "pool_w": a["pool_w"],
        "con": con, "lvl_mask": lvl_mask,
    }
    arrays = {k: np.ascontiguousarray(v) for k, v in arrays.items()}
    nc = bacc.Bacc("TRN2", target_bir_lowering=False, num_devices=1)
    dram = {k: nc.dram_tensor("in_" + k, v.shape, mybir.dt.from_np(v.dtype), kind="ExternalInput").ap() for k, v in arrays.items()}
    dram["out"] = nc.dram_tensor("out", (256, 1024), mybir.dt.float32, kind="ExternalOutput").ap()
    build_program(nc, dram)
    r = run_bass_kernel_spmd(nc, [{"in_" + k: v for k, v in arrays.items()}], core_ids=[0])
    return r.results[0]["out"].reshape(1, 256, 1024)
```

```python
def build_program(nc, dram):
    from contextlib import ExitStack

    import concourse.bass as bass
    from concourse import mybir

    F32, F32R, U8 = mybir.dt.float32, mybir.dt.float32r, mybir.dt.uint8
    ALU, ACT, AX = mybir.AluOpType, mybir.ActivationFunctionType, mybir.AxisListType

    P = 128
    D = 1024
    KT = D // P
    TOK = 256
    TT = TOK // P
    DEPTH = 2
    STEPS = 2816 // 256
    ALPHA = (2.0 * DEPTH) ** 0.25
    LN_EPS, RMS_EPS = 1e-5, 1e-6
    CA_HEADS = 4
    CA_SCALE = (D // CA_HEADS) ** -0.5
    HEADS = 4
    LEVELS = [1, 2, 4, 8, 16, 32, 64]
    F_FLOOR = 2.0 ** -62

    A_FFN1 = 0
    A_RF, A_RQ, A_CK0, A_RI, A_RG = 33, 35, 37, 38, 40
    A_CC, A_CH, A_CB, A_PU = 42, 43, 44, 45
    A_CK, A_CV = 46, 49
    A_WOUT = 51
    A_CQ, A_CV2, A_CO = 55, 59, 61
    A_FFN2 = 65
    A_CHUNKS = 98
    SLOTS = 3

    B_QC, B_KC, B_QA, B_KA, B_QB, B_KVB, B_VA, B_VC = 0, 1, 2, 3, 4, 6, 7, 8
    B_GATE = 9
    B_WC, B_WA, B_WB = 21, 22, 23
    B_WOUT = 25
    B_FFN = 29
    B_CHUNKS = 62
    ZT = 13
    QK_EPS = 1e-6
    GROUPS = 5
    ROUNDS = [(0, 4, 2, 32, [(0, 2, 20), (2, 4, 21)]), (4, 8, 4, 64, [(4, 6, 16), (6, 8, 17)]),
              (8, 12, 6, 64, [(8, 12, 18)]), (12, 13, 2, 64, [(12, 13, 19)])]

    def uses(chunks, slot):
        return len(range(slot, chunks, SLOTS))

    with ExitStack() as ctx:
        def sb(name, shape, dt=F32):
            return ctx.enter_context(nc.sbuf_tensor(name, shape, dt))

        raw = sb("raw", [P, SLOTS, 2048])
        whi = sb("whi", [P, SLOTS, 2048], F32R)
        wlo = sb("wlo", [P, SLOTS, 2048], F32R)
        res = sb("res", [P, TT, D])
        xh = sb("xh", [P, KT, TOK], F32R)
        xl = sb("xl", [P, KT, TOK], F32R)
        yh = sb("yh", [P, KT, TOK], F32R)
        yl = sb("yl", [P, KT, TOK], F32R)
        mh = sb("mh", [P, KT, TOK], F32R)
        ml = sb("ml", [P, KT, TOK], F32R)
        work = sb("work", [P, 17, 1024])
        con = sb("con", [P, dram["con"].shape[1]])
        lvl_mask = sb("lvl_mask", [P, 8, P], U8)
        par = sb("par", [P, dram["par_a"].shape[2]])
        rlb = sb("rlb", [P, 2, HEADS])
        lbt = sb("lbt", [P, 2, 3, HEADS])
        lbc = sb("lbc", [P, 3, HEADS])
        lbw = sb("lbw", [P, 6, HEADS])
        poolw = sb("poolw", [P, 2, P])
        stat = sb("stat", [P, TT, 2, 6])
        mv = sb("mv", [P, TT, 2])
        vare = sb("vare", [P, TT])
        rstd = sb("rstd", [P, TT])
        mhalf = sb("mhalf", [P, 1])
        eps = sb("eps", [P, 1])
        held = sb("held", [P, 2])
        mx = sb("mx", [P, 8])
        nmx = sb("nmx", [P, 8])
        rsum = sb("rsum", [P, 8])
        rinv = sb("rinv", [P, 8])
        ps = ctx.enter_context(nc.psum_tensor("ps", [P, 8, 512], F32))

        parb = sb("parb", [P, dram["par_b"].shape[2]])
        rowb = sb("rowb", [P, dram["row_b"].shape[1]])
        lamw = sb("lamw", [P, 2, 32])
        lams = sb("lams", [P, 4])
        nlam = sb("nlam", [P, 1])
        subg = sb("subg", [P, 1])
        rlam = sb("rlam", [P, 8])
        sinkx = sb("sinkx", [P, 8])
        maskb = sb("maskb", [P, 3, P], mybir.dt.bfloat16)
        OB = sb("OB", [P, 512])
        ident = con[:, 0:128]
        mean128 = con[:, 128:256]
        ones = con[:, 256:384]
        invw = con[:, 384:386]
        edge = con[:, 386:418].rearrange("p (f t) -> p f t", f=2)
        first_half, second_half = con[:, 418:419], con[:, 419:420]

        def units(u, n=1):
            return work[:, u:u + n, :].rearrange("p u n -> p (u n)")

        sg = units(0).rearrange("p (b n) -> p b n", b=2)
        hg = units(1).rearrange("p (b n) -> p b n", b=2)
        tabg, tabb = units(5), units(6)
        ybuf = units(7, 2).rearrange("p (t n) -> p t n", t=TT)
        xf = units(3, 2).rearrange("p (k n) -> p k n", k=KT)
        memf = units(7, 2).rearrange("p (k n) -> p k n", k=KT)
        Q = units(0)
        SIG = units(1)
        KEY = units(2)
        LOGF = units(3)
        EXPD = units(4)
        qlev = [units(5), units(7)]
        klev = [units(6), units(8)]
        AT = units(9).rearrange("p (g t) -> p g t", t=P)
        ATX = work[:, 10, 0:512].rearrange("p (h t) -> p h t", t=P)
        TMP = work[:, 10, 512:1024].rearrange("p (f t) -> p f t", t=TOK)
        VAL = units(11).rearrange("p (t n) -> p t n", t=TT)
        RG = units(12)
        CC = work[:, 13, 0:512].rearrange("p (f t) -> p f t", t=TOK)
        CH = work[:, 13, 512:1024].rearrange("p (f t) -> p f t", t=TOK)
        CB = work[:, 16, 0:512].rearrange("p (f t) -> p f t", t=TOK)
        PU = work[:, 16, 512:1024].rearrange("p (f t) -> p f t", t=TOK)
        CKT = units(14, 2).rearrange("p (k n) -> p k n", k=KT)
        CQT = units(0, 2).rearrange("p (k n) -> p k n", k=KT)
        CVM = [units(2 + n).rearrange("p (t n) -> p t n", t=TT) for n in range(2)]
        PROB = units(7, 2).rearrange("p (g n) -> p g n", g=8)
        PROBT = units(11, 2).rearrange("p (g n) -> p g n", g=8)

        def ln_g(j, k):
            return par[:, j * 8 + k:j * 8 + k + 1]

        def ln_b(j, k):
            return par[:, 32 + j * 8 + k:32 + j * 8 + k + 1]

        def conv_w(tap, ft):
            return par[:, 64 + tap * 2 + ft:65 + tap * 2 + ft]

        def norm_g(h):
            return par[:, 70 + h:71 + h]

        def pool_scale(ft):
            return par[:, 74 + ft:75 + ft]

        flat = work[:].rearrange("p u n -> p (u n)")
        GATE = flat[:, 0:6144].rearrange("p (n c) -> p n c", c=512)
        nbuf = units(0, 2).rearrange("p (t n) -> p t n", t=TT)
        xf2 = units(2, 2).rearrange("p (k n) -> p k n", k=KT)
        junk = units(4)
        cvg = units(5).rearrange("p (b n) -> p b n", b=2)
        cvv = units(6).rearrange("p (b n) -> p b n", b=2)
        Z = flat[:, 6144:9472]
        RZ = flat[:, 9472:12800]
        PR = [flat[:, 9472:11008], flat[:, 11008:12544]]
        PT = flat[:, 12544:14080]
        VA = flat[:, 14080:14592].rearrange("p (t n) -> p t n", t=TT)
        VB = flat[:, 14592:14848].rearrange("p (t n) -> p t n", t=TT)
        VC = flat[:, 14848:15360].rearrange("p (t n) -> p t n", t=TT)
        CONB = flat[:, 15360:17152]
        rope = {64: (CONB[:, 0:256], CONB[:, 256:512]), 32: (CONB[:, 512:768], CONB[:, 768:1024])}
        headmean = {64: CONB[:, 1024:1152], 32: CONB[:, 1152:1280]}
        swap = {64: CONB[:, 1280:1408], 32: CONB[:, 1408:1536]}
        OC = flat[:, 6656:7168]
        CSQ = flat[:, 6144:6656]
        CRS = flat[:, 7168:7680]
        VBF = OB[:, 0:TOK]
        identb, trib, bandb = maskb[:, 0, :], maskb[:, 1, :], maskb[:, 2, :]

        def conv_b2(tile):
            return parb[:, bass.ds(25 + tile, 1)]

        def conv_w2(tap, tile):
            return parb[:, bass.ds(69 + 44 * tap + tile, 1)]

        class Signal:

            def __init__(self, name, per_layer, base=0, sem=None):
                self.sem = ctx.enter_context(nc.semaphore(name)) if sem is None else sem
                self.per_layer, self.base = per_layer, base

            def nth(self, l, n):
                return l * self.per_layer + (self.base + n)

            def again(self, per_layer, between=0):
                return Signal(None, per_layer, self.base + DEPTH * self.per_layer + between, self.sem)

        class Order:

            def __init__(self, eng, results):
                self.eng, self.results, self.n, self.l = eng, results, 0, None

            def layer(self, l):
                self.l, self.n = l, 0

            def next_decoder(self, results):
                self.close()
                self.results, self.l, self.n = results, None, results.base

            def put(self, instruction):
                instruction.then_inc(self.results.sem, 1)
                self.n += 1

            def settle(self):
                if self.l is None:
                    self.eng.wait_ge(self.results.sem, self.n)
                else:
                    self.eng.wait_ge(self.results.sem, self.results.nth(self.l, self.n))

            def close(self):
                want = self.results.base if self.l is None else self.results.per_layer
                assert self.n == want, (self.results.sem, self.n, want)

        raw_full = [Signal(f"raw_full{s}", 16 * uses(A_CHUNKS, s)) for s in range(SLOTS)]
        hi_ready = [Signal(f"hi_ready{s}", uses(A_CHUNKS, s)) for s in range(SLOTS)]
        split_ready = [Signal(f"split_ready{s}", uses(A_CHUNKS, s), 1) for s in range(SLOTS)]
        chunk_done = [Signal(f"chunk_done{s}", uses(A_CHUNKS, s), 1) for s in range(SLOTS)]

        inputs_in = Signal("inputs_in", 0)
        mem_in = Signal("mem_in", 0)
        setup_in = Signal("setup_in", 0)
        mem_turned = Signal("mem_turned", 0)
        mem_full = Signal("mem_full", 0)
        mem_ready = Signal("mem_ready", 0)
        params_in = Signal("params_in", 48)
        tables_in = Signal("tables_in", 4 * 32)
        const_set = Signal("const_set", 0)
        bounds_exp = Signal("bounds_exp", 0)
        bounds_max = Signal("bounds_max", 0)

        gate_ready = Signal("gate_ready", 2 * STEPS)
        hidden_ready = Signal("hidden_ready", 2 * STEPS)
        hidden_hi = Signal("hidden_hi", 2 * STEPS)
        hidden_split = Signal("hidden_split", 2 * STEPS)

        var_ready = Signal("var_ready", 8)
        rstd_ready = Signal("rstd_ready", 8)
        normed = Signal("normed", 8)
        turned = Signal("turned", 16, 4)
        x_full = Signal("x_full", 16, 4)
        x_ready = Signal("x_ready", 16, 4)
        residual_ready = Signal("residual_ready", 8, 2)
        acc_ready = Signal("acc_ready", 12)

        evacuated = Signal("evacuated", 24)
        floored = Signal("floored", 1)
        logs_ready = Signal("logs_ready", 1)
        keys_ready = Signal("keys_ready", 1)
        decay_ready = Signal("decay_ready", 1)
        spread_ready = Signal("spread_ready", 8)
        decay_exp = Signal("decay_exp", 8)
        level_ready = Signal("level_ready", 8)
        level_scored = Signal("level_scored", 9)
        level_merged = Signal("level_merged", 8)
        cross_ready = Signal("cross_ready", 1)
        o_ready = Signal("o_ready", 1)
        o_squared = Signal("o_squared", 1)
        o_summed = Signal("o_summed", 1)
        o_rstd = Signal("o_rstd", 1)
        gate_exp = Signal("gate_exp", 1)
        rec_full = Signal("rec_full", 1)
        rec_read = Signal("rec_read", 1)
        rec_hi = Signal("rec_hi", 1)
        rec_ready = Signal("rec_ready", 1)
        conv_ready = Signal("conv_ready", 1)
        windows_ready = Signal("windows_ready", 1)
        pooled = Signal("pooled", 1)
        pool_full = Signal("pool_full", 1)
        pool_ready = Signal("pool_ready", 1)

        scored = Signal("scored", 2)
        max_ready = Signal("max_ready", 2)
        prob_ready = Signal("prob_ready", 2)
        prob_normed = Signal("prob_normed", 2)
        prob_turned = Signal("prob_turned", 4)
        probt_act = Signal("probt_act", 2)
        probt_dve = Signal("probt_dve", 2)
        attn_ready = Signal("attn_ready", 4)
        attn_hi = Signal("attn_hi", 4)
        attn_split = Signal("attn_split", 4)

        act_order = Signal("act_order", 3)
        dve_order = Signal("dve_order", 91, 22)
        pool_order = Signal("pool_order", 43, 2)
        out_stored = Signal("out_stored", 0)

        class Ring:

            def __init__(self, full, hi, split, done, chunks):
                self.full, self.hi, self.split, self.done, self.chunks = full, hi, split, done, chunks

        A = Ring(raw_full, hi_ready, split_ready, chunk_done, A_CHUNKS)
        AHEAD = 2
        B = Ring([raw_full[s].again(16 * uses(B_CHUNKS, s), 16 * (s < AHEAD)) for s in range(SLOTS)],
                 *[[kind[s].again(uses(B_CHUNKS, s), int(s < AHEAD)) for s in range(SLOTS)]
                   for kind in (hi_ready, split_ready, chunk_done)],
                 B_CHUNKS)

        b_params_in = Signal("b_params_in", 32)
        b_consts_in = Signal("b_consts_in", 0)
        b_masks_set = Signal("b_masks_set", 2)
        b_hidden_ready, b_hidden_hi, b_hidden_split, b_gate_ready = [
            x.again(STEPS) for x in (hidden_ready, hidden_hi, hidden_split, gate_ready)]
        b_gate_scaled = Signal("b_gate_scaled", STEPS)
        b_gate_conv = Signal("b_gate_conv", STEPS)
        b_value_scaled = Signal("b_value_scaled", STEPS)
        b_value_conv = Signal("b_value_conv", STEPS)
        b_taps = Signal("b_taps", 6 * STEPS)
        b_res_ready = Signal("b_res_ready", 8, 4)
        b_acc_ready = acc_ready.again(6)
        b_squares = Signal("b_squares", 4)
        b_var_ready, b_rstd_ready, b_normed = [x.again(4) for x in (var_ready, rstd_ready, normed)]
        b_turned, b_x_full, b_x_ready = [x.again(8) for x in (turned, x_full, x_ready)]
        b_evacuated = Signal("b_evacuated", 21)
        b_summed = Signal("b_summed", 4)
        b_values_turned = Signal("b_values_turned", 1)
        b_qk_rstd = Signal("b_qk_rstd", 4)
        b_qk_normed = Signal("b_qk_normed", 4)
        b_rotated = Signal("b_rotated", 4)
        b_sine = Signal("b_sine", 4)
        b_roped = Signal("b_roped", 4)
        b_cosine = Signal("b_cosine", 4)
        b_lam_sums = Signal("b_lam_sums", 1)
        b_lam_exp = Signal("b_lam_exp", 1)
        b_scored = Signal("b_scored", GROUPS)
        b_row_scored = Signal("b_row_scored", 3 * 2 + 3)
        b_max = Signal("b_max", GROUPS)
        b_prob = Signal("b_prob", GROUPS)
        b_prob_normed = Signal("b_prob_normed", GROUPS)
        b_prob_turned = Signal("b_prob_turned", GROUPS)
        b_pt_act = Signal("b_pt_act", GROUPS)
        b_pt_dve = Signal("b_pt_dve", GROUPS)
        b_pv = Signal("b_pv", GROUPS)
        b_o_out = Signal("b_o_out", GROUPS)
        b_y_ready = Signal("b_y_ready", 3)
        b_c_squared = Signal("b_c_squared", 1)
        b_c_summed = Signal("b_c_summed", 1)
        b_c_rstd = Signal("b_c_rstd", 1)
        b_yc_ready = Signal("b_yc_ready", 1)
        b_gates_open = Signal("b_gates_open", 3)
        b_branch_done = Signal("b_branch_done", 12)
        b_gated = Signal("b_gated", 12)
        b_pair_merged = Signal("b_pair_merged", 4)
        b_merge_ready = Signal("b_merge_ready", 4)
        act_order_b = act_order.again(9)
        dve_order_b = dve_order.again(60)
        pool_order_b = pool_order.again(0)

        def chunk(c, more=0, ring=None):
            if ring is A and c >= A_CHUNKS:
                return c - A_CHUNKS, uses(A_CHUNKS, c - A_CHUNKS)
            return c % SLOTS, c // SLOTS + more

        def chunk_wait(eng, l, c, more=0, ring=A):
            s, u = chunk(c, more)
            eng.wait_ge(ring.done[s].sem, ring.done[s].nth(l, u + 1))

        def branch_bank(bank0, b):
            return bank0 + (b + 2) % 4

        block = ctx.enter_context(nc.Block())

        @block.sync
        def _(sp):
            sp.dma_start(con[:], dram["con"]).then_inc(inputs_in.sem, 16)
            sp.dma_start(res[:], dram["x"].rearrange("(t p) n -> p t n", p=P)).then_inc(inputs_in.sem, 16)

            def load(ring, l, s, u, src):
                sp.wait_ge(ring.split[s].sem, ring.split[s].nth(l, u))
                sp.dma_start(raw[:, s, :], src).then_inc(ring.full[s].sem, 16)

            for ring, name in ((A, "stream_a"), (B, "stream_b")):
                stream, count = dram[name], ring.chunks
                with sp.Fori(0, DEPTH) as l:
                    with sp.Fori(0, count // SLOTS) as u:
                        for s in range(SLOTS):
                            load(ring, l, s, u, stream[bass.ds(l * (count * P) + u * (SLOTS * P) + s * P, P), :])
                    for c in range(count // SLOTS * SLOTS, count):
                        load(ring, l, c % SLOTS, c // SLOTS, stream[bass.ds(l * (count * P) + c * P, P), :])
                if ring is A:
                    for s in range(AHEAD):
                        sp.wait_ge(A.split[s].sem, A.split[s].nth(DEPTH, 0))
                        sp.sem_inc(A.full[s].sem, 16)
                    sp.dma_start(CONB, dram["con_b"]).then_inc(b_consts_in.sem, 16)

            for t in range(TT):
                sp.wait_ge(b_res_ready.sem, b_res_ready.nth(DEPTH, 2 * t - 2))
                sp.dma_start(dram["out"][t * P:(t + 1) * P, :], res[:, t, :]).then_inc(out_stored.sem, 16)
            sp.wait_ge(out_stored.sem, 16 * TT)

        @block.tensor
        def _(pe):
            def chunk_in(l, c, more=0, ring=A):
                s, u = chunk(c, more)
                pe.wait_ge(ring.split[s].sem, ring.split[s].nth(l, u + 1))

            def parts(s, tiles):
                n = 2048 // tiles
                return (whi[:, s, :].rearrange("p (k n) -> p k n", n=n),
                        wlo[:, s, :].rearrange("p (k n) -> p k n", n=n))

            def feature_tiles(l, c, bank, ah, al, more=0, ring=A, arrives=None):
                chunk_in(l, c, more, ring)
                s, _ = chunk(c, more)
                wh, wl = parts(s, KT)
                for ft in range(2):
                    out = ps[:, bank, ft * TOK:(ft + 1) * TOK]
                    cols = slice(ft * P, (ft + 1) * P)
                    for k in range(KT):
                        if arrives and ft == 0 and k % 2 == 0:
                            pe.wait_ge(arrives[0].sem, arrives[0].nth(l, arrives[1] + k // 2 + 1))
                        nc.tensor.matmul(out, wh[:, k, cols], ah[:, k, :], start=(k == 0), stop=False)
                        nc.tensor.matmul(out, wh[:, k, cols], al[:, k, :], start=False, stop=False)
                        last = nc.tensor.matmul(out, wl[:, k, cols], ah[:, k, :], start=False, stop=(k == KT - 1))
                last.then_inc(chunk_done[s].sem, 1)

            def token_tiles(l, c, bank, ah, al, ring=A):
                chunk_in(l, c, 0, ring)
                s, _ = chunk(c)
                wh, wl = parts(s, KT)
                for t in range(TT):
                    out = ps[:, bank, t * 256:(t + 1) * 256]
                    rows = slice(t * P, (t + 1) * P)
                    for k in range(KT):
                        nc.tensor.matmul(out, ah[:, k, rows], wh[:, k, :], start=(k == 0), stop=False)
                        nc.tensor.matmul(out, ah[:, k, rows], wl[:, k, :], start=False, stop=False)
                        last = nc.tensor.matmul(out, al[:, k, rows], wh[:, k, :], start=False, stop=(k == KT - 1))
                last.then_inc(chunk_done[s].sem, 1)

            def accumulate(l, c, ah, al, first, final, more=0, ring=A):
                chunk_in(l, c, more, ring)
                s, _ = chunk(c, more)
                wh, wl = parts(s, 2)
                if final:
                    for b in range(4):
                        t, half = b // 2, b % 2
                        passes = [(a, w, k) for k in range(2) for a, w in ((ah, wh), (ah, wl), (al, wh))]
                        for n, (a, w, k) in enumerate(passes):
                            last = nc.tensor.matmul(ps[:, 4 + b, :], a[:, k, t * P:(t + 1) * P],
                                                    w[:, k, half * 512:(half + 1) * 512], start=False, stop=(n == len(passes) - 1))
                        last.then_inc(*((acc_ready.sem, 1) if b < 3 else (chunk_done[s].sem, 1)))
                    return
                for k in range(2):
                    for t in range(TT):
                        rows = slice(t * P, (t + 1) * P)
                        for n, (a, w) in enumerate(((ah, wh), (ah, wl), (al, wh))):
                            for half in range(2):
                                last = nc.tensor.matmul(
                                    ps[:, 4 + 2 * t + half, :], a[:, k, rows], w[:, k, half * 512:(half + 1) * 512],
                                    start=(first and k == 0 and n == 0), stop=False)
                last.then_inc(chunk_done[s].sem, 1)

            def turn(src, bank0, done=turned):
                for t in range(TT):
                    yield t
                    for k in range(KT):
                        last = nc.tensor.transpose(
                            ps[:, bank0 + k // 2, (k % 2) * TOK + t * P:(k % 2) * TOK + (t + 1) * P],
                            src[:, t, k * P:(k + 1) * P], ident)
                        if t == TT - 1 and k % 2 == 1:
                            last.then_inc(done.sem, 1)

            def ffn(l, c0, f, arrives, ring=A, ready=hidden_ready, split=hidden_split):
                def pair(i, more):
                    if i >= 2:
                        pe.wait_ge(ready.sem, ready.nth(l, f * STEPS + i - 1 + more))
                    b = 2 * (i % 2)
                    c = c0 if i == 0 else c0 + 2 + 3 * (i - 1)
                    feature_tiles(l, c, b, xh, xl, more, ring, arrives if i == 0 else None)
                    feature_tiles(l, c + 1, b + 1, xh, xl, more, ring)

                def down(i, more):
                    b = i % 2
                    pe.wait_ge(split.sem, split.nth(l, f * STEPS + i + 1 + more))
                    c = c0 + 2 + 3 * i + 2 if i < STEPS - 1 else c0 + 3 * STEPS - 1
                    accumulate(l, c, yh[:, 2 * b:2 * b + 2, :], yl[:, 2 * b:2 * b + 2, :],
                               i == 0, i == STEPS - 1, more, ring)

                pair(0, 0)
                for i in (1, 2):
                    pair(i, 0)
                    if i == 1 and c0 == A_FFN1:
                        pe.wait_ge(mem_full.sem, 4)
                    down(i - 1, 0)
                with pe.Fori(0, (STEPS - 3) // 2) as r:
                    for i in (3, 4):
                        pair(i, 2 * r)
                        down(i - 1, 2 * r)
                down(STEPS - 1, 0)

            def norm_turn(l, j):
                for t in turn(ybuf, 0):
                    pe.wait_ge(normed.sem, normed.nth(l, 2 * j + t + 1))

            def level(l, n):
                b = 4 + 2 * (n % 2)
                if n == 0:
                    pe.wait_ge(keys_ready.sem, keys_ready.nth(l, 1))
                    pe.wait_ge(evacuated.sem, evacuated.nth(l, 4))
                else:
                    pe.wait_ge(level_ready.sem, level_ready.nth(l, n))
                if n == 3:
                    pe.wait_ge(cross_ready.sem, cross_ready.nth(l, 1))
                elif n >= 2:
                    pe.wait_ge(level_merged.sem, level_merged.nth(l, max(n - 2, 1)))
                q, k = (Q, KEY) if n == 0 else (qlev[n % 2], klev[n % 2])
                if n == 1:
                    for h in range(HEADS):
                        last = nc.tensor.matmul(ps[:, b, h * P:(h + 1) * P], k[:, h * TOK:h * TOK + P],
                                                q[:, h * TOK + P:(h + 1) * TOK], start=True, stop=True)
                else:
                    for g in range(HEADS * TT):
                        last = nc.tensor.matmul(ps[:, b + g // 4, (g % 4) * P:(g % 4 + 1) * P],
                                                k[:, g * P:(g + 1) * P], q[:, g * P:(g + 1) * P], start=True, stop=True)
                last.then_inc(level_scored.sem, 1)

            def recurrence_out(l):
                pe.wait_ge(level_merged.sem, level_merged.nth(l, 8))
                pe.wait_ge(cross_ready.sem, cross_ready.nth(l, 1))
                pe.wait_ge(evacuated.sem, evacuated.nth(l, 7))
                for h in range(HEADS):
                    v = [VAL[:, t, h * P:(h + 1) * P] for t in range(TT)]
                    out = ps[:, 4 + h // 2, (h % 2) * TOK:(h % 2 + 1) * TOK]
                    nc.tensor.matmul(out[:, 0:P], v[0], AT[:, 2 * h, :], start=True, stop=True)
                    nc.tensor.matmul(out[:, P:TOK], v[0], ATX[:, h, :], start=True, stop=False)
                    last = nc.tensor.matmul(out[:, P:TOK], v[1], AT[:, 2 * h + 1, :], start=False, stop=True)
                last.then_inc(o_ready.sem, 1)

            def recurrence_sums(l):
                pe.wait_ge(o_squared.sem, o_squared.nth(l, 1))
                for b in range(2):
                    last = nc.tensor.matmul(ps[:, 6 + b, :], mean128, EXPD[:, b * 512:(b + 1) * 512], start=True, stop=True)
                last.then_inc(o_summed.sem, 1)

            def mixer(l):
                def bank(c):
                    n = c - A_RF
                    if n >= 4:
                        pe.wait_ge(evacuated.sem, evacuated.nth(l, n - 3))
                    return n % 4

                pe.wait_ge(hidden_ready.sem, hidden_ready.nth(l, STEPS))
                for c in range(A_RF, A_WOUT):
                    b = bank(c)
                    if A_RI <= c < A_RG:
                        token_tiles(l, c, b, xh, xl)
                    elif c >= A_CV:
                        token_tiles(l, c, b, mh, ml)
                    elif c >= A_CK or c == A_CK0:
                        if c == A_CK0:
                            pe.wait_ge(mem_ready.sem, 4)
                        feature_tiles(l, c, b, mh, ml)
                    else:
                        feature_tiles(l, c, b, xh, xl, arrives=(x_ready, 0) if c == A_RF else None)
                    if A_RI <= c < A_RI + 9:
                        level(l, c - A_RI)
                    if c == A_CK + 2:
                        recurrence_out(l)
                    if c == A_CV:
                        recurrence_sums(l)

                pe.wait_ge(windows_ready.sem, windows_ready.nth(l, 1))
                pe.wait_ge(params_in.sem, params_in.nth(l, 48))
                pe.wait_ge(evacuated.sem, evacuated.nth(l, 17))
                for ft in range(2):
                    last = nc.tensor.matmul(ps[:, 0, ft * TOK:(ft + 1) * TOK], poolw[:, ft, :], TMP[:, ft, :],
                                            start=True, stop=True)
                last.then_inc(pooled.sem, 1)

                pe.wait_ge(conv_ready.sem, conv_ready.nth(l, 1))
                pe.wait_ge(rec_read.sem, rec_read.nth(l, 1))
                for n, tiles in enumerate((0, 6, 2, 4)):
                    if n == 1:
                        pe.wait_ge(pool_ready.sem, pool_ready.nth(l, 1))
                    if n == 2:
                        pe.wait_ge(rec_ready.sem, rec_ready.nth(l, 1))
                    accumulate(l, A_WOUT + n, yh[:, tiles:tiles + 2, :], yl[:, tiles:tiles + 2, :], n == 0, n == 3)

            def cross_attention(l):
                for n in range(4):
                    feature_tiles(l, A_CQ + n, n, xh, xl, arrives=None if n else (x_ready, 4))
                pe.wait_ge(evacuated.sem, evacuated.nth(l, 22))
                for t in range(TT):
                    for h in range(CA_HEADS):
                        out = ps[:, 4 + 2 * t + h // 2, (h % 2) * 256:(h % 2 + 1) * 256]
                        for k in range(2):
                            last = nc.tensor.matmul(out, CQT[:, 2 * h + k, t * P:(t + 1) * P], CKT[:, 2 * h + k, :],
                                                    start=(k == 0), stop=(k == 1))
                    last.then_inc(scored.sem, 1)
                for n in range(2):
                    token_tiles(l, A_CV2 + n, n, mh, ml)
                for t in range(TT):
                    pe.wait_ge(prob_normed.sem, prob_normed.nth(l, 2))
                    for mt in range(2):
                        for h in range(CA_HEADS):
                            g = mt * CA_HEADS + h
                            last = nc.tensor.transpose(
                                ps[:, 4 + g // 2, (g % 2) * TOK + t * P:(g % 2) * TOK + (t + 1) * P],
                                PROB[:, t * CA_HEADS + h, mt * P:(mt + 1) * P], ident)
                            if t == TT - 1 and g % 2 == 1:
                                last.then_inc(prob_turned.sem, 1)
                pe.wait_ge(probt_act.sem, probt_act.nth(l, 2))
                pe.wait_ge(probt_dve.sem, probt_dve.nth(l, 2))
                pe.wait_ge(evacuated.sem, evacuated.nth(l, 24))
                for ft in range(KT):
                    for mt in range(2):
                        last = nc.tensor.matmul(ps[:, ft // 2, (ft % 2) * TOK:(ft % 2 + 1) * TOK],
                                                CVM[ft // 4][:, mt, (ft % 4) * P:(ft % 4 + 1) * P],
                                                PROBT[:, mt * CA_HEADS + ft // 2, :], start=(mt == 0), stop=(mt == 1))
                    if ft % 2 == 1:
                        last.then_inc(attn_ready.sem, 1)
                for n in range(4):
                    pe.wait_ge(attn_split.sem, attn_split.nth(l, n + 1))
                    accumulate(l, A_CO + n, yh[:, 2 * n:2 * n + 2, :], yl[:, 2 * n:2 * n + 2, :], n == 0, n == 3)

            for s in range(SLOTS):
                pe.sem_inc(chunk_done[s].sem, 1)
            pe.wait_ge(inputs_in.sem, 32)
            for _ in turn(res, 0):
                pass
            pe.wait_ge(mem_in.sem, 16)
            for _ in turn(units(9, 2).rearrange("p (t n) -> p t n", t=TT), 4, mem_turned):
                pass
            with pe.Fori(0, DEPTH) as l:
                ffn(l, A_FFN1, 0, (x_ready, -4))
                norm_turn(l, 0)
                mixer(l)
                norm_turn(l, 1)
                cross_attention(l)
                norm_turn(l, 2)
                ffn(l, A_FFN2, 1, (x_ready, 8))
                norm_turn(l, 3)
            for s in range(AHEAD):
                pe.wait_ge(A.split[s].sem, A.split[s].nth(DEPTH, 1))
                pe.sem_inc(chunk_done[s].sem, 1)

            def rms_turn(l, j):
                for t in turn(nbuf, 0):
                    pe.wait_ge(b_normed.sem, b_normed.nth(l, 2 * j + t + 1))

            def head_sums(l, r):
                z0, z1, bank, dim, _ = ROUNDS[r]
                if r == 0:
                    pe.wait_ge(b_consts_in.sem, 16)
                pe.wait_ge(b_evacuated.sem, b_evacuated.nth(l, (2, 4, 6, 7)[r]))
                if r == 3:
                    pe.wait_ge(b_sine.sem, b_sine.nth(l, 1))
                for n, z in enumerate(range(z0, z1, 2)):
                    w = min(2, z1 - z) * TOK
                    last = nc.tensor.matmul(ps[:, bank + n, 0:w], headmean[dim], RZ[:, z * TOK:z * TOK + w], start=True, stop=True)
                last.then_inc(b_summed.sem, 1)
                if r == 3:
                    for t in range(TT):
                        last = nc.tensor.transpose(ps[:, 3, t * P:(t + 1) * P], VBF[:, t * P:(t + 1) * P], ident)
                    last.then_inc(b_values_turned.sem, 1)

            def rotate(l, r):
                z0, z1, bank, dim, _ = ROUNDS[r]
                pe.wait_ge(b_qk_normed.sem, b_qk_normed.nth(l, r + 1))
                for n, z in enumerate(range(z0, z1, 2)):
                    w = min(2, z1 - z) * TOK
                    last = nc.tensor.matmul(ps[:, bank + n, 0:w], swap[dim], Z[:, z * TOK:z * TOK + w], start=True, stop=True)
                last.then_inc(b_rotated.sem, 1)

            def rows_of(g):
                if g < 2:
                    return [(g, 2 + g, slice(32 * j, 32 * j + 32)) for j in range(4)]
                tile = 4 if g == 2 else 8 + 2 * (g - 3)
                return [(tile + j // 2, 6 + j // 2 if g == 2 else 12, slice(64 * (j % 2), 64 * (j % 2) + 64)) for j in range(4)]

            def scores(l, g):
                if g == 0:
                    pe.wait_ge(b_masks_set.sem, b_masks_set.nth(l, 2))
                    pe.wait_ge(b_roped.sem, b_roped.nth(l, 4))
                    pe.wait_ge(b_sine.sem, b_sine.nth(l, 4))
                else:
                    pe.wait_ge(b_prob.sem, b_prob.nth(l, g))
                turns = list(range(4)) if g < 2 else [0, 2, 1, 3]
                for n, j in enumerate(turns):
                    qt, kt, rows = rows_of(g)[j]
                    if n and rows != rows_of(g)[turns[n - 1]][2]:
                        pe.wait_ge(b_row_scored.sem, b_row_scored.nth(l, 3 * g + n if g < 2 else 6 + g - 1))
                    q, k = [Z[rows, z * TOK:(z + 1) * TOK] for z in (qt, kt)]
                    for out, qs, ks, mask in (
                            (ps[:, 2, j * P:(j + 1) * P], 0, 0, trib),
                            (ps[:, 3 + j // 2, (j % 2) * 256:(j % 2) * 256 + P], P, 0, bandb if g >= 3 else None),
                            (ps[:, 3 + j // 2, (j % 2) * 256 + P:(j % 2 + 1) * 256], P, P, trib)):
                        last = nc.tensor.matmul(out, q[:, qs:qs + P], k[:, ks:ks + P], start=True, stop=mask is None)
                        if mask is not None:
                            last = nc.tensor.matmul(out, identb, mask, start=False, stop=True)
                    if n < 3 and rows != rows_of(g)[turns[n + 1]][2]:
                        last.then_inc(b_row_scored.sem, 1)
                last.then_inc(b_scored.sem, 1)

            def heads_of(g):
                return 2 if g < 2 else 4

            def prob_turn(l, g):
                pe.wait_ge(b_prob_normed.sem, b_prob_normed.nth(l, g + 1))
                if g:
                    pe.wait_ge(b_o_out.sem, b_o_out.nth(l, g))
                first = PR[g % 2][:, 0:512].rearrange("p (j n) -> p j n", n=P)
                second = PR[g % 2][:, 512:1536].rearrange("p (j n) -> p j n", n=256)
                for n in range(heads_of(g)):
                    j = 2 * n if g < 2 else n
                    near = ps[:, 5 + n // 2, (n % 2) * TOK:(n % 2 + 1) * TOK]
                    nc.tensor.transpose(near[:, 0:P], first[:, j, :], ident)
                    nc.tensor.transpose(near[:, P:TOK], second[:, j, 0:P], ident)
                    last = nc.tensor.transpose(ps[:, 7, n * P:(n + 1) * P], second[:, j, P:256], ident)
                last.then_inc(b_prob_turned.sem, 1)

            def values(l, g):
                pe.wait_ge(b_pt_act.sem, b_pt_act.nth(l, g + 1))
                pe.wait_ge(b_pt_dve.sem, b_pt_dve.nth(l, g + 1))
                for n in range(heads_of(g)):
                    v, head = (VC, 2 * g + n) if g < 2 else (VA, n) if g == 2 else (VB, n % 2)
                    v = v[:, :, head * 64:(head + 1) * 64]
                    out = ps[64 * (n % 2):64 * (n % 2) + 64, 5, (n // 2) * TOK:(n // 2 + 1) * TOK]
                    near, far = PT[:, n * TOK:(n + 1) * TOK], PT[:, 1024 + n * P:1024 + (n + 1) * P]
                    nc.tensor.matmul(out[:, 0:P], v[:, 0, :], near[:, 0:P], start=True, stop=True)
                    nc.tensor.matmul(out[:, P:TOK], v[:, 0, :], near[:, P:TOK], start=True, stop=False)
                    last = nc.tensor.matmul(out[:, P:TOK], v[:, 1, :], far, start=False, stop=True)
                last.then_inc(b_pv.sem, 1)

            def attention(l):
                for c in range(B_GATE + 12):
                    bank = c % 2
                    if c >= 2:
                        pe.wait_ge(b_evacuated.sem, b_evacuated.nth(l, c - 1))
                    if c in (B_VA, B_VC):
                        token_tiles(l, c, bank, xh, xl, B)
                    else:
                        feature_tiles(l, c, bank, xh, xl, 0, B, None if c else (b_x_ready, 0))
                    if c in (2, 4, 6, 8):
                        head_sums(l, c // 2 - 1)
                    if c in (5, 7, 9, 11):
                        rotate(l, (c - 5) // 2)
                    g = c - (B_GATE + 4)
                    if 2 <= g < GROUPS + 2:
                        values(l, g - 2)
                    if 0 <= g < GROUPS:
                        scores(l, g)
                    if 1 <= g < GROUPS + 1:
                        prob_turn(l, g - 1)
                    if g == GROUPS:
                        pe.wait_ge(b_c_squared.sem, b_c_squared.nth(l, 1))
                        nc.tensor.matmul(ps[:, 2, :], headmean[64], CSQ, start=True, stop=True).then_inc(b_c_summed.sem, 1)

            def branch(l, chunks, y0, bank0):
                for c in chunks:
                    chunk_in(l, c, 0, B)
                both = [parts(c % SLOTS, 2) for c in chunks]
                for ft in range(KT):
                    cols = slice(ft * P, (ft + 1) * P)
                    out = ps[:, branch_bank(bank0, ft // 2), (ft % 2) * TOK:(ft % 2 + 1) * TOK]
                    if chunks[0] == B_WC and ft == 4:
                        pe.wait_ge(b_evacuated.sem, b_evacuated.nth(l, 21))
                    steps = [(wh, wl, k, y0 + 2 * n + k) for n, (wh, wl) in enumerate(both) for k in range(2)]
                    for n, (wh, wl, k, y) in enumerate(steps):
                        nc.tensor.matmul(out, wh[:, k, cols], yh[:, y, :], start=(n == 0), stop=False)
                        nc.tensor.matmul(out, wh[:, k, cols], yl[:, y, :], start=False, stop=False)
                        last = nc.tensor.matmul(out, wl[:, k, cols], yh[:, y, :], start=False, stop=(n == len(steps) - 1))
                    if ft % 2 == 1:
                        last.then_inc(b_branch_done.sem, 1)
                for c in chunks:
                    pe.wait_ge(b_branch_done.sem, b_branch_done.nth(l, 4 * (1 + (B_WC, B_WA, B_WB).index(chunks[0]))))
                    pe.sem_inc(chunk_done[c % SLOTS].sem, 1)

            def merge(l):
                pe.wait_ge(b_c_rstd.sem, b_c_rstd.nth(l, 1))
                pe.wait_ge(b_yc_ready.sem, b_yc_ready.nth(l, 1))
                branch(l, [B_WC], 6, 0)
                pe.wait_ge(b_o_out.sem, b_o_out.nth(l, GROUPS))
                pe.wait_ge(b_y_ready.sem, b_y_ready.nth(l, 1))
                branch(l, [B_WA], 0, 4)
                pe.wait_ge(b_y_ready.sem, b_y_ready.nth(l, 3))
                pe.wait_ge(b_gated.sem, b_gated.nth(l, 4))
                branch(l, [B_WB, B_WB + 1], 2, 0)
                pe.wait_ge(b_gated.sem, b_gated.nth(l, 8))
                for n in range(4):
                    pe.wait_ge(b_merge_ready.sem, b_merge_ready.nth(l, n + 1))
                    accumulate(l, B_WOUT + n, xh[:, 2 * n:2 * n + 2, :], xl[:, 2 * n:2 * n + 2, :], n == 0, n == 3, 0, B)

            with pe.Fori(0, DEPTH) as l:
                rms_turn(l, 0)
                attention(l)
                merge(l)
                rms_turn(l, 1)
                ffn(l, B_FFN, 0, (b_x_ready, 4), B, b_hidden_ready, b_hidden_split)

        @block.scalar
        def _(act):
            order = Order(act, act_order)

            def high(l, c, more=0, ring=A):
                if ring is B and isinstance(more, int) and c + 3 * more >= ring.chunks:
                    return
                s, u = chunk(c, more, ring)
                act.wait_ge(ring.full[s].sem, ring.full[s].nth(l, (u + 1) * 16))
                act.wait_ge(ring.done[s].sem, ring.done[s].nth(l, u))
                nc.scalar.activation(whi[:, s, :], raw[:, s, :], ACT.Copy).then_inc(hi_ready[s].sem, 1)

            def ffn(l, c0, f):
                def step(i, more):
                    b, c = i % 2, c0 + 2 + 3 * (i - 1)
                    if i == 0:
                        c = c0
                    n = f * STEPS + i + more
                    high(l, c + 2, more)
                    chunk_wait(act, l, c, more)
                    if i >= 2:
                        act.wait_ge(hidden_ready.sem, hidden_ready.nth(l, n - 1))
                    nc.scalar.activation(sg[:, b, :], ps[:, 2 * b, :], ACT.Silu).then_inc(gate_ready.sem, 1)
                    high(l, c + 3, more)
                    if i and c + 4 < A_CHUNKS:
                        high(l, c + 4, more)
                    act.wait_ge(hidden_ready.sem, hidden_ready.nth(l, n + 1))
                    nc.scalar.activation(yh[:, 2 * b:2 * b + 2, :], hg[:, b, :].rearrange("p (k n) -> p k n", k=2),
                                         ACT.Copy).then_inc(hidden_hi.sem, 1)

                for i in range(3):
                    step(i, 0)
                with act.Fori(0, (STEPS - 5) // 2) as r:
                    for i in (3, 4):
                        step(i, 2 * r)
                for i in (STEPS - 2, STEPS - 1):
                    step(i, 0)
                for c in (c0 + 3 * STEPS, c0 + 3 * STEPS + 1)[0 if f else 1:]:
                    high(l, c)

            def widen(l, n, j):
                for b in range(4):
                    act.wait_ge(turned.sem, turned.nth(l, n + b + 1))
                    if j is None:
                        nc.scalar.activation(xf[:, 2 * b:2 * b + 2, :], ps[:, b, :].rearrange("p (k n) -> p k n", k=2),
                                             ACT.Copy).then_inc(x_full.sem, 1)
                        continue
                    for k in (2 * b, 2 * b + 1):
                        last = nc.scalar.activation(xf[:, k, :], ps[:, b, (k % 2) * TOK:(k % 2 + 1) * TOK], ACT.Identity,
                                                    scale=ln_g(j, k), bias=ln_b(j, k))
                    last.then_inc(x_full.sem, 1)

            def mixer(l):
                def half(buf, n):
                    return buf[:, n * 512:(n + 1) * 512]

                homes = {A_RF: half(SIG, 0), A_RF + 1: half(SIG, 1), A_RQ: half(Q, 0), A_RQ + 1: half(Q, 1),
                         A_RG: half(RG, 0), A_RG + 1: half(RG, 1), A_CC: CC, A_CH: CH, A_CB: CB, A_PU: PU}
                for n, c in enumerate((A_CK0, A_CK, A_CK + 1, A_CK + 2)):
                    homes[c] = CKT[:, 2 * n:2 * n + 2, :]
                for n in range(2):
                    homes[A_RI + n] = VAL[:, :, n * 256:(n + 1) * 256]
                    homes[A_CV + n] = CVM[0][:, :, n * 256:(n + 1) * 256]

                def spread(buf, side, h):
                    return buf.rearrange("p (n s h) -> p n s h", s=2, h=h)[:, :, side, :]

                def decays(n):
                    if n == 1:
                        act.wait_ge(decay_ready.sem, decay_ready.nth(l, 1))
                    act.wait_ge(spread_ready.sem, spread_ready.nth(l, n))
                    if n >= 2:
                        act.wait_ge(level_ready.sem, level_ready.nth(l, n - 1))
                    h = P if n == 1 else LEVELS[::-1][n - 2]
                    late = SIG if n == 1 else LOGF
                    nc.scalar.activation(spread(EXPD, 1, h), spread(late, 1, h), ACT.Exp)
                    nc.scalar.activation(spread(EXPD, 0, h), spread(LOGF, 0, h), ACT.Exp, scale=-1.0)\
                        .then_inc(decay_exp.sem, 1)

                for c in range(A_RF, A_WOUT):
                    if c <= A_CV:
                        high(l, c + 2)
                    if c == A_CV:
                        act.wait_ge(o_ready.sem, o_ready.nth(l, 1))
                        act.wait_ge(level_ready.sem, level_ready.nth(l, 8))
                        nc.scalar.activation(EXPD, ps[:, 4:6, :].rearrange("p b n -> p (b n)"), ACT.Square)\
                            .then_inc(o_squared.sem, 1)
                    if c == A_CV + 1:
                        act.wait_ge(o_summed.sem, o_summed.nth(l, 1))
                        order.put(nc.scalar.activation(LOGF, ps[:, 6:8, :].rearrange("p b n -> p (b n)"), ACT.Ln, bias=eps[:]))
                        order.settle()
                        nc.scalar.activation(LOGF, LOGF, ACT.Exp, scale=-0.5).then_inc(o_rstd.sem, 1)
                        high(l, c + 2)
                    chunk_wait(act, l, c)
                    out = homes[c]
                    src = ps[:, (c - A_RF) % 4, :]
                    if len(out.shape) == 3:
                        src = src.rearrange("p (a n) -> p a n", a=2)
                    if c == A_RF:
                        act.wait_ge(x_ready.sem, x_ready.nth(l, 4))
                    nc.scalar.activation(out, src, ACT.Sigmoid if c < A_RQ else ACT.Copy).then_inc(evacuated.sem, 1)
                    if c == A_RF + 1:
                        act.wait_ge(floored.sem, floored.nth(l, 1))
                        for h in range(HEADS):
                            s = slice(h * TOK, (h + 1) * TOK)
                            last = nc.scalar.activation(LOGF[:, s], SIG[:, s], ACT.Ln,
                                                        scale=lbc[:, 1, h:h + 1], bias=lbc[:, 0, h:h + 1])
                        last.then_inc(logs_ready.sem, 1)
                    if c == A_RQ + 1:
                        decays(1)
                    if A_RI <= c < A_RI + 7:
                        decays(c - A_RI + 2)
                    if c == A_RI + 3:
                        act.wait_ge(level_scored.sem, level_scored.nth(l, 2))
                        nc.scalar.activation(ATX, ps[:, 6, :].rearrange("p (h t) -> p h t", t=P), ACT.Copy)\
                            .then_inc(cross_ready.sem, 1)
                    if c == A_CC:
                        act.wait_ge(evacuated.sem, evacuated.nth(l, 9))
                        nc.scalar.activation(RG, RG, ACT.Exp, scale=-1.0).then_inc(gate_exp.sem, 1)
                act.wait_ge(pooled.sem, pooled.nth(l, 1))
                for ft in range(2):
                    order.put(nc.scalar.activation(PU[:, ft, :], ps[:, 0, ft * TOK:(ft + 1) * TOK], ACT.Identity,
                                                   scale=pool_scale(ft)))
                order.settle()
                nc.scalar.activation(yh[:, 6:8, :], PU, ACT.Copy).then_inc(pool_full.sem, 1)
                act.wait_ge(rec_full.sem, rec_full.nth(l, 1))
                nc.scalar.activation(yh[:, 2:6, :], Q.rearrange("p (k n) -> p k n", n=TOK), ACT.Copy)\
                    .then_inc(rec_hi.sem, 1)
                for c in range(A_WOUT, A_CQ):
                    high(l, c + 2)

            def cross_attention(l):
                for n in range(4):
                    high(l, A_CQ + n + 2)
                    chunk_wait(act, l, A_CQ + n)
                    nc.scalar.activation(CQT[:, 2 * n:2 * n + 2, :], ps[:, n, :].rearrange("p (k n) -> p k n", k=2),
                                         ACT.Copy).then_inc(evacuated.sem, 1)
                high(l, A_CV2 + 2)
                act.wait_ge(residual_ready.sem, residual_ready.nth(l, 4))
                for t in range(TT):
                    act.wait_ge(max_ready.sem, max_ready.nth(l, t + 1))
                    for h in range(CA_HEADS):
                        g = t * CA_HEADS + h
                        last = nc.scalar.activation(PROB[:, g, :], ps[:, 4 + g // 2, (g % 2) * 256:(g % 2 + 1) * 256],
                                                    ACT.Exp, scale=CA_SCALE, bias=nmx[:, g:g + 1],
                                                    accum_out=rsum[:, g:g + 1])
                    last.then_inc(prob_ready.sem, 1)
                for n in range(2):
                    if n:
                        high(l, A_CV2 + n + 2)
                    chunk_wait(act, l, A_CV2 + n)
                    nc.scalar.activation(CVM[1][:, :, n * 256:(n + 1) * 256], ps[:, n, :].rearrange("p (t n) -> p t n", t=2),
                                         ACT.Copy).then_inc(evacuated.sem, 1)
                for b in range(2):
                    act.wait_ge(prob_turned.sem, prob_turned.nth(l, b + 1))
                    nc.scalar.activation(PROBT[:, 2 * b:2 * b + 2, :], ps[:, 4 + b, :].rearrange("p (g n) -> p g n", g=2),
                                         ACT.Copy).then_inc(probt_act.sem, 1)
                for b in range(4):
                    act.wait_ge(attn_ready.sem, attn_ready.nth(l, b + 1))
                    nc.scalar.activation(yh[:, 2 * b:2 * b + 2, :], ps[:, b, :].rearrange("p (k n) -> p k n", k=2),
                                         ACT.Copy).then_inc(attn_hi.sem, 1)
                for n in range(4):
                    high(l, A_CO + n + 2)

            widen(0, -4, None)
            for c in range(AHEAD):
                high(0, c)
            for b in range(4):
                act.wait_ge(mem_turned.sem, b + 1)
                nc.scalar.activation(memf[:, 2 * b:2 * b + 2, :], ps[:, 4 + b, :].rearrange("p (k n) -> p k n", k=2), ACT.Copy)\
                    .then_inc(mem_full.sem, 1)
            act.wait_ge(bounds_max.sem, 1)
            nc.scalar.activation(lbw[:, 3:5, :], lbw[:, 1:3, :], ACT.Exp).then_inc(bounds_exp.sem, 1)
            with act.Fori(0, DEPTH) as l:
                order.layer(l)
                ffn(l, A_FFN1, 0)
                widen(l, 0, 0)
                mixer(l)
                widen(l, 4, 1)
                cross_attention(l)
                widen(l, 8, 2)
                ffn(l, A_FFN2, 1)
                widen(l, 12, 3)

            order.next_decoder(act_order_b)

            def squares(l, j):
                for t in range(TT):
                    act.wait_ge(b_res_ready.sem, b_res_ready.nth(l, 4 * j - 2 + 2 * t if j == 0 else 2 * t + 2))
                    if t:
                        order.settle()
                    order.put(nc.scalar.activation(junk, res[:, t, :], ACT.Square, accum_out=mv[:, t, 0:1]))
                    order.settle()
                    nc.scalar.activation(mv[:, t, 1:2], mv[:, t, 0:1], ACT.Copy).then_inc(b_squares.sem, 1)

            def rms_widen(l, j):
                for b in range(4):
                    act.wait_ge(b_turned.sem, b_turned.nth(l, 4 * j + b + 1))
                    for k in (2 * b, 2 * b + 1):
                        last = nc.scalar.activation(xf2[:, k, :], ps[:, b, (k % 2) * TOK:(k % 2 + 1) * TOK], ACT.Identity,
                                                    scale=parb[:, 8 * j + k:8 * j + k + 1])
                    last.then_inc(b_x_full.sem, 1)

            def qk_rstd(l, r):
                z0, z1, bank, _, _ = ROUNDS[r]
                out = RZ[:, z0 * TOK:z1 * TOK]
                act.wait_ge(b_summed.sem, b_summed.nth(l, r + 1))
                src = ps[:, bank:bank + 2, :].rearrange("p b n -> p (b n)")[:, 0:(z1 - z0) * TOK]
                order.put(nc.scalar.activation(out, src, ACT.Ln, bias=eps[:]))
                order.settle()
                nc.scalar.activation(out, out, ACT.Exp, scale=-0.5).then_inc(b_qk_rstd.sem, 1)

            def exponentials(l, g):
                scale = (32 if g < 2 else 64) ** -0.5
                act.wait_ge(b_max.sem, b_max.nth(l, g + 1))
                if g >= 2:
                    act.wait_ge(b_prob_turned.sem, b_prob_turned.nth(l, g - 1))
                for j in range(4):
                    nc.scalar.activation(PR[g % 2][:, j * P:(j + 1) * P], ps[:, 2, j * P:(j + 1) * P], ACT.Exp, scale=scale,
                                         bias=nmx[:, j:j + 1], accum_out=rsum[:, j:j + 1])
                for j in range(4):
                    last = nc.scalar.activation(PR[g % 2][:, 512 + j * 256:768 + j * 256],
                                                ps[:, 3 + j // 2, (j % 2) * 256:(j % 2 + 1) * 256], ACT.Exp, scale=scale,
                                                bias=nmx[:, 4 + j:5 + j], accum_out=rsum[:, 4 + j:5 + j])
                if g >= 3:
                    last = nc.scalar.activation(sinkx[:], sinkx[:], ACT.Exp)
                last.then_inc(b_prob.sem, 1)

            def attention(l):
                for c in range(B_GATE + 12):
                    high(l, c + 2, 0, B)
                    chunk_wait(act, l, c, 0, B)
                    bank = ps[:, c % 2, :]
                    if c == B_VA or c == B_VC:
                        nc.scalar.activation(VA if c == B_VA else VC, bank.rearrange("p (t n) -> p t n", t=TT), ACT.Copy)\
                            .then_inc(b_evacuated.sem, 1)
                    elif c >= B_GATE:
                        nc.scalar.activation(GATE[:, c - B_GATE, :], bank, ACT.Copy).then_inc(b_evacuated.sem, 1)
                    else:
                        w = TOK if c == B_KVB else 512
                        cols = slice(c * 512, c * 512 + w)
                        nc.scalar.activation(Z[:, cols], bank[:, 0:w], ACT.Copy)
                        if c == B_KVB:
                            nc.scalar.activation(VBF, bank[:, TOK:], ACT.Copy)
                        nc.scalar.activation(RZ[:, cols], bank[:, 0:w], ACT.Square).then_inc(b_evacuated.sem, 1)
                    if c == 1:
                        act.wait_ge(b_lam_sums.sem, b_lam_sums.nth(l, 1))
                        nc.scalar.activation(lams[:, 2:4], lams[:, 0:2], ACT.Exp).then_inc(b_lam_exp.sem, 1)
                    if c in (3, 5, 7, 9):
                        qk_rstd(l, (c - 3) // 2)
                    if c == 9:
                        act.wait_ge(b_values_turned.sem, b_values_turned.nth(l, 1))
                        nc.scalar.activation(VB, ps[:, 3, 0:TOK].rearrange("p (t n) -> p t n", t=TT), ACT.Copy)
                    g = c - (B_GATE + 4)
                    if 2 <= g < GROUPS + 2:
                        act.wait_ge(b_pv.sem, b_pv.nth(l, g - 1))
                        if g - 2 < 2:
                            nc.scalar.activation(OC[:, (g - 2) * TOK:(g - 1) * TOK], ps[:, 5, 0:TOK], ACT.Copy).then_inc(b_o_out.sem, 1)
                        else:
                            if g - 2 > 2:
                                act.wait_ge(b_y_ready.sem, b_y_ready.nth(l, g - 4))
                            nc.scalar.activation(OB[:], ps[:, 5, :], ACT.Copy).then_inc(b_o_out.sem, 1)
                    if g == 3:
                        act.wait_ge(b_o_out.sem, b_o_out.nth(l, 2))
                        nc.scalar.activation(CSQ, OC, ACT.Square).then_inc(b_c_squared.sem, 1)
                    if 1 <= g < GROUPS + 1:
                        act.wait_ge(b_prob_turned.sem, b_prob_turned.nth(l, g))
                        if g >= 2:
                            act.wait_ge(b_pv.sem, b_pv.nth(l, g - 1))
                        n = 512 if g - 1 < 2 else 1024
                        nc.scalar.activation(PT[:, 0:n], ps[:, 5:7, :].rearrange("p b n -> p (b n)")[:, 0:n], ACT.Copy)\
                            .then_inc(b_pt_act.sem, 1)
                    if 0 <= g < GROUPS:
                        exponentials(l, g)
                    if g == GROUPS + 1:
                        act.wait_ge(b_c_summed.sem, b_c_summed.nth(l, 1))
                        order.put(nc.scalar.activation(CRS, ps[:, 2, :], ACT.Ln, bias=eps[:]))
                        order.settle()
                        nc.scalar.activation(CRS, CRS, ACT.Exp, scale=-0.5).then_inc(b_c_rstd.sem, 1)
                act.wait_ge(b_evacuated.sem, b_evacuated.nth(l, 21))
                for n, c in ((2, B_WC), (0, B_WA), (1, B_WB)):
                    gates = flat[:, n * 2048:(n + 1) * 2048]
                    nc.scalar.activation(gates, gates, ACT.Sigmoid).then_inc(b_gates_open.sem, 1)
                    high(l, c + 2, 0, B)
                for c in range(B_WB + 1, B_FFN):
                    high(l, c + 2, 0, B)

            def conv_ffn(l):
                def step(i, more):
                    b, c = i % 2, B_FFN + 2 + 3 * (i - 1)
                    if i == 0:
                        c = B_FFN
                    n = i + more
                    high(l, c + 2, more, B)
                    if i >= 2:
                        act.wait_ge(b_hidden_split.sem, b_hidden_split.nth(l, n - 1))
                    chunk_wait(act, l, c, more, B)
                    for ft in range(2):
                        tile = 2 * n + ft
                        last = nc.scalar.activation(cvg[:, b, ft * TOK:(ft + 1) * TOK], ps[:, 2 * b, ft * TOK:(ft + 1) * TOK],
                                                    ACT.Identity, scale=conv_w2(2, tile), bias=conv_b2(tile))
                    last.then_inc(b_gate_scaled.sem, 1)
                    high(l, c + 3, more, B)
                    chunk_wait(act, l, c + 1, more, B)
                    for ft in range(2):
                        tile = 2 * n + 22 + ft
                        last = nc.scalar.activation(cvv[:, b, ft * TOK:(ft + 1) * TOK], ps[:, 2 * b + 1, ft * TOK:(ft + 1) * TOK],
                                                    ACT.Identity, scale=conv_w2(2, tile), bias=conv_b2(tile))
                    last.then_inc(b_value_scaled.sem, 1)
                    act.wait_ge(b_gate_conv.sem, b_gate_conv.nth(l, n + 1))
                    nc.scalar.activation(cvg[:, b, :], cvg[:, b, :], ACT.Silu).then_inc(gate_ready.sem, 1)
                    if i:
                        high(l, c + 4, more, B)
                    act.wait_ge(b_hidden_ready.sem, b_hidden_ready.nth(l, n + 1))
                    nc.scalar.activation(yh[:, 2 * b:2 * b + 2, :], cvv[:, b, :].rearrange("p (k n) -> p k n", k=2),
                                         ACT.Copy).then_inc(hidden_hi.sem, 1)

                for i in range(3):
                    step(i, 0)
                with act.Fori(0, (STEPS - 5) // 2) as r:
                    for i in (3, 4):
                        step(i, 2 * r)
                for i in (STEPS - 2, STEPS - 1):
                    step(i, 0)

            with act.Fori(0, DEPTH) as l:
                order.layer(l)
                act.wait_ge(b_res_ready.sem, b_res_ready.nth(l, -2))
                act.dma_start(parb[:], dram["par_b"][bass.ds(l, 1), :, :].rearrange("l p n -> (l p) n")).then_inc(b_params_in.sem, 16)
                act.dma_start(rowb[:], dram["row_b"][bass.ds(l, 1), :].rearrange("l n -> (l n)").partition_broadcast(P))\
                    .then_inc(b_params_in.sem, 16)
                squares(l, 0)
                high(l, 0, 0, B)
                high(l, 1, 0, B)
                act.wait_ge(b_params_in.sem, b_params_in.nth(l, 32))
                rms_widen(l, 0)
                attention(l)
                squares(l, 1)
                rms_widen(l, 1)
                conv_ffn(l)
            order.close()

        @block.vector
        def _(dve):
            order = Order(dve, dve_order)

            def hold():
                order.settle()
                order.put(nc.vector.tensor_copy(held[:, 0:1], eps[:]))

            def low(l, c, more=0, ring=A):
                if ring is B and isinstance(more, int) and c + 3 * more >= ring.chunks:
                    return
                s, u = chunk(c, more, ring)
                dve.wait_ge(ring.hi[s].sem, ring.hi[s].nth(l, u + 1))
                nc.vector.tensor_tensor(wlo[:, s, :], raw[:, s, :], whi[:, s, :].bitcast(F32), ALU.subtract)\
                    .then_inc(split_ready[s].sem, 1)

            def ffn(l, c0, f):
                def step(i, more):
                    b, c = i % 2, c0 + 2 + 3 * (i - 1)
                    if i == 0:
                        c = c0
                    n = f * STEPS + i + more
                    low(l, c + 2, more)
                    low(l, c + 3, more)
                    dve.wait_ge(gate_ready.sem, gate_ready.nth(l, n + 1))
                    chunk_wait(dve, l, c + 1, more)
                    nc.vector.scalar_tensor_tensor(hg[:, b, :], sg[:, b, :], 0.5, ps[:, 2 * b + 1, :], ALU.mult, ALU.mult)\
                        .then_inc(hidden_ready.sem, 1)
                    if i and c + 4 < A_CHUNKS:
                        low(l, c + 4, more)
                    dve.wait_ge(hidden_hi.sem, hidden_hi.nth(l, n + 1))
                    nc.vector.tensor_tensor(yl[:, 2 * b:2 * b + 2, :], hg[:, b, :].rearrange("p (k n) -> p k n", k=2),
                                            yh[:, 2 * b:2 * b + 2, :].bitcast(F32), ALU.subtract)\
                        .then_inc(hidden_split.sem, 1)

                for i in range(3):
                    step(i, 0)
                with dve.Fori(0, (STEPS - 5) // 2) as r:
                    for i in (3, 4):
                        step(i, 2 * r)
                for i in (STEPS - 2, STEPS - 1):
                    step(i, 0)

            def split_stream(l, n, hi, lo, src=xf, full=x_full, ready=x_ready):
                for b in range(4):
                    tiles = slice(2 * b, 2 * b + 2)
                    dve.wait_ge(full.sem, full.nth(l, n + b + 1))
                    order.put(nc.vector.tensor_copy(hi[:, tiles, :], src[:, tiles, :]))
                    order.settle()
                    nc.vector.tensor_tensor(lo[:, tiles, :], src[:, tiles, :], hi[:, tiles, :].bitcast(F32), ALU.subtract)\
                        .then_inc(ready.sem, 1)

            def norm(l, j, c, spare):
                def add(t, half):
                    b, cols = 2 * t + half, slice(half * 512, (half + 1) * 512)
                    if b < 3:
                        dve.wait_ge(acc_ready.sem, acc_ready.nth(l, 3 * j + b + 1))
                    else:
                        chunk_wait(dve, l, c)
                    order.put(nc.vector.scalar_tensor_tensor(ybuf[:, t, cols], res[:, t, cols], ALPHA, ps[:, 4 + b, :],
                                                             ALU.mult, ALU.add))
                    order.settle()
                    order.put(nc.vector.bn_stats(stat[:, t, half, :], ybuf[:, t, cols]))

                def variance(t):
                    hold()
                    order.put(nc.vector.bn_aggr(mv[:, t, :], stat[:, t, :, :].rearrange("p a b -> p (a b)")))
                    order.settle()
                    nc.vector.tensor_scalar_add(vare[:, t:t + 1], mv[:, t, 1:2], LN_EPS).then_inc(var_ready.sem, 1)

                def scaled(t):
                    dve.wait_ge(rstd_ready.sem, rstd_ready.nth(l, 2 * j + t + 1))
                    nc.vector.tensor_scalar(ybuf[:, t, :], ybuf[:, t, :], mv[:, t, 0:1], rstd[:, t:t + 1],
                                            ALU.subtract, ALU.mult).then_inc(normed.sem, 1)

                if j == 0:
                    dve.wait_ge(params_in.sem, params_in.nth(l, 48))
                dve.wait_ge(residual_ready.sem, residual_ready.nth(l, 2 * j))
                add(0, 0)
                add(0, 1)
                variance(0)
                add(1, 0)
                add(1, 1)
                variance(1)
                scaled(0)
                scaled(1)
                low(l, spare)
                split_stream(l, 4 * j, xh, xl)

            def mixer(l):
                def spread(buf, side, h):
                    return buf.rearrange("p (n s h) -> p n s h", s=2, h=h)[:, :, side, :]

                def decayed(n):
                    if n == 1:
                        dve.wait_ge(residual_ready.sem, residual_ready.nth(l, 2))
                        dve.wait_ge(evacuated.sem, evacuated.nth(l, 4))
                    if n >= 2:
                        dve.wait_ge(level_scored.sem, level_scored.nth(l, n - 1))
                    dve.wait_ge(decay_exp.sem, decay_exp.nth(l, n))
                    h = P if n == 1 else LEVELS[::-1][n - 2]
                    order.put(nc.vector.tensor_tensor(spread(qlev[n % 2], 1, h), spread(Q, 1, h), spread(EXPD, 1, h), ALU.mult))
                    order.settle()
                    nc.vector.tensor_tensor(spread(klev[n % 2], 0, h), spread(KEY, 0, h), spread(EXPD, 0, h), ALU.mult)\
                        .then_inc(level_ready.sem, 1)

                def merge(n):
                    dve.wait_ge(level_scored.sem, level_scored.nth(l, n + 1))
                    m = 0 if n == 0 else 9 - n
                    b = 4 + 2 * (n % 2)
                    if n:
                        dve.wait_ge(level_merged.sem, level_merged.nth(l, n - 1))
                    hold()
                    nc.vector.copy_predicated(
                        AT, lvl_mask[:, m:m + 1, :].broadcast_to([P, HEADS * TT, P]),
                        ps[:, b:b + 2, :].rearrange("p b (g t) -> p (b g) t", t=P)).then_inc(level_merged.sem, 1)

                for c in range(A_RF, A_WOUT):
                    if c <= A_CV:
                        low(l, c + 2)
                    if c == A_RF + 1:
                        dve.wait_ge(evacuated.sem, evacuated.nth(l, 2))
                        order.put(nc.vector.tensor_scalar_max(SIG, SIG, F_FLOOR))
                        order.settle()
                        order.put(nc.vector.tensor_copy(lbc[:], lbt[:, bass.ds(l, 1), :, :].rearrange("p l a h -> p (l a) h")))
                        order.settle()
                        for h in range(HEADS):
                            s = slice(h * TOK, (h + 1) * TOK)
                            last = nc.vector.tensor_scalar(KEY[:, s], SIG[:, s], lbc[:, 2, h:h + 1], lbc[:, 1, h:h + 1],
                                                           ALU.mult, ALU.add)
                            if h == 0:
                                last.then_inc(floored.sem, 1)
                        last.then_inc(keys_ready.sem, 1)
                    if c == A_RQ:
                        dve.wait_ge(logs_ready.sem, logs_ready.nth(l, 1))
                        dve.wait_ge(keys_ready.sem, keys_ready.nth(l, 1))
                        for g in range(HEADS * TT):
                            s = slice(g * P, (g + 1) * P)
                            last = nc.vector.tensor_tensor_scan(SIG[:, s], ones, LOGF[:, s], 0.0, ALU.mult, ALU.add)
                        last.then_inc(decay_ready.sem, 1)
                    if c == A_CK0:
                        decayed(1)
                    if A_RI < c < A_RI + 8:
                        decayed(c - A_RI + 1)
                    if c == A_RI + 1:
                        merge(0)
                    if A_RI + 3 <= c < A_RI + 10:
                        merge(c - A_RI - 1)
                    if c == A_CB:
                        dve.wait_ge(gate_exp.sem, gate_exp.nth(l, 1))
                        order.put(nc.vector.tensor_scalar_add(RG, RG, 1.0))
                        order.settle()
                        order.put(nc.vector.reciprocal(RG, RG))
                dve.wait_ge(o_rstd.sem, o_rstd.nth(l, 1))
                order.settle()
                for h in range(HEADS):
                    s = slice(h * TOK, (h + 1) * TOK)
                    last = nc.vector.scalar_tensor_tensor(Q[:, s], ps[:, 4 + h // 2, (h % 2) * TOK:(h % 2 + 1) * TOK],
                                                          norm_g(h), LOGF[:, s], ALU.mult, ALU.mult)
                    if h < HEADS - 1:
                        order.put(last)
                last.then_inc(rec_read.sem, 1)
                order.settle()
                dve.wait_ge(rec_read.sem, rec_read.nth(l, 1))
                nc.vector.tensor_tensor(Q, Q, RG, ALU.mult).then_inc(rec_full.sem, 1)
                low(l, A_WOUT + 1)
                dve.wait_ge(pool_full.sem, pool_full.nth(l, 1))
                nc.vector.tensor_tensor(yl[:, 6:8, :], PU, yh[:, 6:8, :].bitcast(F32), ALU.subtract).then_inc(pool_ready.sem, 1)
                dve.wait_ge(rec_hi.sem, rec_hi.nth(l, 1))
                nc.vector.tensor_tensor(yl[:, 2:6, :], Q.rearrange("p (k n) -> p k n", n=TOK), yh[:, 2:6, :].bitcast(F32),
                                        ALU.subtract).then_inc(rec_ready.sem, 1)
                for c in range(A_WOUT, A_CQ - 1):
                    low(l, c + 2)

            def cross_attention(l):
                for n in range(4):
                    low(l, A_CQ + n + 2)
                low(l, A_CV2 + 2)
                for t in range(TT):
                    g = slice(t * CA_HEADS, (t + 1) * CA_HEADS)
                    dve.wait_ge(scored.sem, scored.nth(l, t + 1))
                    order.put(nc.vector.tensor_reduce(
                        mx[:, g], ps[:, 4 + 2 * t:6 + 2 * t, :].rearrange("p b (h n) -> p (b h) n", n=256), AX.X, ALU.max))
                    order.settle()
                    nc.vector.tensor_scalar_mul(nmx[:, g], mx[:, g], -CA_SCALE).then_inc(max_ready.sem, 1)
                for t in range(TT):
                    g = slice(t * CA_HEADS, (t + 1) * CA_HEADS)
                    dve.wait_ge(prob_ready.sem, prob_ready.nth(l, t + 1))
                    order.put(nc.vector.reciprocal(rinv[:, g], rsum[:, g]))
                    order.settle()
                    nc.vector.tensor_tensor(PROB[:, g, :], PROB[:, g, :], rinv[:, g].unsqueeze(2).broadcast_to([P, CA_HEADS, 256]),
                                            ALU.mult).then_inc(prob_normed.sem, 1)
                low(l, A_CV2 + 3)
                for b in range(2, 4):
                    dve.wait_ge(prob_turned.sem, prob_turned.nth(l, b + 1))
                    nc.vector.tensor_copy(PROBT[:, 2 * b:2 * b + 2, :], ps[:, 4 + b, :].rearrange("p (g n) -> p g n", g=2))\
                        .then_inc(probt_dve.sem, 1)
                for b in range(4):
                    dve.wait_ge(attn_hi.sem, attn_hi.nth(l, b + 1))
                    nc.vector.tensor_tensor(yl[:, 2 * b:2 * b + 2, :], ps[:, b, :].rearrange("p (k n) -> p k n", k=2),
                                            yh[:, 2 * b:2 * b + 2, :].bitcast(F32), ALU.subtract).then_inc(attn_split.sem, 1)
                for n in range(3):
                    low(l, A_CO + n + 2)

            def bounds():
                m, e = lbw[:, 0, :], lbw[:, 3:5, :]
                order.put(nc.vector.tensor_tensor(m, rlb[:, 0, :], rlb[:, 1, :], ALU.max))
                order.settle()
                order.put(nc.vector.tensor_tensor(lbw[:, 1, :], rlb[:, 0, :], m, ALU.subtract))
                nc.vector.tensor_tensor(lbw[:, 2, :], rlb[:, 1, :], m, ALU.subtract).then_inc(bounds_max.sem, 1)
                order.settle()
                dve.wait_ge(bounds_exp.sem, 1)
                order.put(nc.vector.tensor_tensor(m, lbw[:, 3, :], lbw[:, 4, :], ALU.add))
                order.settle()
                order.put(nc.vector.reciprocal(lbw[:, 5, :], m))
                order.settle()
                for i in range(2):
                    order.put(nc.vector.tensor_tensor(lbw[:, 1 + i, :], lbw[:, 3 + i, :], lbw[:, 5, :], ALU.mult))
                order.settle()
                order.put(nc.vector.tensor_tensor(lbw[:, 3, :], lbw[:, 1, :], lbw[:, 2, :], ALU.add))
                order.put(nc.vector.tensor_tensor(lbt[:, 0, 0, :], lbw[:, 1, :], lbw[:, 1, :], ALU.subtract))
                order.settle()
                order.put(nc.vector.tensor_tensor(lbt[:, 1, 0, :], lbw[:, 3, :], lbw[:, 1, :], ALU.subtract))
                order.settle()
                order.put(nc.vector.tensor_scalar(lbt[:, :, 1, :], lbt[:, :, 0, :], -1.0, 1.0, ALU.mult, ALU.add))
                order.put(nc.vector.tensor_scalar_add(lbt[:, :, 2, :], lbt[:, :, 0, :], -1.0))
                order.settle()

            for s in range(SLOTS):
                dve.sem_inc(split_ready[s].sem, 1)
            order.put(nc.vector.memset(eps[:], RMS_EPS))
            dve.wait_ge(inputs_in.sem, 32)
            split_stream(0, -4, xh, xl)
            for c in range(AHEAD):
                low(0, c)
            dve.wait_ge(setup_in.sem, 32)
            order.put(nc.vector.tensor_copy(lvl_mask[:], units(11).rearrange("p (v t) -> p v t", t=P)))
            bounds()
            split_stream(0, 0, mh, ml, memf, mem_full, mem_ready)
            dve.wait_ge(mem_in.sem, 16)
            dve.wait_ge(mem_turned.sem, 4)
            order.put(nc.vector.memset(AT, 0.0))
            order.settle()
            order.close()
            with dve.Fori(0, DEPTH) as l:
                order.layer(l)
                ffn(l, A_FFN1, 0)
                norm(l, 0, A_RF - 1, A_RF + 1)
                mixer(l)
                norm(l, 1, A_CQ - 1, A_CQ + 1)
                cross_attention(l)
                norm(l, 2, A_FFN2 - 1, A_FFN2 + 1)
                ffn(l, A_FFN2, 1)
                norm(l, 3, A_CHUNKS - 1, A_CHUNKS)
                low(l, A_CHUNKS + 1)

            order.next_decoder(dve_order_b)

            def add_to_stream(l, j, c):
                for b in range(4):
                    t, cols = b // 2, slice(b % 2 * 512, (b % 2 + 1) * 512)
                    if b < 3:
                        dve.wait_ge(b_acc_ready.sem, b_acc_ready.nth(l, 3 * j + b + 1))
                    else:
                        chunk_wait(dve, l, c, 0, B)
                    nc.vector.tensor_tensor(res[:, t, cols], res[:, t, cols], ps[:, 4 + b, :], ALU.add).then_inc(b_res_ready.sem, 1)

            def rms(l, j, spare):
                for t in range(TT):
                    dve.wait_ge(b_squares.sem, b_squares.nth(l, 2 * j + t + 1))
                    nc.vector.tensor_scalar(vare[:, t:t + 1], mv[:, t, 1:2], 1.0 / D, QK_EPS, ALU.mult, ALU.add)\
                        .then_inc(var_ready.sem, 1)
                    dve.wait_ge(b_rstd_ready.sem, b_rstd_ready.nth(l, 2 * j + t + 1))
                    nc.vector.tensor_scalar(nbuf[:, t, :], res[:, t, :], rstd[:, t:t + 1], None, ALU.mult)\
                        .then_inc(normed.sem, 1)
                low(l, spare, 0, B)
                for b in range(4):
                    tiles = slice(2 * b, 2 * b + 2)
                    dve.wait_ge(b_x_full.sem, b_x_full.nth(l, 4 * j + b + 1))
                    order.put(nc.vector.tensor_copy(xh[:, tiles, :], xf2[:, tiles, :]))
                    order.settle()
                    nc.vector.tensor_tensor(xl[:, tiles, :], xf2[:, tiles, :], xh[:, tiles, :].bitcast(F32), ALU.subtract)\
                        .then_inc(x_ready.sem, 1)

            def lambdas(l):
                v = rowb[:, 0:128].rearrange("p (a b n) -> p a b n", a=2, b=2)
                order.put(nc.vector.tensor_tensor(lamw[:], v[:, :, 0, :], v[:, :, 1, :], ALU.mult))
                order.settle()
                nc.vector.tensor_reduce(lams[:, 0:2], lamw[:], AX.X, ALU.add).then_inc(b_lam_sums.sem, 1)
                order.put(nc.vector.tensor_tensor(subg[:], parb[:, 22:23], parb[:, 24:25], ALU.mult))
                dve.wait_ge(b_lam_exp.sem, b_lam_exp.nth(l, 1))
                order.put(nc.vector.tensor_tensor(nlam[:], lams[:, 3:4], lams[:, 2:3], ALU.subtract))
                order.settle()
                order.put(nc.vector.tensor_tensor(nlam[:], nlam[:], parb[:, 23:24], ALU.subtract))

            def qk_norm(l, r):
                z0, z1, bank, _, gains = ROUNDS[r]
                dve.wait_ge(b_qk_rstd.sem, b_qk_rstd.nth(l, r + 1))
                for a, b, col in gains:
                    cols = slice(a * TOK, b * TOK)
                    last = nc.vector.scalar_tensor_tensor(Z[:, cols], Z[:, cols], parb[:, col:col + 1], RZ[:, cols],
                                                          ALU.mult, ALU.mult)
                last.then_inc(b_qk_normed.sem, 1)

            def sine(l, r):
                z0, z1, bank, dim, _ = ROUNDS[r]
                n = z1 - z0
                dve.wait_ge(b_rotated.sem, b_rotated.nth(l, r + 1))
                src = ps[:, bank:bank + 2, :].rearrange("p b n -> p (b n)")[:, 0:n * TOK].rearrange("p (z t) -> p z t", t=TOK)
                out = RZ[:, z0 * TOK:z1 * TOK].rearrange("p (z t) -> p z t", t=TOK)
                nc.vector.tensor_tensor(out, src, rope[dim][1].unsqueeze(1).broadcast_to([P, n, TOK]), ALU.mult)\
                    .then_inc(b_sine.sem, 1)

            def maxima(l, g):
                scale = (32 if g < 2 else 64) ** -0.5
                dve.wait_ge(b_scored.sem, b_scored.nth(l, g + 1))
                order.put(nc.vector.tensor_reduce(mx[:, 0:4], ps[:, 2, :].rearrange("p (j n) -> p j n", n=P), AX.X, ALU.max))
                order.put(nc.vector.tensor_reduce(mx[:, 4:8], ps[:, 3:5, :].rearrange("p b (j n) -> p (b j) n", n=256), AX.X, ALU.max))
                order.settle()
                if g < 3:
                    nc.vector.tensor_scalar_mul(nmx[:], mx[:], -scale).then_inc(b_max.sem, 1)
                    return
                sink = rowb[:, 128 + 4 * (g - 3):132 + 4 * (g - 3)]
                for t in range(TT):
                    order.put(nc.vector.scalar_tensor_tensor(mx[:, 4 * t:4 * t + 4], mx[:, 4 * t:4 * t + 4], scale, sink,
                                                             ALU.mult, ALU.max))
                order.settle()
                order.put(nc.vector.tensor_scalar_mul(nmx[:], mx[:], -1.0))
                order.settle()
                for t in range(TT):
                    last = nc.vector.tensor_tensor(sinkx[:, 4 * t:4 * t + 4], nmx[:, 4 * t:4 * t + 4], sink, ALU.add)
                    if t == 0:
                        order.put(last)
                last.then_inc(b_max.sem, 1)

            def normalise(l, g):
                dve.wait_ge(b_prob.sem, b_prob.nth(l, g + 1))
                if g >= 3:
                    order.put(nc.vector.tensor_tensor(rsum[:], rsum[:], sinkx[:], ALU.add))
                    order.settle()
                order.put(nc.vector.reciprocal(rinv[:], rsum[:]))
                order.settle()
                first = PR[g % 2][:, 0:512].rearrange("p (j n) -> p j n", n=P)
                second = PR[g % 2][:, 512:1536].rearrange("p (j n) -> p j n", n=256)
                if g >= 2:
                    nc.vector.tensor_tensor(first, first, rinv[:, 0:4].unsqueeze(2).broadcast_to([P, 4, P]), ALU.mult)
                    nc.vector.tensor_tensor(second, second, rinv[:, 4:8].unsqueeze(2).broadcast_to([P, 4, 256]), ALU.mult)\
                        .then_inc(b_prob_normed.sem, 1)
                    return
                order.put(nc.vector.tensor_scalar(rlam[:], rinv[:], nlam[:], None, ALU.mult))
                for t, part in enumerate((first, second)):
                    for h in range(2):
                        order.put(nc.vector.tensor_scalar(part[:, 2 * h, :], part[:, 2 * h, :],
                                                          rinv[:, 4 * t + 2 * h:4 * t + 2 * h + 1], None, ALU.mult))
                order.settle()
                for t, part in enumerate((first, second)):
                    for h in range(2):
                        j = 4 * t + 2 * h + 1
                        last = nc.vector.scalar_tensor_tensor(part[:, 2 * h, :], part[:, 2 * h + 1, :], rlam[:, j:j + 1],
                                                              part[:, 2 * h, :], ALU.mult, ALU.add)
                last.then_inc(b_prob_normed.sem, 1)

            def split_y(src, y0, done):
                order.put(nc.vector.tensor_copy(yh[:, y0:y0 + 2, :], src.rearrange("p (k n) -> p k n", n=TOK)))
                order.settle()
                nc.vector.tensor_tensor(yl[:, y0:y0 + 2, :], src.rearrange("p (k n) -> p k n", n=TOK),
                                        yh[:, y0:y0 + 2, :].bitcast(F32), ALU.subtract).then_inc(done.sem, 1)

            def attention(l):
                for c in range(B_GATE + 12):
                    low(l, c + 2, 0, B)
                    if c == 1:
                        lambdas(l)
                    if c == 2:
                        dve.wait_ge(b_consts_in.sem, 16)
                        nc.vector.tensor_copy(maskb[:, 0, :], ident).then_inc(b_masks_set.sem, 1)
                        nc.vector.tensor_copy(maskb[:, 1:3, :], CONB[:, 1536:1792].rearrange("p (a n) -> p a n", a=2))\
                            .then_inc(b_masks_set.sem, 1)
                    if c in (4, 6, 8, 10):
                        qk_norm(l, c // 2 - 2)
                    if c in (6, 8, 10, 12):
                        sine(l, c // 2 - 3)
                    g = c - (B_GATE + 4)
                    if 0 <= g < GROUPS:
                        maxima(l, g)
                    if 4 <= g < GROUPS + 2:
                        dve.wait_ge(b_o_out.sem, b_o_out.nth(l, g - 1))
                        split_y(OB[:], 2 * (g - 4), b_y_ready)
                    if 1 <= g < GROUPS + 1:
                        dve.wait_ge(b_prob_turned.sem, b_prob_turned.nth(l, g))
                        if g >= 2:
                            dve.wait_ge(b_pv.sem, b_pv.nth(l, g - 1))
                        n = 256 if g - 1 < 2 else 512
                        nc.vector.tensor_copy(PT[:, 1024:1024 + n], ps[:, 7, 0:n]).then_inc(b_pt_dve.sem, 1)
                    if 0 <= g < GROUPS:
                        normalise(l, g)
                    if g == GROUPS + 1:
                        dve.wait_ge(b_c_rstd.sem, b_c_rstd.nth(l, 1))
                        order.put(nc.vector.scalar_tensor_tensor(OC, OC, subg[:], CRS, ALU.mult, ALU.mult))
                        order.settle()
                        split_y(OC, 6, b_yc_ready)
                for n, (chunks, gate0, bank0) in enumerate((([B_WC], 8, 0), ([B_WA], 0, 4), ([B_WB, B_WB + 1], 4, 0))):
                    low(l, chunks[0] + 2, 0, B)
                    dve.wait_ge(b_gates_open.sem, b_gates_open.nth(l, n + 1))
                    for b in range(4):
                        dve.wait_ge(b_branch_done.sem, b_branch_done.nth(l, 4 * n + b + 1))
                        nc.vector.tensor_tensor(GATE[:, gate0 + b, :], GATE[:, gate0 + b, :], ps[:, branch_bank(bank0, b), :], ALU.mult)\
                            .then_inc(b_gated.sem, 1)
                        if n < 2:
                            continue
                        dve.wait_ge(b_gated.sem, b_gated.nth(l, 8 + b + 1))
                        dve.wait_ge(b_pair_merged.sem, b_pair_merged.nth(l, b + 1))
                        order.put(nc.vector.tensor_tensor(GATE[:, 8 + b, :], GATE[:, 8 + b, :], GATE[:, 4 + b, :], ALU.add))
                        order.settle()
                        m = GATE[:, 8 + b, :].rearrange("p (k n) -> p k n", n=TOK)
                        tiles = slice(2 * b, 2 * b + 2)
                        order.put(nc.vector.tensor_copy(xh[:, tiles, :], m))
                        order.settle()
                        nc.vector.tensor_tensor(xl[:, tiles, :], m, xh[:, tiles, :].bitcast(F32), ALU.subtract)\
                            .then_inc(b_merge_ready.sem, 1)
                for c in range(B_WB + 1, B_FFN - 1):
                    low(l, c + 2, 0, B)

            def conv_ffn(l):
                def taps(buf, bank, b, tile, done):
                    for lag in (1, 2):
                        for ft in range(2):
                            t0 = ft * TOK
                            out = buf[:, b, t0 + lag:t0 + TOK]
                            last = nc.vector.scalar_tensor_tensor(out, ps[:, bank, t0:t0 + TOK - lag], conv_w2(2 - lag, tile + ft), out,
                                                                  ALU.mult, ALU.add)
                            if not (lag == 2 and ft == 1):
                                last.then_inc(done[0].sem, 1)
                        if lag == 1:
                            dve.wait_ge(done[0].sem, done[1])
                    return last

                def step(i, more):
                    b, c = i % 2, B_FFN + 2 + 3 * (i - 1)
                    if i == 0:
                        c = B_FFN
                    n = i + more
                    low(l, c + 2, more, B)
                    dve.wait_ge(b_gate_scaled.sem, b_gate_scaled.nth(l, n + 1))
                    taps(cvg, 2 * b, b, 2 * n, (b_taps, b_taps.nth(l, 6 * n + 2))).then_inc(b_gate_conv.sem, 1)
                    low(l, c + 3, more, B)
                    dve.wait_ge(b_value_scaled.sem, b_value_scaled.nth(l, n + 1))
                    taps(cvv, 2 * b + 1, b, 2 * n + 22, (b_taps, b_taps.nth(l, 6 * n + 5))).then_inc(b_value_conv.sem, 1)
                    dve.wait_ge(gate_ready.sem, b_gate_ready.nth(l, n + 1))
                    dve.wait_ge(b_value_conv.sem, b_value_conv.nth(l, n + 1))
                    dve.wait_ge(b_taps.sem, b_taps.nth(l, 6 * n + 6))
                    nc.vector.tensor_tensor(cvv[:, b, :], cvv[:, b, :], cvg[:, b, :], ALU.mult).then_inc(hidden_ready.sem, 1)
                    if i:
                        low(l, c + 4, more, B)
                    dve.wait_ge(b_hidden_hi.sem, b_hidden_hi.nth(l, n + 1))
                    nc.vector.tensor_tensor(yl[:, 2 * b:2 * b + 2, :], cvv[:, b, :].rearrange("p (k n) -> p k n", k=2),
                                            yh[:, 2 * b:2 * b + 2, :].bitcast(F32), ALU.subtract).then_inc(hidden_split.sem, 1)

                for i in range(3):
                    step(i, 0)
                with dve.Fori(0, (STEPS - 5) // 2) as r:
                    for i in (3, 4):
                        step(i, 2 * r)
                for i in (STEPS - 2, STEPS - 1):
                    step(i, 0)

            dve.wait_ge(x_ready.sem, x_ready.nth(DEPTH, 0))
            dve.wait_ge(residual_ready.sem, residual_ready.nth(DEPTH, -1))
            dve.sem_inc(b_res_ready.sem, 2)
            dve.wait_ge(residual_ready.sem, residual_ready.nth(DEPTH, 0))
            dve.sem_inc(b_res_ready.sem, 2)
            with dve.Fori(0, DEPTH) as l:
                order.layer(l)
                rms(l, 0, 0)
                low(l, 1, 0, B)
                attention(l)
                add_to_stream(l, 0, B_FFN - 1)
                rms(l, 1, B_FFN + 1)
                conv_ffn(l)
                add_to_stream(l, 1, B_CHUNKS - 1)
            order.close()

        @block.gpsimd
        def _(pool):
            order = Order(pool, pool_order)

            def hold():
                order.settle()
                order.put(nc.gpsimd.tensor_tensor(held[:, 1:2], mhalf[:], mhalf[:], ALU.mult))

            def norm(l, j):
                pool.wait_ge(residual_ready.sem, residual_ready.nth(l, 2 * j))
                if j == 1:
                    pool.wait_ge(level_scored.sem, level_scored.nth(l, 9))
                for tab, name in ((tabg, "ln_g"), (tabb, "ln_b")):
                    pool.dma_start(tab, dram[name][bass.ds(l * 4 + j, 1), :].rearrange("a n -> (a n)").partition_broadcast(P))\
                        .then_inc(tables_in.sem, 16)
                for t in range(TT):
                    pool.wait_ge(var_ready.sem, var_ready.nth(l, 2 * j + t + 1))
                    nc.gpsimd.tensor_tensor(rstd[:, t:t + 1], vare[:, t:t + 1], mhalf[:], ALU.pow).then_inc(rstd_ready.sem, 1)
                pool.wait_ge(tables_in.sem, tables_in.nth(l, 32 * (j + 1)))
                for t in range(TT):
                    pool.wait_ge(normed.sem, normed.nth(l, 2 * j + t + 1))
                    order.put(nc.gpsimd.tensor_tensor(res[:, t, :], ybuf[:, t, :], tabg, ALU.mult))
                    order.settle()
                    nc.gpsimd.tensor_tensor(res[:, t, :], res[:, t, :], tabb, ALU.add).then_inc(residual_ready.sem, 1)

            def spreads(l):
                pool.wait_ge(decay_ready.sem, decay_ready.nth(l, 1))
                for n in range(1, 9):
                    if n >= 2:
                        pool.wait_ge(decay_exp.sem, decay_exp.nth(l, n - 1))
                    if n == 1:
                        d = LOGF.rearrange("p (n s) -> p n s", s=TOK)[:, :, 0:P]
                        b = SIG.rearrange("p (n s) -> p n s", s=TOK)
                        nc.gpsimd.tensor_tensor(d, b[:, :, 0:P], b[:, :, P - 1:P].broadcast_to([P, HEADS, P]), ALU.subtract)\
                            .then_inc(spread_ready.sem, 1)
                        continue
                    h = LEVELS[::-1][n - 2]
                    d = LOGF.rearrange("p (n s) -> p n s", s=2 * h)
                    b = SIG.rearrange("p (n s) -> p n s", s=2 * h)
                    nc.gpsimd.tensor_tensor(d, b, b[:, :, h - 1:h].broadcast_to([P, 1024 // (2 * h), 2 * h]), ALU.subtract)\
                        .then_inc(spread_ready.sem, 1)

            def short_conv(l):
                pool.wait_ge(evacuated.sem, evacuated.nth(l, 12))
                order.put(nc.gpsimd.tensor_tensor(CC, CC, CH, ALU.mult))
                hold()
                for ft in range(2):
                    order.put(nc.gpsimd.tensor_scalar(CH[:, ft, :], CC[:, ft, :], conv_w(2, ft), None, ALU.mult))
                for lag in (1, 2):
                    for ft in range(2):
                        order.put(nc.gpsimd.tensor_scalar(TMP[:, ft, lag:], CC[:, ft, :TOK - lag], conv_w(2 - lag, ft), None,
                                                          ALU.mult))
                    order.settle()
                    order.put(nc.gpsimd.tensor_tensor(CH[:, :, lag:], CH[:, :, lag:], TMP[:, :, lag:], ALU.add))
                    hold()
                order.put(nc.gpsimd.tensor_tensor(CH, CH, CB, ALU.mult))
                hold()
                order.put(nc.gpsimd.tensor_copy(yh[:, 0:2, :], CH))
                order.settle()
                nc.gpsimd.tensor_tensor(yl[:, 0:2, :], CH, yh[:, 0:2, :].bitcast(F32), ALU.subtract).then_inc(conv_ready.sem, 1)

            def windows(l):
                def widen(dst, src, w, f0):
                    order.put(nc.gpsimd.tensor_copy(dst[:, f0:, 0:w], src[:, f0:, 0:w]))
                    order.put(nc.gpsimd.tensor_tensor(dst[:, f0:, w:], src[:, f0:, w:], src[:, f0:, :TOK - w], ALU.add))
                    hold()

                s, t = CC, CH
                pool.wait_ge(conv_ready.sem, conv_ready.nth(l, 1))
                pool.wait_ge(evacuated.sem, evacuated.nth(l, 13))
                hold()
                widen(s, PU, 1, 0)
                widen(t, s, 2, 0)
                widen(s, t, 4, 1)
                widen(t, s, 8, 1)
                order.put(nc.gpsimd.tensor_scalar(s, s, first_half, None, ALU.mult))
                order.put(nc.gpsimd.tensor_scalar(t, t, second_half, None, ALU.mult))
                order.settle()
                order.put(nc.gpsimd.tensor_tensor(s, s, t, ALU.add))
                hold()
                for ft in range(2):
                    order.put(nc.gpsimd.tensor_scalar(TMP[:, ft, 16:], s[:, ft, 16:], invw[:, ft:ft + 1], None, ALU.mult))
                order.put(nc.gpsimd.tensor_tensor(TMP[:, :, 0:16], s[:, :, 0:16], edge, ALU.mult))
                order.settle()
                nc.gpsimd.tensor_tensor(TMP, TMP, PU, ALU.subtract).then_inc(windows_ready.sem, 1)

            pool.dma_start(units(9, 2).rearrange("p (t n) -> p t n", t=TT),
                           dram["mem"].rearrange("(t p) n -> p t n", p=P)).then_inc(mem_in.sem, 16)
            pool.dma_start(rlb[:], dram["rec_lb"].rearrange("p (l h) -> p l h", l=2)).then_inc(setup_in.sem, 16)
            pool.dma_start(units(11), dram["lvl_mask"]).then_inc(setup_in.sem, 16)
            order.put(nc.gpsimd.memset(mhalf[:], -0.5))
            order.put(nc.gpsimd.memset(poolw[:], 0.0))
            pool.wait_ge(inputs_in.sem, 32)
            pool.sem_inc(residual_ready.sem, 2)
            order.settle()
            order.close()
            with pool.Fori(0, DEPTH) as l:
                order.layer(l)
                pool.wait_ge(x_ready.sem, x_ready.nth(l, 0))
                pool.dma_start(par[:], dram["par_a"][bass.ds(l, 1), :, :].rearrange("l p n -> (l p) n")).then_inc(params_in.sem, 16)
                for half in range(2):
                    rows = slice(half * 64, (half + 1) * 64)
                    pool.dma_start(poolw[rows, :, rows],
                                   dram["pool_w"][bass.ds(l, 1), half:4:2, :, :].rearrange("l g c d -> c (l g) d"))\
                        .then_inc(params_in.sem, 16)
                norm(l, 0)
                spreads(l)
                short_conv(l)
                windows(l)
                norm(l, 1)
                norm(l, 2)
                norm(l, 3)

            order.close()
            with pool.Fori(0, DEPTH) as l:
                for j in range(2):
                    for t in range(TT):
                        pool.wait_ge(b_var_ready.sem, b_var_ready.nth(l, 2 * j + t + 1))
                        nc.gpsimd.tensor_tensor(rstd[:, t:t + 1], vare[:, t:t + 1], mhalf[:], ALU.pow).then_inc(rstd_ready.sem, 1)
                    if j:
                        continue
                    for r, (z0, z1, _, dim, _) in enumerate(ROUNDS):
                        z = Z[:, z0 * TOK:z1 * TOK].rearrange("p (z t) -> p z t", t=TOK)
                        pool.wait_ge(b_rotated.sem, b_rotated.nth(l, r + 1))
                        nc.gpsimd.tensor_tensor(z, z, rope[dim][0].unsqueeze(1).broadcast_to([P, z1 - z0, TOK]), ALU.mult)\
                            .then_inc(b_cosine.sem, 1)
                        pool.wait_ge(b_cosine.sem, b_cosine.nth(l, r + 1))
                        pool.wait_ge(b_sine.sem, b_sine.nth(l, r + 1))
                        nc.gpsimd.tensor_tensor(z, z, RZ[:, z0 * TOK:z1 * TOK].rearrange("p (z t) -> p z t", t=TOK), ALU.add)\
                            .then_inc(b_roped.sem, 1)
                    for b in range(4):
                        pool.wait_ge(b_gated.sem, b_gated.nth(l, 4 + b + 1))
                        nc.gpsimd.tensor_tensor(GATE[:, 8 + b, :], GATE[:, 8 + b, :], GATE[:, b, :], ALU.add).then_inc(b_pair_merged.sem, 1)


def kernel(**inputs):
    import numpy as np
    import concourse.bacc as bacc
    from concourse import mybir
    from concourse.bass_utils import run_bass_kernel_spmd

    P = 128
    a = {k: np.asarray(v) for k, v in inputs.items()}

    def columns(w, c0):
        n = w.shape[0]
        return w[:, :, c0:c0 + 256].reshape(n, 8, P, 256).transpose(0, 2, 1, 3).reshape(n, P, 2048)

    def rows(w, r0):
        n = w.shape[0]
        return w[:, r0:r0 + 256, :].reshape(n, 2, P, 1024).transpose(0, 2, 1, 3).reshape(n, P, 2048)

    def stream(chunks):
        out = np.empty((2, len(chunks), P, 2048), np.float32)
        for i, (cut, w, at) in enumerate(chunks):
            out[:, i] = cut(w, at)
        return out.reshape(-1, 2048)

    def ffn(gate, up, down):
        seq = []
        for i in range(11):
            seq += [(columns, *gate(i)), (columns, *up(i))]
            if i:
                seq.append((rows, down, 256 * (i - 1)))
        return seq + [(rows, down, 2560)]

    def plain_ffn(g, u, d):
        return ffn(lambda i: (a[g], 256 * i), lambda i: (a[u], 256 * i), a[d])

    conv, rec = 256, 512
    cb, cc, ch, rq = 0, conv, 2 * conv, 3 * conv
    rf, ri, rg, pu = rq + rec, rq + 2 * rec, rq + 3 * rec, rq + 4 * rec
    seq = plain_ffn("ffn1_gate", "ffn1_up", "ffn1_down")
    def key(n):
        return columns, a["ca_k"], 256 * n

    def value(n):
        return columns, a["ca_v"], 256 * n

    seq += [(columns, a["w_in"], c) for c in (rf, rf + 256, rq, rq + 256)] + [key(0)]
    seq += [(columns, a["w_in"], c) for c in (ri, ri + 256, rg, rg + 256, cc, ch, cb, pu)]
    seq += [key(1), key(2), key(3), value(0), value(1)]
    seq += [(rows, a["w_out"], r) for r in (0, 768, 256, 512)]
    seq += [(columns, a["ca_q"], 256 * n) for n in range(4)] + [value(2), value(3)]
    seq += [(rows, a["ca_o"], 256 * n) for n in range(4)]
    seq += plain_ffn("ffn2_gate", "ffn2_up", "ffn2_down")
    stream_a = stream(seq)

    def features(v):
        return v.reshape(2, -1, P).transpose(0, 2, 1)

    par_a = np.concatenate([features(a[n]) for n in ("ln_g", "ln_b", "conv_w", "rec_norm_g", "pool_scale")], axis=2)
    rec_lb = features(a["rec_lb"]).transpose(1, 0, 2).reshape(P, 8)

    a_w, b_q, b_kv, c_w = 256, 512, 128, 256
    w2 = a["w_in_2"]
    qa, ka, va, qb = 0, a_w, 2 * a_w, 3 * a_w
    kb = qb + b_q
    qc = kb + 2 * b_kv
    kc, vc, gates = qc + c_w, qc + 2 * c_w, qc + 3 * c_w
    paired = np.concatenate([np.arange(64) + 64 * h for i in range(4) for h in (i, i + 4)])
    wqb = w2[:, :, qb:kb][:, :, paired]
    wpb = a["w_pb_2"][:, paired, :]
    up, down = a["w_up_2"], a["w_down_2"]
    seq = [(columns, w2, qc), (columns, w2, kc), (columns, w2, qa), (columns, w2, ka), (columns, wqb, 0), (columns, wqb, 256),
           (columns, w2, kb), (columns, w2, va), (columns, w2, vc)]
    seq += [(columns, w2, gates + 256 * n) for n in range(12)]
    seq += [(rows, a["w_pc_2"], 0), (rows, a["w_pa_2"], 0), (rows, wpb, 0), (rows, wpb, 256)]
    seq += [(rows, a["w_out_2"], 256 * n) for n in range(4)]
    seq += ffn(lambda i: (up, 256 * i), lambda i: (up, 2816 + 256 * i), down)
    stream_b = stream(seq)

    lam_init = np.array([0.8 - 0.6 * float(np.exp(-0.3 * l)) for l in range(2)], np.float32)
    per_layer = np.stack([lam_init, np.float32(1.0) - lam_init], axis=1)
    par_b = np.concatenate(
        [features(a["attn_norm_2"]), features(a["mlp_norm_2"])]
        + [features(np.tile(a[n], (1, P // a[n].shape[1])))
           for n in ("qn_a_2", "kn_a_2", "qn_b_2", "kn_b_2", "qn_c_2", "kn_c_2", "subln_2")]
        + [np.broadcast_to(per_layer[:, None, :], (2, P, 2)), features(a["conv_b_2"]), features(a["conv_w_2"])], axis=2)
    grouped = [(j % 2) * 4 + 2 * g + j // 2 for g in range(2) for j in range(4)]
    row_b = np.concatenate([a["lam_q1_2"], a["lam_k1_2"], a["lam_q2_2"], a["lam_k2_2"], a["sinks_2"][:, grouped]], axis=1)

    i = np.arange(P)
    widths = np.array([[2, 8], [4, 16]])[i // 64]
    edge = 1.0 / np.minimum(np.arange(16)[None, None, :] + 1, widths[:, :, None])
    con = np.concatenate([np.eye(P), np.full((P, P), 1.0 / P), np.ones((P, P)), 1.0 / widths, edge.reshape(P, 32),
                          i[:, None] < 64, i[:, None] >= 64], axis=1).astype(np.float32)
    s, t = i[:, None], i[None, :]
    masks = [s == t] + [(s // (2 * h) == t // (2 * h)) & (s // h % 2 == 0) & (t // h % 2 == 1)
                        for h in (1, 2, 4, 8, 16, 32, 64)]
    lvl_mask = np.concatenate(masks, axis=1).astype(np.float32)

    def rope_table(dim):
        inv = np.float32(1.0) / (np.float32(10000.0) ** (np.arange(0, dim, 2, dtype=np.float32) / np.float32(dim)))
        ang = np.arange(256, dtype=np.float32)[None, :] * inv[i % (dim // 2)][:, None]
        return [np.cos(ang), np.sin(ang)]

    def head_mean(dim):
        return (s // dim == t // dim) / dim

    def swap_halves(dim):
        half = dim // 2
        return np.where((s == t + half) & (t % dim < half), -1.0, 0.0) + np.where((s == t - half) & (t % dim >= half), 1.0, 0.0)

    con_b = np.concatenate(rope_table(64) + rope_table(32) + [head_mean(64), head_mean(32), swap_halves(64), swap_halves(32)]
                           + [np.where(t <= s, 0.0, -1e30), np.where(t > s, 0.0, -1e30)], axis=1).astype(np.float32)

    arrays = {
        "stream_b": stream_b, "par_b": par_b, "row_b": row_b, "con_b": con_b,
        "x": a["x"][0], "mem": a["mem"][0], "stream_a": stream_a, "par_a": par_a, "rec_lb": rec_lb,
        "ln_g": a["ln_g"].reshape(8, 1024), "ln_b": a["ln_b"].reshape(8, 1024), "pool_w": a["pool_w"],
        "con": con, "lvl_mask": lvl_mask,
    }
    arrays = {k: np.ascontiguousarray(v) for k, v in arrays.items()}
    nc = bacc.Bacc("TRN2", target_bir_lowering=False, num_devices=1)
    dram = {k: nc.dram_tensor("in_" + k, v.shape, mybir.dt.from_np(v.dtype), kind="ExternalInput").ap() for k, v in arrays.items()}
    dram["out"] = nc.dram_tensor("out", (256, 1024), mybir.dt.float32, kind="ExternalOutput").ap()
    build_program(nc, dram)
    r = run_bass_kernel_spmd(nc, [{"in_" + k: v for k, v in arrays.items()}], core_ids=[0])
    return r.results[0]["out"].reshape(1, 256, 1024)
```
